# Optimizing a Trainium2 kernel written in Bass

```python
import math
import jax, jax.numpy as jnp
from jax import lax
import numpy as np

D_MODEL = 1024
BATCH = 1
SEQ = 1024
DEPTH = 1
DEC_BATCH = 1
DEC_SEQ = 64
PAST_LEN = 512

CHUNK = 64
Q_BLOCK = 128
MLA_HEADS = 8
MLA_NOPE = 64
MLA_ROPE = 32
MLA_V = 64
MLA_Q_RANK = 384
MLA_KV_RANK = 256
RET_HEADS = 4
RET_DK = 64
RET_DV = 64
SB_HEADS = 4
SB_DK = 64
SB_DV = 64
MIX_WIDTH = MLA_HEADS * MLA_V + RET_HEADS * RET_DV + SB_HEADS * SB_DV
IN_WIDTHS = (MLA_Q_RANK, MLA_KV_RANK, MLA_ROPE,
             RET_HEADS * RET_DK, RET_HEADS * RET_DK, RET_HEADS * RET_DV, RET_HEADS * RET_DV,
             SB_HEADS * SB_DK, SB_HEADS * SB_DK, SB_HEADS * SB_DV)
IN_COLS = sum(IN_WIDTHS)
D_FF = 2816
CONV_W = 3
ROPE_BASE = 10000.0
EPS = 1e-6

kernel_name = "hybrid_streaming_encoder_step"

def rmsnorm(x, g):
    xf = x.astype(jnp.float32)
    y = xf * lax.rsqrt(jnp.mean(xf * xf, axis=-1, keepdims=True) + EPS)
    return (y * g.astype(jnp.float32)).astype(x.dtype)

def rope(x, pos):
    d = x.shape[-1]
    inv = ROPE_BASE ** (-jnp.arange(0, d, 2, dtype=jnp.float32) / d)
    ang = pos.astype(jnp.float32)[:, None] * inv[None, :]
    ang = ang.reshape((ang.shape[0],) + (1,) * (x.ndim - 3) + (d // 2,))
    cos, sin = jnp.cos(ang), jnp.sin(ang)
    x1 = x[..., : d // 2].astype(jnp.float32)
    x2 = x[..., d // 2:].astype(jnp.float32)
    return jnp.concatenate([x1 * cos - x2 * sin, x1 * sin + x2 * cos], axis=-1).astype(x.dtype)

def sweep_query_blocks(fn, q_args, q_pos):
    nq = q_pos.shape[0]
    if nq <= Q_BLOCK:
        return fn(q_args, q_pos)
    nb = nq // Q_BLOCK

    def one(i):
        s = i * Q_BLOCK
        qa = tuple(lax.dynamic_slice_in_dim(a, s, Q_BLOCK, axis=1) for a in q_args)
        return fn(qa, lax.dynamic_slice_in_dim(q_pos, s, Q_BLOCK))

    out = jnp.moveaxis(lax.map(one, jnp.arange(nb)), 0, 1)
    return out.reshape((out.shape[0], nq) + out.shape[3:])

def _retention_chunk(S, q, k, v):
    L = q.shape[1]
    lg = jnp.log(1.0 - 2.0 ** (-5.0 - jnp.arange(RET_HEADS, dtype=jnp.float32)))
    i = jnp.arange(L, dtype=jnp.float32)
    rel = i[:, None] - i[None, :]
    decay = jnp.where(rel >= 0, jnp.exp(lg[:, None, None] * jnp.maximum(rel, 0.0)), 0.0)
    qf, kf, vf = q.astype(jnp.float32), k.astype(jnp.float32), v.astype(jnp.float32)
    att = jnp.einsum("blhd,bmhd->bhlm", qf, kf) * decay[None]
    o = jnp.einsum("bhlm,bmhe->blhe", att, vf)
    q_decay = jnp.exp(lg[None, :] * (i[:, None] + 1.0))
    o = o + jnp.einsum("blhd,bhde->blhe", qf, S) * q_decay[None, :, :, None]
    k_decay = jnp.exp(lg[None, :] * (L - 1.0 - i[:, None]))
    S_new = jnp.exp(lg * L)[None, :, None, None] * S + jnp.einsum(
        "blhd,blhe->bhde", kf * k_decay[None, :, :, None], vf)
    return S_new, o

def _mixers(h, l, pos0, cache, p):
    B, L, _ = h.shape
    pos = pos0 + jnp.arange(L)
    z = h @ p["w_in"][l]
    splits = [int(s) for s in np.cumsum(IN_WIDTHS)[:-1]]
    zq, zkv, zkr, rq, rk, rv, rg, sq, sk, sv = jnp.split(z, splits, axis=-1)

    q = (rmsnorm(zq, p["g_q_norm"][l]) @ p["w_uq"][l]).reshape(B, L, MLA_HEADS, MLA_NOPE + MLA_ROPE)
    q_nope = q[..., :MLA_NOPE]
    q_rope = rope(q[..., MLA_NOPE:], pos)
    latent = rmsnorm(zkv, p["g_kv_norm"][l])
    k_rope = rope(zkr, pos)
    rq = rope(rq.reshape(B, L, RET_HEADS, RET_DK), pos) * (RET_DK ** -0.5)
    rk = rope(rk.reshape(B, L, RET_HEADS, RET_DK), pos)
    rv = rv.reshape(B, L, RET_HEADS, RET_DV)
    sq = sq.reshape(B, L, SB_HEADS, SB_DK)
    sk = sk.reshape(B, L, SB_HEADS, SB_DK)
    sv = sv.reshape(B, L, SB_HEADS, SB_DV)

    if cache is None:
        lat_all, kr_all, sk_all, sv_all = latent, k_rope, sk, sv
        S0 = jnp.zeros((B, RET_HEADS, RET_DK, RET_DV), jnp.float32)
    else:
        lat_all = jnp.concatenate([cache["lat"].astype(latent.dtype), latent], axis=1)
        kr_all = jnp.concatenate([cache["kr"].astype(k_rope.dtype), k_rope], axis=1)
        sk_all = jnp.concatenate([cache["sk"].astype(sk.dtype), sk], axis=1)
        sv_all = jnp.concatenate([cache["sv"].astype(sv.dtype), sv], axis=1)
        S0 = cache["S"].astype(jnp.float32)
    k_pos = jnp.arange(lat_all.shape[1])

    kv = (lat_all @ p["w_ukv"][l]).reshape(B, -1, MLA_HEADS, MLA_NOPE + MLA_V)
    k_nope, v_mla = kv[..., :MLA_NOPE], kv[..., MLA_NOPE:]
    mla_scale = (MLA_NOPE + MLA_ROPE) ** -0.5

    def mla_fn(qa, qp):
        qn, qr = qa
        s = (jnp.einsum("bqhd,bkhd->bhqk", qn, k_nope) + jnp.einsum("bqhd,bkd->bhqk", qr, kr_all)).astype(jnp.float32) * mla_scale
        mask = (k_pos[None, :] // CHUNK) <= (qp[:, None] // CHUNK)
        s = jnp.where(mask, s, -1e30)
        w = jax.nn.softmax(s, axis=-1).astype(v_mla.dtype)
        return jnp.einsum("bhqk,bkhd->bqhd", w, v_mla)

    mla_out = sweep_query_blocks(mla_fn, (q_nope, q_rope), pos).reshape(B, L, MLA_HEADS * MLA_V)

    if cache is None:
        n = L // CHUNK
        def to_chunks(a):
            return jnp.swapaxes(a.reshape((B, n, CHUNK) + a.shape[2:]), 0, 1)
        def step(S, inp):
            return _retention_chunk(S, *inp)
        S_new, ro = lax.scan(step, S0, (to_chunks(rq), to_chunks(rk), to_chunks(rv)))
        ro = jnp.swapaxes(ro, 0, 1).reshape(B, L, RET_HEADS, RET_DV)
    else:
        S_new, ro = _retention_chunk(S0, rq, rk, rv)
    mu = jnp.mean(ro, axis=-1, keepdims=True)
    var = jnp.mean((ro - mu) ** 2, axis=-1, keepdims=True)
    ro = ((ro - mu) * lax.rsqrt(var + EPS)).reshape(B, L, RET_HEADS * RET_DV) * p["g_ret_norm"][l].astype(jnp.float32)
    ret_out = (jax.nn.silu(rg.astype(jnp.float32)) * ro).astype(h.dtype)

    sb_scale = SB_DK ** -0.5

    def sb_fn(qa, qp):
        (qs,) = qa
        zz = jnp.einsum("bqhd,bkhd->bhqk", qs, sk_all).astype(jnp.float32) * sb_scale
        mask = k_pos[None, :] < qp[:, None]
        log_beta = jax.nn.log_sigmoid(zz)
        log_1mb = jnp.where(mask, log_beta - zz, 0.0)
        after = lax.cumsum(log_1mb, axis=3, reverse=True) - log_1mb
        w = jnp.where(mask, jnp.exp(log_beta + after), 0.0).astype(sv_all.dtype)
        return jnp.einsum("bhqk,bkhd->bqhd", w, sv_all)

    sb_out = sweep_query_blocks(sb_fn, (sq,), pos).reshape(B, L, SB_HEADS * SB_DV)

    mix = jnp.concatenate([mla_out, ret_out, sb_out], axis=-1) @ p["w_o"][l]
    return mix, (latent, k_rope, sk, sv, S_new.astype(h.dtype))

def _conv_ffn(h, prev, l, p):
    L = h.shape[1]
    up = h @ p["w_up"][l]
    a, b = up[..., :D_FF], up[..., D_FF:]
    a_ext = jnp.concatenate([prev.astype(a.dtype), a], axis=1)
    w = p["conv_w"][l]
    conv = p["conv_b"][l] + w[0] * a_ext[:, 0:L]
    for j in range(1, CONV_W):
        conv = conv + w[j] * a_ext[:, j:j + L]
    y = (jax.nn.silu(conv) * b) @ p["w_down"][l]
    return y, a_ext[:, -(CONV_W - 1):]

def _trunk(x, c, pos0, cache, p):
    new = [[] for _ in range(6)]
    B = x.shape[0]
    for l in range(DEPTH):
        mod = (jax.nn.silu(c) @ p["w_ada"][l] + p["b_ada"][l])[:, None, :]
        sh1, sc1, g1, sh2, sc2, g2 = jnp.split(mod, 6, axis=-1)
        lc = None if cache is None else {k: v[l] for k, v in cache.items()}
        h = rmsnorm(x, p["g_norm1"][l]) * (1.0 + sc1) + sh1
        mix, st = _mixers(h, l, pos0, lc, p)
        x = x + g1 * mix
        h = rmsnorm(x, p["g_norm2"][l]) * (1.0 + sc2) + sh2
        prev = jnp.zeros((B, CONV_W - 1, D_FF), x.dtype) if lc is None else lc["conv"]
        f, buf = _conv_ffn(h, prev, l, p)
        x = x + g2 * f
        for lst, s in zip(new, st + (buf,)):
            lst.append(s)
    y = rmsnorm(x, p["g_final"])
    return y, [jnp.stack(s, axis=0) for s in new]

def setup_inputs(seed: int = 0) -> dict:
    key = jax.random.key(seed)
    ks = jax.random.split(key, 32)
    nrm = jax.random.normal
    f32 = jnp.float32
    return {
        "x_prompt": nrm(ks[0], (BATCH, SEQ, D_MODEL), f32),
        "x_sample": nrm(ks[1], (DEC_BATCH, DEC_SEQ, D_MODEL), f32),
        "c_prompt": nrm(ks[2], (BATCH, D_MODEL), f32),
        "c_sample": nrm(ks[3], (DEC_BATCH, D_MODEL), f32),
        "cache_mla_latent": nrm(ks[4], (DEPTH, DEC_BATCH, PAST_LEN, MLA_KV_RANK), f32),
        "cache_mla_krope": nrm(ks[5], (DEPTH, DEC_BATCH, PAST_LEN, MLA_ROPE), f32),
        "cache_sb_k": nrm(ks[6], (DEPTH, DEC_BATCH, PAST_LEN, SB_HEADS, SB_DK), f32),
        "cache_sb_v": nrm(ks[7], (DEPTH, DEC_BATCH, PAST_LEN, SB_HEADS, SB_DV), f32),
        "state_ret": 2.0 * nrm(ks[8], (DEPTH, DEC_BATCH, RET_HEADS, RET_DK, RET_DV), f32),
        "state_ffn_conv": nrm(ks[9], (DEPTH, DEC_BATCH, CONV_W - 1, D_FF), f32),
        "w_in": nrm(ks[10], (DEPTH, D_MODEL, IN_COLS), f32) * D_MODEL ** -0.5,
        "g_q_norm": 1.0 + 0.02 * nrm(ks[11], (DEPTH, MLA_Q_RANK), f32),
        "w_uq": nrm(ks[12], (DEPTH, MLA_Q_RANK, MLA_HEADS * (MLA_NOPE + MLA_ROPE)), f32) * MLA_Q_RANK ** -0.5,
        "g_kv_norm": 1.0 + 0.02 * nrm(ks[13], (DEPTH, MLA_KV_RANK), f32),
        "w_ukv": nrm(ks[14], (DEPTH, MLA_KV_RANK, MLA_HEADS * (MLA_NOPE + MLA_V)), f32) * MLA_KV_RANK ** -0.5,
        "g_ret_norm": 1.0 + 0.02 * nrm(ks[15], (DEPTH, RET_HEADS * RET_DV), f32),
        "w_o": nrm(ks[16], (DEPTH, MIX_WIDTH, D_MODEL), f32) * MIX_WIDTH ** -0.5,
        "w_up": nrm(ks[17], (DEPTH, D_MODEL, 2 * D_FF), f32) * D_MODEL ** -0.5,
        "conv_w": nrm(ks[18], (DEPTH, CONV_W, D_FF), f32) * CONV_W ** -0.5,
        "conv_b": 0.02 * nrm(ks[19], (DEPTH, D_FF), f32),
        "w_down": nrm(ks[20], (DEPTH, D_FF, D_MODEL), f32) * D_FF ** -0.5,
        "g_norm1": 1.0 + 0.02 * nrm(ks[21], (DEPTH, D_MODEL), f32),
        "g_norm2": 1.0 + 0.02 * nrm(ks[22], (DEPTH, D_MODEL), f32),
        "w_ada": nrm(ks[23], (DEPTH, D_MODEL, 6 * D_MODEL), f32) * (0.5 * D_MODEL ** -0.5),
        "b_ada": 0.02 * nrm(ks[24], (DEPTH, 6 * D_MODEL), f32),
        "g_final": 1.0 + 0.02 * nrm(ks[25], (D_MODEL,), f32),
    }

def reference(x_prompt, x_sample, c_prompt, c_sample, cache_mla_latent, cache_mla_krope, cache_sb_k, cache_sb_v,
              state_ret, state_ffn_conv, w_in, g_q_norm, w_uq, g_kv_norm, w_ukv, g_ret_norm, w_o, w_up, conv_w,
              conv_b, w_down, g_norm1, g_norm2, w_ada, b_ada, g_final):
    p = dict(w_in=w_in, g_q_norm=g_q_norm, w_uq=w_uq, g_kv_norm=g_kv_norm, w_ukv=w_ukv, g_ret_norm=g_ret_norm,
             w_o=w_o, w_up=w_up, conv_w=conv_w, conv_b=conv_b, w_down=w_down, g_norm1=g_norm1, g_norm2=g_norm2,
             w_ada=w_ada, b_ada=b_ada, g_final=g_final)
    y_prompt, (p_lat, p_kr, p_sk, p_sv, p_S, p_conv) = _trunk(x_prompt, c_prompt, 0, None, p)
    cache = dict(lat=cache_mla_latent, kr=cache_mla_krope, sk=cache_sb_k, sv=cache_sb_v, S=state_ret,
                 conv=state_ffn_conv)
    y_sample, (s_lat, s_kr, s_sk, s_sv, s_S, s_conv) = _trunk(x_sample, c_sample, PAST_LEN, cache, p)
    return (y_prompt, y_sample, p_lat, p_kr, p_sk, p_sv, p_S, p_conv, s_lat, s_kr, s_sk, s_sv, s_S, s_conv)


_drawn_inputs = setup_inputs


def setup_inputs(seed=0):
    import zlib

    import numpy as np

    out = dict(_drawn_inputs(seed))
    spreads = {}
    factors = {'cache_mla_latent': 3.93,
     'cache_mla_krope': 8.0,
     'cache_sb_k': 8.0,
     'cache_sb_v': 3.743,
     'state_ffn_conv': 2.716,
     'g_q_norm': 8.0,
     'w_uq': 2.833,
     'g_kv_norm': 2.704,
     'g_ret_norm': 8.0,
     'conv_b': 8.0,
     'g_norm2': 2.896,
     'g_final': 2.781}
    for name, (base, spread) in spreads.items():
        noise = np.random.default_rng([zlib.crc32(name.encode()), seed]).standard_normal(out[name].shape)
        drawn = base * np.exp(spread * noise) if base else spread * noise
        out[name] = __import__('jax').numpy.asarray(drawn.astype(out[name].dtype))
    for name, factor in factors.items():
        out[name] = (out[name] * factor).astype(out[name].dtype)
    return out
```

```python
from contextlib import ExitStack

import numpy as np

import concourse.bass as bass
from concourse import mybir

F32 = mybir.dt.float32
F32R = mybir.dt.float32r
ALU = mybir.AluOpType
ACT = mybir.ActivationFunctionType
AX = mybir.AxisListType.X

P = 128
D = 1024
KT = D // P
LP, LS = 1024, 64
T = LP + LS
PAST = 512
NTILE = 9
ROWS = [P] * 8 + [LS]
CHUNKS = [(0, 364), (364, 726), (726, 1088)]
CW = 364
H_MLA, NOPE, ROPE, HV = 8, 64, 32, 64
QD = NOPE + ROPE
QR, KVR = 384, 256
H_RET, H_SB, DH = 4, 4, 64
IN_COLS = 2464
ZG = 352
NZG = IN_COLS // ZG
O_ZQ, O_KV, O_KR, O_RQ, O_RK, O_RV, O_RG, O_SQ, O_SK, O_SV = 0, 384, 640, 672, 928, 1184, 1440, 1696, 1952, 2208
FF = 2816
NF = FF // P
EPS = 1e-6
NEG = -1e30
RAW_SLOTS, WT_SLOTS = 3, 6
N_TAB = 12
ADA_G = 24
MLA_SCALE = float(QD) ** -0.5
SB_SCALE = float(DH) ** -0.5


def segments(c):
    a, b = CHUNKS[c]
    return [(a, b, 0)] if b <= LP else [(a, LP, 0), (LP, b, 1)]


def chunk_of(t):
    end = min(P * (t + 1), T)
    return next(c for c, (a, b) in enumerate(CHUNKS) if end <= b)


def tables():
    out = {}
    pos = np.arange(T, dtype=np.float64)
    pos[LP:] = PAST + np.arange(LS)
    for name, d in (("rope64", DH), ("rope32", ROPE)):
        inv = (10000.0 ** (-np.arange(0, d, 2, dtype=np.float32) / np.float32(d))).astype(np.float32)
        ang = (pos.astype(np.float32)[:, None] * inv[None, :]).astype(np.float64)
        cos, sin = np.cos(ang), np.sin(ang)
        tab = np.concatenate([cos, cos, -sin, sin], axis=1)
        pad = np.zeros((NTILE * P, 2 * d), np.float32)
        pad[:T] = tab
        out[name] = pad.reshape(NTILE, P, 2 * d).transpose(1, 0, 2).reshape(P, NTILE * 2 * d).copy()
    lg = np.log(1.0 - 2.0 ** (-5.0 - np.arange(H_RET, dtype=np.float32))).astype(np.float64)
    i = np.arange(P)
    rel = i[None, :] - i[:, None]
    dec = np.where(rel[:, None, :] >= 0, np.exp(lg[None, :, None] * np.maximum(rel, 0)[:, None, :]), 0.0)
    out["decayT"] = dec.reshape(P, H_RET * P).astype(np.float32)
    qd = np.zeros((P, 2, P))
    gam = np.zeros((P, 2, 2, P))
    for h in range(H_RET):
        rows = slice(64 * (h % 2), 64 * (h % 2) + 64)
        qd[rows, h // 2, :] = np.exp(lg[h] * (i + 1.0)) * DH ** -0.5
        for n, length in enumerate((P, LS)):
            gam[rows, n, h // 2, :] = np.exp(lg[h] * length)
    out["q_decayT"] = qd.reshape(P, 2 * P).astype(np.float32)
    out["state_decay"] = gam.reshape(P, 4 * P).astype(np.float32)
    kd = np.zeros((P, 2, H_RET))
    for n, length in enumerate((P, LS)):
        kd[:length, n, :] = np.exp(lg[None, :] * (length - 1.0 - i[:length, None]))
    out["k_decay"] = kd.reshape(P, 2 * H_RET).astype(np.float32)
    out["ident"] = np.eye(P, dtype=np.float32)
    out["causal"] = np.where(i[None, :] < i[:, None], 0.0, NEG).astype(np.float32)
    return out


TABLES = {"rope64": (P, NTILE * 128), "rope32": (P, NTILE * 64), "decayT": (P, 512), "q_decayT": (P, 256),
          "state_decay": (P, 512), "k_decay": (P, 8), "ident": (P, P), "causal": (P, P)}
INS = {"x_prompt": (LP, D), "x_sample": (LS, D), "c_prompt": (8, P), "c_sample": (8, P),
       "cache_mla_latent": (PAST, KVR), "cache_mla_krope": (PAST, ROPE), "cache_sb_k": (PAST, 256),
       "cache_sb_v": (PAST, 256), "state_ret": (256, 64), "state_ffn_conv": (44, P), "w_in": (D, IN_COLS),
       "g_q_norm": (3, P), "w_uq": (QR, 768), "g_kv_norm": (1, KVR), "w_ukv": (KVR, 1024), "g_ret_norm": (1, 256),
       "w_o": (D, D), "w_up": (D, 2 * FF), "conv_w": (66, P), "conv_b": (22, P), "w_down": (FF, D),
       "g_norm1": (8, P), "g_norm2": (8, P), "w_ada": (D, 6 * D), "b_ada": (48, P), "g_final": (1, D)}
OUTS = [("y_prompt", (1, LP, D)), ("y_sample", (1, LS, D)),
        ("p_mla_latent", (1, 1, LP, KVR)), ("p_mla_krope", (1, 1, LP, ROPE)),
        ("p_sb_k", (1, 1, LP, 4, 64)), ("p_sb_v", (1, 1, LP, 4, 64)),
        ("p_ret_state", (1, 1, 4, 64, 64)), ("p_ffn_conv", (1, 1, 2, FF)),
        ("s_mla_latent", (1, 1, LS, KVR)), ("s_mla_krope", (1, 1, LS, ROPE)),
        ("s_sb_k", (1, 1, LS, 4, 64)), ("s_sb_v", (1, 1, LS, 4, 64)),
        ("s_ret_state", (1, 1, 4, 64, 64)), ("s_ffn_conv", (1, 1, 2, FF))]
VEC_A = [("b_ada", 48, 0), ("g_norm1", 8, 48), ("g_norm2", 8, 56), ("c_prompt", 8, 64), ("c_sample", 8, 72),
         ("g_q_norm", 3, 80)]
N_A = 83
VEC_B = [("conv_w", 66, 0), ("conv_b", 22, 66)]
N_B = 88
N_C = 44


SEQ = [8] + list(range(8))
KINDS = [("S", 0), ("M", 0), ("M", 1), ("S", 1), ("M", 2), ("M", 3), ("S", 2), ("M", 4), ("M", 5), ("S", 3),
         ("M", 6), ("M", 7)]
UNITS = [(n, kind, h) for n in range(NTILE) for kind, h in KINDS]
T_LAG = {"M": 1, "S": 4}
MIX_STEP = 16




def rows_of(n):
    return ROWS[SEQ[n]]


def key_col(n):
    return P * SEQ[n]


def key_blocks(n):
    if n == 0:
        return [(512 + P * j, P, 4 + j) for j in range(4)] + [(LP, LS, 8)]
    return [(P * j, P, j) for j in range(SEQ[n] + 1)]


def n_keys(n):
    return sum(size for _, size, _ in key_blocks(n))


def count_units(kind, i):
    return sum(k == kind for _, k, _ in UNITS[:i])


def plan_pieces():
    steps = {}
    for step in range(12 * (NTILE - 1) + MIX_STEP + 1):
        out = []
        for kind in "MS":
            i = step - T_LAG[kind]
            if 0 <= i < len(UNITS) and UNITS[i][1] == kind:
                nb = len(key_blocks(UNITS[i][0]))
                out += [(kind, i, j) for j in range((nb + 3) // 4)]
        n, rest = divmod(step - MIX_STEP, 12)
        if rest == 0 and 0 <= n < NTILE:
            out += [("X", n, 0), ("X", n, 1)]
        steps[step] = out
    return steps


PIECES = plan_pieces()
STEPS = len(PIECES)
ORDER = [x for step in range(STEPS) for x in PIECES[step]]
PIECE_NO = {x: q for q, x in enumerate(ORDER)}
W_NO = {x: w for w, x in enumerate(x for x in ORDER if x[0] != "X")}
COPIER = {"M": "A", "S": "D", "X": "A"}
COPY_NO = {x: sum(COPIER[y[0]] == COPIER[x[0]] for y in ORDER[:q]) for q, x in enumerate(ORDER)}
PV_ORDER = [x[1] for x in ORDER if x[0] != "X" and x[2] == 0]
PV_NO = {i: v for v, i in enumerate(PV_ORDER)}
READ_A = [0, 1, 2, 3, 4, 5, 7, 8, 9]
READ_D = [0, 2, 3, 4, 6, 7, 9, 10, 11]


def read_a(m, s):
    return len(READ_A) * m + sum(x < s for x in READ_A)


def read_d(m, s):
    return len(READ_D) * m + sum(x < s for x in READ_D)


def build(nc, I, O, stop_after=None):
    ctx = ExitStack()
    z_dram = nc.dram_tensor("z_scratch", (T, IN_COLS), F32, kind="Internal").ap()
    xT_dram = nc.dram_tensor("xT_scratch", (P, KT, T), F32, kind="Internal").ap()
    mixT_dram = nc.dram_tensor("mixT_scratch", (P, KT, T), F32, kind="Internal").ap()
    with ctx:
        def sem(name):
            return ctx.enter_context(nc.semaphore(name))

        def sbuf(scope):
            return lambda name, shape, dt=F32: scope.enter_context(nc.sbuf_tensor(name, [P, *shape], dt))

        keep = sbuf(ctx)
        psum = ctx.enter_context(nc.psum_tensor("psum", [P, 8, 512], F32))
        bank = [psum[:, i, :] for i in range(8)]

        ident = keep("ident_sb", [P])
        ones = keep("ones", [P])
        vec_a = keep("vec_a", [N_A])
        vec_b = keep("vec_b", [N_B])
        vec_c = keep("vec_c", [N_C])
        mod = keep("mod", [48, 2])
        scale_n = keep("scale_n", [2, KT, 2])
        eps = keep("eps", [1])

        early = ExitStack()
        s1 = sbuf(early)
        xT = s1("xT", [KT, T])
        h_hi = s1("h_hi", [KT, T], F32R)
        h_lo = s1("h_lo", [KT, T], F32R)
        rb = s1("rb", [T])
        sq = s1("sq", [2, CW])
        hn = s1("hn", [3, CW])
        x_in = s1("x_in", [2, D])
        vec_in = s1("vec_in", [3, P])
        silu_c = s1("silu_c", [2, KT])
        silu_e = s1("silu_e", [2, KT])
        ada_w = s1("ada_w", [2, KT, 256])
        w_raw = s1("w_raw", [2, 4, ZG])
        w_hi = s1("w_hi", [2, KT, ZG], F32R)
        w_lo = s1("w_lo", [2, KT, ZG], F32R)
        z_out = s1("z_out", [3, ZG])
        early.close()

        mid = ExitStack()
        s3 = sbuf(mid)
        kT = s3("kT", [H_MLA, T])
        v_mla = s3("v_mla", [NTILE, 512])
        skT = s3("skT", [2, T])
        sv = s3("sv", [NTILE, 256])
        w_uq = s3("w_uq_sb", [3, 768])
        w_uk = s3("w_uk", [2, 512])
        w_uv = s3("w_uv", [2, 512])
        z_in = s3("z_in", [2, IN_COLS])
        rope_t = s3("rope_t", [2, 192])
        qtok = s3("qtok", [768])
        qT = s3("qT", [2, H_MLA, P])
        sqT = s3("sqT", [2, 2, P])
        prob = s3("prob", [2, 1024])
        zsb = s3("zsb", [2, 1024])
        esb = s3("esb", [2, 1024])
        pT = s3("pT", [4, 4, P])
        mixtok = s3("mixtok", [2, D])
        mixT = s3("mixT", [KT, P])
        decayT = s3("decayT_sb", [H_RET, P])
        q_decayT = s3("q_decayT_sb", [2, P])
        state_decay = s3("state_decay_sb", [2, 2, P])
        k_decay = s3("k_decay_sb", [2, H_RET])
        causal = s3("causal_sb", [P])
        g_kv = s3("g_kv_sb", [KVR])
        g_ret = s3("g_ret_sb", [256])
        zeros = s3("zeros", [1024])
        zqn = s3("zqn", [QR])
        lat = s3("lat", [KVR])
        latT = s3("latT", [2, P])
        qnT = s3("qnT", [3, P])
        junk = s3("junk", [QR + KVR])
        sums = s3("sums", [2])
        rs = s3("rs", [2])
        rope_a = s3("rope_a", [512])
        rope_b = s3("rope_b", [512])
        q_a = s3("q_a", [4, ROPE])
        q_b = s3("q_b", [4, ROPE])
        kr = s3("kr", [ROPE])
        rqk = s3("rqk", [8, DH])
        kd = s3("kd", [H_RET, DH])
        rqT = s3("rqT", [2, 2, P])
        rkT = s3("rkT", [2, P])
        rqdT = s3("rqdT", [2, P])
        att = s3("att", [H_RET, P])
        state = s3("state", [2, 2, P])
        eg = s3("eg", [256])
        gate = s3("gate", [256])
        oc = s3("oc", [H_RET, DH])
        oc2 = s3("oc2", [H_RET, DH])
        stat = s3("stat", [4, H_RET])
        maxes = s3("maxes", [2, 2])
        rowsum = s3("rowsum", [4, 2])
        mid.close()
        late = ExitStack()
        s4 = sbuf(late)
        res = s4("residual", [KT, T])
        a_hi = s4("act_hi", [KT, T], F32R)
        a_lo = s4("act_lo", [KT, T], F32R)
        wt_raw = s4("wt_raw", [RAW_SLOTS, KT * P])
        wt_hi = s4("wt_hi", [WT_SLOTS, KT * P], F32R)
        wt_lo = s4("wt_lo", [WT_SLOTS, KT * P], F32R)
        u_hi = s4("u_hi", [2, T], F32R)
        u_lo = s4("u_lo", [2, T], F32R)
        a_ext = s4("a_ext", [2, T + 4])
        conv = s4("conv", [T + 2])
        f_vec = s4("f_vec", [2, 4])
        conv_out = s4("conv_out", [4, NF])
        u_val = s4("u_val", [2, CW])
        fin = s4("final_stats", [2, 3])
        late.close()
        norm_bufs = [dict(x=xT, hi=h_hi, lo=h_lo, rb=rb, sq=sq, hn=hn),
                     dict(x=res, hi=a_hi, lo=a_lo, rb=conv,
                          sq=a_ext[:, 0, 0:2 * CW].rearrange("p (a n) -> p a n", a=2),
                          hn=a_ext[:, 1, 0:3 * CW].rearrange("p (a n) -> p a n", a=3))]
        mix_raw = a_ext[:, :, 0:T]
        late_out = a_ext[:].rearrange("p a n -> p (a n)")
        g_fin = conv[:, 0:D]
        y_out = late_out[:, 0:2 * D].rearrange("p (a n) -> p a n", a=2)
        conv_rows = u_val[:, 0, 0:P]
        c_lat = prob[:, 0, :].rearrange("p (j c) -> p j c", j=4)
        c_sk = prob[:, 1, :].rearrange("p (j c) -> p j c", j=4)
        c_kr = mixT[:, 0, :].rearrange("p (j c) -> p j c", j=4)
        c_latT = zsb[:, :, :].rearrange("p a (b c) -> p a b c", b=2)[:, :, 0, :]

        s_const = sem("constants_loaded")
        s_x = [sem(f"x_loaded_{i}") for i in range(2)]
        s_set = sem("memsets_done")
        s_xt = sem("x_transposed")
        s_xeD = sem("xT_first_half_written")
        s_xeA = sem("xT_second_half_written")
        s_vt = sem("vectors_transposed")
        s_vec = sem("vectors_written")
        s_silu = sem("silu_steps")
        s_siluv = sem("silu_ready")
        s_ada = [sem(f"ada_loaded_{i}") for i in range(2)]
        s_adamm = sem("ada_multiplied")
        s_mod = sem("mod_written")
        s_scale = sem("norm_scales_written")
        s_sq = sem("squares_written")
        s_ms = sem("squares_summed")
        s_ln = sem("log_written")
        s_rb = sem("rstd_written")
        s_hn = sem("normed_written")
        s_hhi = sem("h_hi_written")
        s_h = sem("h_lo_written")
        s_raw = [sem(f"w_raw_loaded_{i}") for i in range(2)]
        s_whi = sem("w_hi_written")
        s_wlo = sem("w_lo_written")
        s_z = sem("z_multiplied")
        s_zc = sem("z_copied")
        s_zst = [sem(f"z_stored_{i}") for i in range(3)]

        s_xst = sem("xT_stored")
        s_tab = sem("mixer_constants_loaded")
        s_cache = sem("caches_loaded")
        s_init = sem("mixer_memsets_done")
        s_sv = sem("values_loaded")
        s_wuq = sem("w_uq_scaled")
        s_zi = [sem(f"z_tile_loaded_{i}") for i in range(2)]
        s_cT = sem("cache_stage_multiplied")
        s_cA = sem("cache_copied_by_scalar")
        s_cD = sem("cache_copied_by_vector")
        s_rs = sem("latent_rstd_ready")
        s_eg = sem("gate_exp_ready")
        s_lat = sem("latents_normed")
        s_latst = sem("latents_stored")
        s_kr = sem("k_rope_ready")
        s_rot = sem("retention_qk_ready")
        s_g1 = sem("gate_denominator_ready")
        s_g2 = sem("gate_reciprocal_ready")
        s_gate = sem("gate_ready")
        s_fp = sem("front_step_multiplied")
        s_fA = sem("front_bank_read_by_scalar")
        s_fD = sem("front_bank_read_by_vector")
        s_var = sem("group_variance_ready")
        s_rr = sem("group_rstd_ready")
        s_ret = sem("retention_written")
        s_sc = sem("scores_multiplied")
        s_mx = sem("maximum_ready")
        s_p = sem("softmax_exp_written")
        s_zsb = sem("stick_logits_copied")
        s_l = sem("stick_log_written")
        s_c = sem("stick_sums_written")
        s_wa = sem("stick_exponents_written")
        s_w = sem("stick_weights_written")
        s_tr = sem("piece_transposed")
        s_ptA = sem("piece_copied_by_scalar")
        s_ptD = sem("piece_copied_by_vector")
        s_pv = sem("piece_weighed")
        s_o = sem("head_output_written")
        s_mst = sem("mixT_stored")
        s_out = sem("outputs_stored")
        s_res = sem("residual_loaded")
        s_mx4 = [sem(f"mix_rows_loaded_{i}") for i in range(2)]
        s_mhi = sem("mix_hi_written")
        s_mlo = sem("mix_lo_written")
        s_wl = [sem(f"weight_tile_loaded_{i}") for i in range(RAW_SLOTS)]
        s_wh = sem("weight_hi_written")
        s_wlow = sem("weight_lo_written")
        s_y = sem("projection_multiplied")
        s_yr = sem("residual_updated")
        s_up = sem("ffn_chunk_multiplied")
        s_ac = sem("ffn_a_copied")
        s_fv = sem("ffn_vectors_copied")
        s_cv = sem("conv_first_tap")
        s_c1 = sem("conv_second_tap")
        s_cs = sem("conv_summed")
        s_sl = sem("silu_written")
        s_u = sem("u_written")
        s_uh = sem("u_hi_written")
        s_ul = sem("u_lo_written")
        s_co = sem("conv_state_kept")
        s_dn = sem("down_multiplied")
        s_dr = sem("down_added")
        s_cvt = sem("conv_state_transposed")
        s_cvc = sem("conv_state_copied")
        s_ft = sem("final_transposed")
        s_fs = sem("final_rstd_ready")
        s_fy = sem("final_written")
        s_yst = [sem(f"final_stored_{i}") for i in range(2)]
        s_gf = sem("final_gain_loaded")
        s_cvi = sem("conv_edges_cleared")
        s_chA = sem("scalar_chain")
        s_chD = sem("vector_chain")
        s_chP = sem("pool_chain")

        def score_bank(i, width):
            return psum[:, 2 * (i % 2):2 * (i % 2) + 2, :].rearrange("p a b -> p (a b)")[:, :width]

        def pieces_done(eng, x):
            eng.wait_ge(s_ptA if COPIER[x[0]] == "A" else s_ptD, COPY_NO[x] + 1)

        class Chain:

            def __init__(self, eng, s):
                self.eng, self.s, self.n = eng, s, 0

            def link(self, ins):
                self.n += 1
                ins.then_inc(self.s, 1)
                self.eng.wait_ge(self.s, self.n)

        w_in_v = I["w_in"].rearrange("(k p) n -> p k n", p=P)
        w_ada_v = I["w_ada"].rearrange("(k p) n -> p k n", p=P)
        n_const = 1 + len(VEC_A) + len(VEC_B) + 1

        def x_rows(t):
            return I["x_prompt"][P * t:P * t + P, :] if t < 8 else I["x_sample"]

        block = ctx.enter_context(nc.Block())

        @block.sync
        def _(sp):
            sp.dma_start(ident[:], I["ident"]).then_inc(s_const, 16)
            for i, vecs in enumerate((VEC_A, VEC_B, [("state_ffn_conv", 44, 0)])):
                for name, rows, at in vecs:
                    sp.dma_start(vec_in[at:at + rows, i, :], I[name]).then_inc(s_const, 16)

            def load_x(t):
                if t >= 2:
                    sp.wait_ge(s_xt, 2 * (t - 1))
                sp.dma_start(x_in[:ROWS[t], t % 2, :], x_rows(t)).then_inc(s_x[t % 2], 16)

            def load_ada(g, slot):
                sp.dma_start(ada_w[:, slot], w_ada_v[:, :, bass.ds(g * 256, 256)]).then_inc(s_ada[slot], 16)

            def load_w_in(g, half):
                sp.dma_start(w_raw[:, half], w_in_v[:, 4 * half:4 * half + 4, bass.ds(g * ZG, ZG)])\
                    .then_inc(s_raw[half], 16)

            load_ada(0, 0)
            load_ada(1, 1)
            load_x(0)
            load_x(1)
            for g in range(2, 8):
                sp.wait_ge(s_adamm, g - 1)
                load_ada(g, g % 2)
                load_x(g)
            load_x(8)
            load_w_in(0, 0)
            load_w_in(0, 1)

            def group_loads(g, last=False):
                if not last:
                    for half in range(2):
                        sp.wait_ge(s_wlo, 2 * g + half + 1)
                        load_w_in(g + 1, half)
                for j in range(2):
                    sp.wait_ge(s_adamm, 2 * g + 7 + j)
                    load_ada(2 * g + 8 + j, j)

            with sp.Fori(0, NZG - 1) as g:
                group_loads(g)
            group_loads(NZG - 1, last=True)
            for j in range(2):
                sp.wait_ge(s_adamm, 21 + j)
                load_ada(22 + j, j)
            sp.wait_ge(s_xeD, NTILE)
            sp.wait_ge(s_xeA, NTILE)
            sp.dma_start(xT_dram, xT[:]).then_inc(s_xst, 16)

            sp.wait_ge(s_z, 9 * NZG)
            sp.wait_ge(s_adamm, ADA_G)
            sp.wait_ge(s_h, 24)
            sp.wait_ge(s_xst, 16)
            for i in range(3):
                sp.wait_ge(s_zst[i], 16 * 3 * NZG)
            for name, tile_ in (("decayT", decayT), ("q_decayT", q_decayT), ("state_decay", state_decay),
                                ("k_decay", k_decay), ("causal", causal)):
                flat = tile_[:]
                if len(flat.shape) == 3:
                    flat = flat.rearrange("p a b -> p (a b)")
                elif len(flat.shape) == 4:
                    flat = flat.rearrange("p a b c -> p (a b c)")
                sp.dma_start(flat, I[name]).then_inc(s_tab, 16)
            sp.dma_start(g_kv[:], I["g_kv_norm"].broadcast_to([P, KVR])).then_inc(s_tab, 16)
            sp.dma_start(g_ret[:], I["g_ret_norm"].broadcast_to([P, 256])).then_inc(s_tab, 16)
            sp.dma_start(w_uq[:], I["w_uq"].rearrange("(k p) n -> p k n", p=P)).then_inc(s_tab, 16)
            for part, lo in ((w_uk, 0), (w_uv, NOPE)):
                for k in range(2):
                    sp.dma_start(part[:, k, :].rearrange("p (h c) -> p h c", h=8),
                                 I["w_ukv"][P * k:P * k + P, :].rearrange("p (h c) -> p h c", h=8)[:, :, lo:lo + 64])\
                        .then_inc(s_tab, 16)
            sp.dma_start(c_lat, I["cache_mla_latent"].rearrange("(j p) c -> p j c", p=P)).then_inc(s_cache, 16)
            sp.dma_start(c_sk, I["cache_sb_k"].rearrange("(j p) c -> p j c", p=P)).then_inc(s_cache, 16)
            sp.dma_start(c_kr, I["cache_mla_krope"].rearrange("(j p) c -> p j c", p=P)).then_inc(s_cache, 16)

            def load_z(m):
                r, t = rows_of(m), SEQ[m]
                sp.dma_start(z_in[:r, m % 2, :], z_dram[P * t:P * t + r, :]).then_inc(s_zi[m % 2], 16)
                sp.dma_start(rope_t[:, m % 2, 0:128], I["rope64"][:, 128 * t:128 * t + 128]).then_inc(s_zi[m % 2], 16)
                sp.dma_start(rope_t[:, m % 2, 128:192], I["rope32"][:, 64 * t:64 * t + 64]).then_inc(s_zi[m % 2], 16)

            def diagonal(of, n):
                heads = of.rearrange("(q two) d e -> two d q e", two=2)
                for two in range(2):
                    lo = 64 * two
                    yield state[lo:lo + 64, n, :, lo:lo + 64], heads[two]

            load_z(0)
            load_z(1)
            sp.dma_start(sv[:, 4:8, :], I["cache_sb_v"].rearrange("(j p) c -> p j c", p=P)).then_inc(s_sv, 16)
            sp.dma_start(sv[:LS, 8, :], z_dram[LP:T, O_SV:O_SV + 256]).then_inc(s_sv, 16)
            sp.dma_start(sv[:, 0:4, :], z_dram[0:512, O_SV:O_SV + 256].rearrange("(j p) c -> p j c", p=P))\
                .then_inc(s_sv, 16)
            sp.wait_ge(s_init, 1)
            for part, heads in diagonal(I["state_ret"].rearrange("(h d) e -> h d e", h=4), 0):
                sp.dma_start(part, heads).then_inc(s_sv, 16)
            for name, at in (("sb_k", O_SK), ("sb_v", O_SV)):
                for who, lo, hi in (("p", 0, LP), ("s", LP, T)):
                    sp.dma_start(O[f"{who}_{name}"].rearrange("a b t h d -> (a b t) (h d)"),
                                 z_dram[lo:hi, at:at + 256]).then_inc(s_out, 16)

            def store_latent(m):
                who, a, r = ("s", 0, LS) if m == 0 else ("p", P * (m - 1), P)
                sp.wait_ge(s_lat, m + 1)
                sp.dma_start(O[f"{who}_mla_latent"].rearrange("a b t c -> (a b t) c")[a:a + r, :], lat[:r, :])\
                    .then_inc(s_latst, 16)
                sp.wait_ge(s_kr, m + 1)
                sp.dma_start(O[f"{who}_mla_krope"].rearrange("a b t c -> (a b t) c")[a:a + r, :], kr[:r, :])\
                    .then_inc(s_latst, 16)

            def store_state(m, name):
                sp.wait_ge(s_fD, read_d(m + 1, 0))
                for part, heads in diagonal(O[name].rearrange("a b h d e -> (a b h) d e"), int(m > 0)):
                    sp.dma_start(heads, part).then_inc(s_out, 16)

            def store_mix(n):
                r, t = rows_of(n), SEQ[n]
                pieces_done(sp, ("X", n, 1))
                sp.dma_start(mixT_dram[:, :, P * t:P * t + r], mixT[:, :, :r]).then_inc(s_mst, 16)

            store_latent(0)
            for n in range(NTILE):
                if n == 0:
                    store_state(0, "s_ret_state")
                if n + 2 < NTILE:
                    sp.wait_ge(s_ret, n + 1)
                    sp.wait_ge(s_gate, n + 1)
                    sp.wait_ge(s_fp, 12 * (n + 1))
                    load_z(n + 2)
                if n + 1 < NTILE:
                    store_latent(n + 1)
                if n == 2:
                    sp.wait_ge(s_o, 12)
                    sp.dma_start(sv[:, 4:8, :], z_dram[512:LP, O_SV:O_SV + 256].rearrange("(j p) c -> p j c", p=P))\
                        .then_inc(s_sv, 16)
                if n:
                    store_mix(n - 1)
            store_state(8, "p_ret_state")
            store_mix(8)
            sp.wait_ge(s_mst, 16 * NTILE)
            sp.wait_ge(s_latst, 32 * NTILE)
            sp.wait_ge(s_out, 16 * 8)
            sp.wait_ge(s_tr, len(ORDER))
            sp.wait_ge(s_ret, NTILE)
            sp.wait_ge(s_o, len(UNITS))

            def load_mix(k):
                if k >= 2:
                    sp.wait_ge(s_mlo, k - 1)
                sp.dma_start(mix_raw[:, k % 2], mixT_dram[:, k, :]).then_inc(s_mx4[k % 2], 16)

            w_o_v = I["w_o"].rearrange("(k p) n -> p k n", p=P)
            w_up_v = I["w_up"].rearrange("(k p) n -> p k n", p=P)

            def load_tile(idx, slot, src, first=False):
                if not first:
                    sp.wait_ge(s_wlow, idx - 2)
                dst = wt_raw[:, slot, :]
                if len(src.shape) == 3:
                    dst = dst.rearrange("p (k n) -> p k n", k=KT)
                sp.dma_start(dst, src).then_inc(s_wl[slot], 16)

            def load_up(idx, slot, f, branch):
                load_tile(idx, slot, w_up_v[:, :, bass.ds(FF * branch + f * P, P)])

            def load_down(idx, slot, f):
                load_tile(idx, slot, I["w_down"][bass.ds(f * P, P), :])

            load_mix(0)
            load_mix(1)
            for d in range(3):
                load_tile(d, d, w_o_v[:, :, P * d:P * d + P], first=True)
            for k in range(2, KT):
                load_mix(k)
            sp.dma_start(res[:], xT_dram).then_inc(s_res, 16)
            for d in range(3, KT):
                load_tile(d, d % 3, w_o_v[:, :, P * d:P * d + P])

            load_up(8, 2, 0, 0)
            load_up(9, 0, 0, 1)
            with sp.Fori(0, NF // 2 - 1) as i:
                for half in range(2):
                    at = 10 + 6 * i + 3 * half
                    load_up(at, 1, 2 * i + 1 + half, 0)
                    load_up(at + 1, 2, 2 * i + 1 + half, 1)
                    load_down(at + 2, 0, 2 * i + half)
            load_up(70, 1, 21, 0)
            load_up(71, 2, 21, 1)
            load_down(72, 0, 20)
            load_down(73, 1, 21)

            sp.wait_ge(s_wlow, 74)
            sp.wait_ge(s_dn, 24 * NF)
            sp.dma_start(g_fin, I["g_final"].broadcast_to([P, D])).then_inc(s_gf, 16)
            sp.wait_ge(s_cvc, 1)
            for who, lo in (("p", 0), ("s", 44)):
                sp.dma_start(O[f"{who}_ffn_conv"].rearrange("a b j (f p) -> (a b j f) p", p=P),
                             conv_rows[lo:lo + 44, :]).then_inc(s_out, 16)
            for t in range(NTILE):
                sp.wait_ge(s_fy, t + 1)
                dst = O["y_prompt"][0, P * t:P * t + P, :] if t < 8 else O["y_sample"][0]
                sp.dma_start(dst, y_out[:ROWS[t], t % 2, :]).then_inc(s_yst[t % 2], 16)
            sp.wait_ge(s_out, 16 * 10)
            sp.wait_ge(s_yst[0], 16 * 5)
            sp.wait_ge(s_yst[1], 16 * 4)

        @block.gpsimd
        def _(pool):
            def store_z(g):
                for t in range(NTILE):
                    pool.wait_ge(s_zc, 9 * g + t + 1)
                    pool.dma_start(z_dram[P * t:P * t + ROWS[t], bass.ds(g * ZG, ZG)],
                                   z_out[:ROWS[t], t % 3, :]).then_inc(s_zst[t % 3], 16)

            with pool.Fori(0, NZG) as g:
                store_z(g)

            ch = Chain(pool, s_chP)
            pool.wait_ge(s_tab, 16 * N_TAB)

            def rope(x, heads, half, table, out, r):
                d = 2 * half

                def tab(a, n):
                    return table[:r, a:a + n].unsqueeze(1).broadcast_to([r, heads, n])

                a = rope_a[:r, :heads * d].rearrange("p (h d) -> p h d", h=heads)
                b = rope_b[:r, :heads * d].rearrange("p (h d) -> p h d", h=heads)
                pool.tensor_tensor(a, x, tab(0, d), ALU.mult)
                pool.tensor_tensor(b[:, :, :half], x[:, :, half:], tab(d, half), ALU.mult)
                ch.link(pool.tensor_tensor(b[:, :, half:], x[:, :, :half], tab(d + half, half), ALU.mult))
                return pool.tensor_tensor(out, a, b, ALU.add)

            def front(m, s):
                r, slot = rows_of(m), m % 2
                if s == 0:
                    pool.wait_ge(s_zi[slot], 48 * (m // 2 + 1))
                    if m:
                        pool.wait_ge(s_latst, 32 * m)
                        pool.wait_ge(s_fp, 12 * m)
                    x = z_in[:r, slot, :]
                    ch.link(rope(x[:, O_KR:O_KR + ROPE].unsqueeze(1), 1, 16, rope_t[:, slot, 128:192],
                                 kr[:r, :].unsqueeze(1), r))
                    pool.sem_inc(s_kr, 1)
                    ch.link(rope(x[:, O_RQ:O_RQ + 512].rearrange("p (h d) -> p h d", h=8), 8, 32,
                                 rope_t[:, slot, 0:128], rqk[:r], r))
                    pool.tensor_tensor(kd[:r], rqk[:r, 4:8, :],
                                       k_decay[:r, int(m == 0), :].unsqueeze(2).broadcast_to([r, H_RET, DH]),
                                       ALU.mult).then_inc(s_rot, 1)
                if s == 1:
                    x = z_in[:r, slot, O_RG:O_RG + 256]
                    pool.wait_ge(s_eg, m + 1)
                    if m:
                        pool.wait_ge(s_ret, m)
                    pool.tensor_scalar(eg[:r], eg[:r], 1.0, None, ALU.add).then_inc(s_g1, 1)
                    ch.link(pool.tensor_tensor(gate[:r], x, g_ret[:r], ALU.mult))
                if s == 2:
                    pool.wait_ge(s_g2, m + 1)
                    pool.tensor_tensor(gate[:r], gate[:r], eg[:r], ALU.mult).then_inc(s_gate, 1)

            def stick_exponents(i):
                n = UNITS[i][0]
                r, w, j = rows_of(n), n_keys(n), count_units("S", i)
                pool.wait_ge(s_c, j + 1)
                pool.tensor_tensor(esb[:r, j % 2, :w], zsb[:r, j % 2, :w], esb[:r, j % 2, :w], ALU.subtract)\
                    .then_inc(s_wa, 1)

            for step in range(-12, STEPS):
                m, s = divmod(step + 12, 12)
                if m < NTILE:
                    front(m, s)
                if 0 <= step - 2 < len(UNITS) and UNITS[step - 2][1] == "S":
                    stick_exponents(step - 2)

        @block.scalar
        def _(act):
            act.preload_act_table_set("natural_log_exp_and_others")
            act.wait_ge(s_vec, 1)
            act.activation(silu_e[:], vec_a[:, 64:80].rearrange("p (c k) -> p c k", c=2), ACT.Exp, scale=-1.0)\
                .then_inc(s_silu, 1)
            for t in range(0, NTILE):
                act.wait_ge(s_xt, 2 * t + 2)
                act.activation(xT[:, 4:8, P * t:P * t + ROWS[t]],
                               bank[2 * (t % 2) + 1][:, :].rearrange("p (k n) -> p k n", k=4)[:, :, :ROWS[t]],
                               ACT.Copy).then_inc(s_xeA, 1)

            def square(n, c, k, j):
                a, b = CHUNKS[c]
                if j >= 2:
                    act.wait_ge(s_ms, 24 * n + j - 1)
                act.activation(norm_bufs[n]["sq"][:, j % 2, :b - a], norm_bufs[n]["x"][:, k, a:b], ACT.Square)\
                    .then_inc(s_sq, 1)

            def squares(n, c):
                for k in range(KT):
                    square(n, c, k, 8 * c + k)

            def rstd(n, c):
                a, b = CHUNKS[c]
                j = 3 * n + c
                out = norm_bufs[n]["rb"][:, a:b]
                act.wait_ge(s_ms, 8 * (j + 1) if n == 0 else 24 + 21 + c + 1)
                act.activation(out, bank[4 if n == 0 else 5 + c][:, :b - a], ACT.Ln, bias=eps[:], scale=1.0 / D)\
                    .then_inc(s_ln, 1)
                act.wait_ge(s_ln, j + 1)
                act.activation(out, out, ACT.Exp, scale=-0.5).then_inc(s_rb, 1)

            def h_high(n, c):
                for k in range(KT):
                    j = 24 * n + 8 * c + k
                    act.wait_ge(s_hn, j + 1)
                    for a, b, which in segments(c):
                        last = act.activation(norm_bufs[n]["hi"][:, k, a:b],
                                              norm_bufs[n]["hn"][:, (8 * c + k) % 3, a - CHUNKS[c][0]:b - CHUNKS[c][0]],
                                              ACT.Identity, bias=mod[:, 24 * n + k, which:which + 1])
                    last.then_inc(s_hhi, 1)

            def norm(n):
                squares(n, 0)
                rstd(n, 0)
                squares(n, 1)
                h_high(n, 0)
                rstd(n, 1)
                squares(n, 2)
                h_high(n, 1)
                rstd(n, 2)
                h_high(n, 2)

            act.wait_ge(s_set, 2)
            act.wait_ge(s_xeD, NTILE)
            act.wait_ge(s_xeA, NTILE)
            norm(0)

            def split_w_in(g, slot):
                for half in range(2):
                    act.wait_ge(s_raw[half], 16 * (g + 1))
                    act.activation(w_hi[:, slot, 4 * half:4 * half + 4], w_raw[:, half], ACT.Copy)\
                        .then_inc(s_whi, 1)

            split_w_in(0, 0)
            split_w_in(1, 1)
            with act.Fori(0, 2) as i:
                for s in range(2):
                    act.wait_ge(s_z, 18 * i + 9 * (s + 1))
                    split_w_in(2 * i + 2 + s, s)
            act.wait_ge(s_z, 9 * 5)
            split_w_in(6, 0)

            ch = Chain(act, s_chA)
            act.wait_ge(s_cT, 1)
            act.activation(c_latT, psum[:, 0:2, :], ACT.Copy).then_inc(s_cA, 1)
            act.wait_ge(s_cT, 3)
            act.activation(kT[64:96, :, 512:1024], bank[4][0:32, :].unsqueeze(1).broadcast_to([32, H_MLA, 512]),
                           ACT.Copy).then_inc(s_cA, 1)
            act.wait_ge(s_cT, 4)
            for q in range(4):
                last = act.activation(kT[0:64, 2 * q, 512:1024], bank[q][0:64, :], ACT.Copy)
            last.then_inc(s_cA, 1)
            act.wait_ge(s_cT, 5)
            act.activation(v_mla[:, 4:6, :], psum[:, 4:6, :], ACT.Copy).then_inc(s_cA, 1)

            def front(m, s):
                r, slot = rows_of(m), m % 2
                b7, col = bank[7], key_col(m)
                x = z_in[:r, slot, :]
                if s == 0:
                    act.wait_ge(s_zi[slot], 48 * (m // 2 + 1))
                    if m:
                        act.wait_ge(s_lat, m)
                    act.activation(junk[:r, :QR], x[:, O_ZQ:O_ZQ + QR], ACT.Square, scale=QR ** -0.5,
                                   accum_out=sums[:r, 0:1])
                    ch.link(act.activation(junk[:r, QR:], x[:, O_KV:O_KV + KVR], ACT.Square, scale=KVR ** -0.5,
                                           accum_out=sums[:r, 1:2]))
                    ch.link(act.activation(rs[:r], sums[:r], ACT.Ln, bias=eps[:r]))
                    act.activation(rs[:r], rs[:r], ACT.Exp, scale=-0.5).then_inc(s_rs, 1)
                    if m:
                        act.wait_ge(s_gate, m)
                    act.activation(eg[:r], x[:, O_RG:O_RG + 256], ACT.Exp, scale=-1.0).then_inc(s_eg, 1)
                if s not in READ_A:
                    return
                act.wait_ge(s_fp, 12 * m + s + 1)
                v4 = b7.rearrange("p (k n) -> p k n", k=4)
                if s == 0:
                    last = act.activation(sqT[:, slot, :, :r], v4[:, 0:2, :r], ACT.Copy, scale=SB_SCALE)
                elif s == 1:
                    last = act.activation(qnT[:, :, :r], v4[:, 0:3, :r], ACT.Copy)
                elif s in (2, 3):
                    q4 = b7[:r, 0:384].rearrange("p (h d) -> p h d", h=4)
                    last = act.activation(qtok[:r, 384 * (s - 2):384 * (s - 1)].rearrange("p (h d) -> p h d", h=4)
                                          [:, :, 0:NOPE], q4[:, :, 0:NOPE], ACT.Copy)
                elif s == 4:
                    last = act.activation(latT[:, :, :r], v4[:, 0:2, :r], ACT.Copy)
                elif s == 5:
                    last = act.activation(qT[:QD, slot, 0:4, :r], v4[:QD, :, :r], ACT.Copy)
                elif s == 7:
                    last = act.activation(kT[0:64, 0:H_MLA:2, col:col + r], v4[0:64, :, :r], ACT.Copy)
                elif s == 8:
                    last = act.activation(v_mla[:r, SEQ[m], :], b7[:r, :], ACT.Copy)
                elif s == 9:
                    if m == 0:
                        act.wait_ge(s_init, 3)
                    for a in range(2):
                        act.activation(rqT[64 * a:64 * a + 64, :, a, :r], v4[64 * a:64 * a + 64, 0:2, :r], ACT.Copy,
                                       scale=DH ** -0.5)
                    last = act.activation(rkT[:, :, :r], v4[:, 2:4, :r], ACT.Copy)
                last.then_inc(s_fA, 1)

            def group_rstd(m):
                r = rows_of(m)
                act.wait_ge(s_var, m + 1)
                ch.link(act.activation(stat[:r, 2, :], stat[:r, 1, :], ACT.Ln, bias=eps[:r], scale=1.0 / DH))
                act.activation(stat[:r, 3, :], stat[:r, 2, :], ACT.Exp, scale=-0.5).then_inc(s_rr, 1)

            def softmax_exp(i):
                n = UNITS[i][0]
                r, w, j = rows_of(n), n_keys(n), count_units("M", i)
                act.wait_ge(s_mx, j + 1)
                if j >= 2:
                    before = max(x for x in range(i) if UNITS[x][1] == "M" and count_units("M", x) == j - 2)
                    nb = len(key_blocks(UNITS[before][0]))
                    act.wait_ge(s_tr, PIECE_NO["M", before, (nb + 3) // 4 - 1] + 1)
                if j >= 4:
                    act.wait_ge(s_o, 1 + PV_NO[[x for x in range(i) if UNITS[x][1] == "M"][-4]])
                act.activation(prob[:r, j % 2, :w], score_bank(i, w)[:r], ACT.Exp, bias=maxes[:r, j % 2, 1:2],
                               scale=MLA_SCALE, accum_out=rowsum[:r, j % 4, 0:1]).then_inc(s_p, 1)

            def stick_log(i):
                n = UNITS[i][0]
                r, w, j = rows_of(n), n_keys(n), count_units("S", i)
                e = esb[:r, j % 2, :w]
                act.wait_ge(s_zsb, j + 1)
                if j >= 2:
                    before = [x for x in range(i) if UNITS[x][1] == "S"][-2]
                    nb = len(key_blocks(UNITS[before][0]))
                    act.wait_ge(s_tr, PIECE_NO["S", before, (nb + 3) // 4 - 1] + 1)
                ch.link(act.activation(e, zsb[:r, j % 2, :w], ACT.Abs))
                ch.link(act.activation(e, e, ACT.Exp, scale=-1.0))
                act.activation(e, e, ACT.Ln, bias=1.0).then_inc(s_l, 1)

            def stick_weights(i):
                n = UNITS[i][0]
                r, w, j = rows_of(n), n_keys(n), count_units("S", i)
                act.wait_ge(s_wa, j + 1)
                act.activation(esb[:r, j % 2, :w], esb[:r, j % 2, :w], ACT.Exp).then_inc(s_w, 1)

            def copy_piece(x):
                kind, i, j = x
                q = PIECE_NO[x]
                act.wait_ge(s_tr, q + 1)
                src = bank[4 + q % 2].rearrange("p (k n) -> p k n", k=4)
                if kind == "X":
                    if i and j == 0:
                        act.wait_ge(s_mst, 16 * i)
                    r = rows_of(i)
                    act.activation(mixT[:, 4 * j:4 * j + 4, :r], src[:, :, :r], ACT.Copy).then_inc(s_ptA, 1)
                    return
                n, wn = UNITS[i][0], W_NO[x]
                r = rows_of(n)
                blocks = key_blocks(n)[4 * j:4 * j + 4]
                if wn >= 4:
                    act.wait_ge(s_pv, wn - 3)
                last = act.activation(pT[:, wn % 4, :len(blocks), :r], src[:, :len(blocks), :r], ACT.Copy)\
                    if blocks[-1][1] == P else None
                if last is None:
                    if len(blocks) > 1:
                        act.activation(pT[:, wn % 4, :len(blocks) - 1, :r], src[:, :len(blocks) - 1, :r], ACT.Copy)
                    last = act.activation(pT[:LS, wn % 4, len(blocks) - 1, :r], src[:LS, len(blocks) - 1, :r], ACT.Copy)
                last.then_inc(s_ptA, 1)

            for step in range(-12, STEPS):
                m, s = divmod(step + 12, 12)
                if 0 <= step < len(UNITS) and UNITS[step][1] == "M":
                    softmax_exp(step)
                for lag, do in ((1, stick_log), (3, stick_weights)):
                    if 0 <= step - lag < len(UNITS) and UNITS[step - lag][1] == "S":
                        do(step - lag)
                for x in PIECES.get(step, []):
                    if COPIER[x[0]] == "A":
                        copy_piece(x)
                if m < NTILE:
                    front(m, s)
                if s == 0 and 0 < m <= NTILE:
                    group_rstd(m - 1)

            def split_hi(n3, raw, slot, first=False):
                act.wait_ge(s_wl[raw], 16 * n3 + 16)
                if not first:
                    idx = 3 * n3 + raw if isinstance(n3, int) else 16
                    if idx < 14:
                        act.wait_ge(s_y, 3 * (idx - 5))
                    elif idx < 16:
                        act.wait_ge(s_up, 3 * (idx - 13))
                    elif raw == 0:
                        act.wait_ge(s_dn, 24 * (n3 - 5))
                    else:
                        act.wait_ge(s_up, 6 * (n3 - 4) + 3 * raw)
                act.activation(wt_hi[:, slot], wt_raw[:, raw], ACT.Copy).then_inc(s_wh, 1)

            for k in range(KT):
                act.wait_ge(s_mx4[k % 2], 16 * (k // 2 + 1))
                act.activation(a_hi[:, k], mix_raw[:, k % 2], ACT.Copy).then_inc(s_mhi, 1)
                if k < 3:
                    split_hi(0, k, k, first=True)
            for idx in range(3, 6):
                split_hi(1, idx % 3, idx, first=True)
            n_sq = 0
            for d in range(KT):
                if d + 6 < 10:
                    split_hi((d + 6) // 3, d % 3, d)
                for c in range(3):
                    act.wait_ge(s_yr, 3 * d + c + 1)
                    if n_sq == 0:
                        act.wait_ge(s_mlo, KT)
                    square(1, c, d, n_sq)
                    n_sq += 1
            rstd(1, 0)
            rstd(1, 1)
            rstd(1, 2)
            for c in range(3):
                h_high(1, c)

            act.preload_act_table_set("silu_and_others")
            act.wait_ge(s_h, 48)

            def copy_a(f, slot, first=False):
                for c in range(3):
                    act.wait_ge(s_up, 6 * f + c + 1)
                    if c == 0 and not first:
                        act.wait_ge(s_cs, f - 1)
                        act.wait_ge(s_co, f - 1)
                    for a, b, which in segments(c):
                        at = a + 2 + 2 * which
                        last = act.activation(a_ext[:, slot, at:at + b - a],
                                              bank[(3 * slot + c) % 2][:, a - CHUNKS[c][0]:b - CHUNKS[c][0]], ACT.Copy)
                    last.then_inc(s_ac, 1)

            def first_tap(f, slot, first=False):
                act.wait_ge(s_ac, 3 * f + 3)
                act.wait_ge(s_fv, f + 1)
                if not first:
                    act.wait_ge(s_u, 3 * f)
                act.activation(conv[:], a_ext[:, slot, 2:T + 4], ACT.Identity, bias=f_vec[:, slot, 3:4],
                               scale=f_vec[:, slot, 2:3]).then_inc(s_cv, 1)

            def silu(f):
                act.wait_ge(s_cs, f + 1)
                act.activation(conv[:], conv[:], ACT.Silu).then_inc(s_sl, 1)

            def u_high(f, slot, c, first=False):
                act.wait_ge(s_u, 3 * f + c + 1)
                if not first and c == 0:
                    act.wait_ge(s_dn, 24 * (f - 1))
                a, b = CHUNKS[c]
                act.activation(u_hi[:, slot, a:b], u_val[:, c % 2, :b - a], ACT.Copy).then_inc(s_uh, 1)

            def ffn_tile(f, slot, tiles, first=False, early=False):
                for n3, raw, ring in tiles[:1]:
                    split_hi(n3, raw, ring)
                copy_a(f, slot, first=early)
                first_tap(f, slot, first)
                for n3, raw, ring in tiles[1:2]:
                    split_hi(n3, raw, ring)
                silu(f)
                for c in range(3):
                    u_high(f, slot, c, first=early)
                for n3, raw, ring in tiles[2:]:
                    split_hi(n3, raw, ring)

            for idx in (10, 11):
                split_hi(idx // 3, idx % 3, idx % 6)
            ffn_tile(0, 0, [(4, 0, 0), (4, 1, 1), (4, 2, 2)], first=True, early=True)
            ffn_tile(1, 1, [(5, 0, 3), (5, 1, 4), (5, 2, 5)], early=True)
            with act.Fori(1, NF // 2 - 1) as i:
                ffn_tile(2 * i, 0, [(2 * i + 4, raw, raw) for raw in range(3)])
                ffn_tile(2 * i + 1, 1, [(2 * i + 5, raw, raw + 3) for raw in range(3)])
            ffn_tile(20, 0, [(24, 0, 0), (24, 1, 1)])
            ffn_tile(21, 1, [])

            act.preload_act_table_set("natural_log_exp_and_others")
            for t in range(NTILE):
                r, slot = ROWS[t], t % 2
                act.wait_ge(s_ft, t + 1)
                full = psum[:r, 2 * slot:2 * slot + 2, :].rearrange("p a b -> p (a b)")
                if t == 0:
                    act.wait_ge(s_wlow, 74)
                ch.link(act.activation(wt_raw[:r, t % 2, :], full, ACT.Square, accum_out=fin[:r, slot, 0:1]))
                ch.link(act.activation(fin[:r, slot, 1:2], fin[:r, slot, 0:1], ACT.Ln, bias=eps[:r], scale=1.0 / D))
                if t >= 2:
                    act.wait_ge(s_fy, t - 1)
                act.activation(fin[:r, slot, 2:3], fin[:r, slot, 1:2], ACT.Exp, scale=-0.5).then_inc(s_fs, 1)

        @block.vector
        def _(dve):
            dve.memset(ones[:], 1.0).then_inc(s_set, 1)
            dve.memset(eps[:], EPS).then_inc(s_set, 1)
            dve.wait_ge(s_vt, 3)
            dve.tensor_copy(vec_a[:], bank[7][:, 0:N_A]).then_inc(s_vec, 1)
            dve.tensor_copy(vec_b[:], bank[7][:, 128:128 + N_B]).then_inc(s_vec, 1)
            dve.tensor_copy(vec_c[:], bank[7][:, 256:256 + N_C]).then_inc(s_vec, 1)
            dve.wait_ge(s_silu, 1)
            dve.tensor_scalar(silu_e[:], silu_e[:], 1.0, None, ALU.add).then_inc(s_silu, 1)
            dve.wait_ge(s_silu, 2)
            dve.reciprocal(silu_e[:], silu_e[:]).then_inc(s_silu, 1)
            dve.wait_ge(s_silu, 3)
            dve.tensor_tensor(silu_c[:], silu_e[:], vec_a[:, 64:80].rearrange("p (c k) -> p c k", c=2), ALU.mult)\
                .then_inc(s_siluv, 1)

            def write_mod(g, slot):
                dve.wait_ge(s_adamm, g + 1)
                dve.tensor_tensor(mod[:, bass.ds(2 * g, 2), :],
                                  bank[5 + slot][:, 0:4].rearrange("p (j c) -> p j c", j=2),
                                  vec_a[:, bass.ds(2 * g, 2)].unsqueeze(2).broadcast_to([P, 2, 2]),
                                  ALU.add).then_inc(s_mod, 1)

            for t in range(NTILE):
                dve.wait_ge(s_xt, 2 * t + 1)
                dve.tensor_copy(xT[:, 0:4, P * t:P * t + ROWS[t]],
                                bank[2 * (t % 2)][:, :].rearrange("p (k n) -> p k n", k=4)[:, :, :ROWS[t]])\
                    .then_inc(s_xeD, 1)
                if t < 8:
                    write_mod(t, t % 2)

            def norm_scale(n):
                dve.scalar_tensor_tensor(out=scale_n[:, n], in0=mod[:, 24 * n + 8:24 * n + 16, :], scalar=1.0,
                                         in1=vec_a[:, 48 + 8 * n:56 + 8 * n].unsqueeze(2).broadcast_to([P, KT, 2]),
                                         op0=ALU.add, op1=ALU.mult).then_inc(s_scale, 1)

            dve.wait_ge(s_mod, 8)
            norm_scale(0)
            dve.wait_ge(s_scale, 1)

            def normed(n, c, k):
                bufs = norm_bufs[n]
                j = 24 * n + 8 * c + k
                if k == 0:
                    dve.wait_ge(s_rb, 3 * n + c + 1)
                if j >= 3:
                    dve.wait_ge(s_h, j - 2)
                for a, b, which in segments(c):
                    last = dve.scalar_tensor_tensor(out=bufs["hn"][:, (8 * c + k) % 3, a - CHUNKS[c][0]:b - CHUNKS[c][0]],
                                                    in0=bufs["x"][:, k, a:b], scalar=scale_n[:, n, k, which:which + 1],
                                                    in1=bufs["rb"][:, a:b], op0=ALU.mult, op1=ALU.mult)
                last.then_inc(s_hn, 1)

            def h_low(n, c, k):
                bufs = norm_bufs[n]
                j = 24 * n + 8 * c + k
                dve.wait_ge(s_hn, j + 1)
                dve.wait_ge(s_hhi, j + 1)
                for a, b, which in segments(c):
                    last = dve.scalar_tensor_tensor(out=bufs["lo"][:, k, a:b],
                                                    in0=bufs["hn"][:, (8 * c + k) % 3, a - CHUNKS[c][0]:b - CHUNKS[c][0]],
                                                    scalar=mod[:, 24 * n + k, which:which + 1],
                                                    in1=bufs["hi"][:, k, a:b].bitcast(F32), op0=ALU.add, op1=ALU.subtract)
                last.then_inc(s_h, 1)

            def norm(n):
                order = [(c, k) for c in range(3) for k in range(KT)]
                for i, (c, k) in enumerate(order):
                    normed(n, c, k)
                    if i:
                        h_low(n, *order[i - 1])
                h_low(n, *order[-1])

            norm(0)

            def split_w_in(g, slot, half):
                dve.wait_ge(s_whi, 2 * g + half + 1)
                dve.tensor_tensor(w_lo[:, slot, 4 * half:4 * half + 4], w_raw[:, half],
                                  w_hi[:, slot, 4 * half:4 * half + 4].bitcast(F32), ALU.subtract)\
                    .then_inc(s_wlo, 1)

            def z_group(g, slot, split_next, first=False):
                for t in range(NTILE):
                    dve.wait_ge(s_z, 9 * g + t + 1)
                    if not first or t >= 3:
                        dve.wait_ge(s_zst[t % 3], 48 * g + 16 * (t // 3))
                    dve.tensor_copy(z_out[:ROWS[t], t % 3, :], bank[t % 3][:ROWS[t], 0:ZG]).then_inc(s_zc, 1)
                    if split_next and t in (2, 4):
                        split_w_in(g + 1, 1 - slot, t // 2 - 1)
                for j in range(2):
                    write_mod(2 * g + 8 + j, j)

            split_w_in(0, 0, 0)
            split_w_in(0, 0, 1)
            z_group(0, 0, True, first=True)
            z_group(1, 1, True)
            with dve.Fori(1, 3) as i:
                for s in range(2):
                    z_group(2 * i + s, s, True)
            z_group(NZG - 1, 0, False)
            for j in range(2):
                write_mod(22 + j, j)
            dve.wait_ge(s_mod, ADA_G)
            norm_scale(1)

            ch = Chain(dve, s_chD)
            dve.wait_ge(s_z, 9 * NZG)
            dve.wait_ge(s_adamm, ADA_G)
            dve.wait_ge(s_xst, 16)
            for i in range(3):
                dve.wait_ge(s_zst[i], 16 * 3 * NZG)
            dve.memset(state[:], 0.0).then_inc(s_init, 1)
            dve.memset(zeros[:], 0.0).then_inc(s_init, 1)
            dve.memset(rqT[:], 0.0).then_inc(s_init, 1)
            dve.wait_ge(s_tab, 16 * N_TAB)
            for k in range(3):
                last = dve.tensor_scalar(w_uq[:, k, :], w_uq[:, k, :], vec_a[:, 80 + k:81 + k], None, ALU.mult)
            last.then_inc(s_wuq, 1)
            dve.wait_ge(s_cT, 2)
            dve.tensor_copy(skT[:, :, 512:1024], psum[:, 2:4, :]).then_inc(s_cD, 1)
            dve.wait_ge(s_cT, 4)
            for q in range(4):
                last = dve.tensor_copy(kT[0:64, 2 * q + 1, 512:1024], bank[q][64:128, :])
            last.then_inc(s_cD, 1)
            dve.wait_ge(s_cT, 6)
            dve.tensor_copy(v_mla[:, 6:8, :], psum[:, 6:8, :]).then_inc(s_cD, 1)

            def front(m, s):
                r, slot = rows_of(m), m % 2
                b7, col = bank[7], key_col(m)
                v4 = b7.rearrange("p (k n) -> p k n", k=4)
                x = z_in[:r, slot, :]
                if s == 0:
                    dve.wait_ge(s_rs, m + 1)
                    if m:
                        dve.wait_ge(s_fp, 12 * m)
                        dve.wait_ge(s_latst, 32 * m)
                    dve.tensor_scalar(zqn[:r], x[:, O_ZQ:O_ZQ + QR], rs[:r, 0:1], None, ALU.mult)
                    dve.scalar_tensor_tensor(out=lat[:r], in0=x[:, O_KV:O_KV + KVR], scalar=rs[:r, 1:2],
                                             in1=g_kv[:r], op0=ALU.mult, op1=ALU.mult).then_inc(s_lat, 1)
                if s == 1:
                    dve.wait_ge(s_g1, m + 1)
                    dve.reciprocal(eg[:r], eg[:r]).then_inc(s_g2, 1)
                if s not in READ_D:
                    return
                dve.wait_ge(s_fp, 12 * m + s + 1)
                if s in READ_A and s != 7:
                    dve.wait_ge(s_fA, read_a(m, s) + 1)
                if s == 0:
                    last = dve.tensor_copy(skT[:, :, col:col + r], v4[:, 2:4, :r])
                elif s in (2, 3):
                    q4 = b7[:r, 0:384].rearrange("p (h d) -> p h d", h=4)

                    def tab(a, n):
                        return rope_t[:r, slot, 128 + a:128 + a + n].unsqueeze(1).broadcast_to([r, 4, n])

                    if not (m == 0 and s == 2):
                        dve.wait_ge(s_fD, read_d(m, s))
                    dve.tensor_tensor(q_a[:r], q4[:, :, NOPE:QD], tab(0, ROPE), ALU.mult)
                    dve.tensor_tensor(q_b[:r, :, 0:16], q4[:, :, NOPE + 16:QD], tab(32, 16), ALU.mult)
                    ch.link(dve.tensor_tensor(q_b[:r, :, 16:32], q4[:, :, NOPE:NOPE + 16], tab(48, 16), ALU.mult))
                    last = dve.tensor_tensor(qtok[:r, 384 * (s - 2):384 * (s - 1)]
                                             .rearrange("p (h d) -> p h d", h=4)[:, :, NOPE:QD],
                                             q_a[:r], q_b[:r], ALU.add)
                elif s == 4:
                    last = dve.tensor_copy(kT[64:96, :, col:col + r],
                                           v4[0:32, 2, :r].unsqueeze(1).broadcast_to([32, H_MLA, r]))
                elif s == 6:
                    last = dve.tensor_copy(qT[:QD, slot, 4:8, :r], v4[:QD, :, :r])
                elif s == 7:
                    last = dve.tensor_copy(kT[0:64, 1:H_MLA:2, col:col + r], v4[64:128, :, :r])
                elif s == 9:
                    last = dve.tensor_tensor(rqdT[:, :, :r], v4[:, 0:2, :r], q_decayT[:, :, :r], ALU.mult)
                elif s == 10:
                    last = dve.tensor_tensor(att[:r, :, :r], v4[:r, :, :r], decayT[:r, :, :r], ALU.mult)
                elif s == 11:
                    st = state[:, int(m > 0)]
                    o4 = b7[:r, 0:256].rearrange("p (h d) -> p h d", h=4)
                    ch.link(dve.tensor_tensor(st, st, state_decay[:, int(m == 0)], ALU.mult))
                    dve.tensor_reduce(stat[:r, 0, :], o4, AX, ALU.add)
                    dve.tensor_tensor(st[0:64, :, 0:64], st[0:64, :, 0:64], v4[0:64, 2:4, 0:64], ALU.add)
                    ch.link(dve.tensor_tensor(st[64:128, :, 64:128], st[64:128, :, 64:128], v4[64:128, 2:4, 64:128],
                                              ALU.add))
                    ch.link(dve.tensor_scalar(stat[:r, 0, :], stat[:r, 0, :], -1.0 / DH, None, ALU.mult))
                    last = dve.tensor_tensor(oc[:r], o4, stat[:r, 0, :].unsqueeze(2).broadcast_to([r, H_RET, DH]),
                                             ALU.add)
                last.then_inc(s_fD, 1)
                if s == 11:
                    dve.wait_ge(s_fD, read_d(m + 1, 0))
                    ch.link(dve.tensor_tensor(oc2[:r], oc[:r], oc[:r], ALU.mult))
                    dve.tensor_reduce(stat[:r, 1, :], oc2[:r], AX, ALU.add).then_inc(s_var, 1)

            def retention_out(m):
                r = rows_of(m)
                dve.wait_ge(s_rr, m + 1)
                ch.link(dve.tensor_tensor(oc[:r], oc[:r], stat[:r, 3, :].unsqueeze(2).broadcast_to([r, H_RET, DH]),
                                          ALU.mult))
                dve.wait_ge(s_gate, m + 1)
                dve.tensor_tensor(mixtok[:r, m % 2, 512:768], oc[:r].rearrange("p h d -> p (h d)"), gate[:r],
                                  ALU.mult).then_inc(s_ret, 1)

            def row_max(i):
                n = UNITS[i][0]
                r, w, j = rows_of(n), n_keys(n), count_units("M", i)
                dve.wait_ge(s_sc, i + 1)
                if n:
                    ch.link(dve.memset(score_bank(i, w)[0:64, w - 64:w], NEG))
                if j >= 2:
                    dve.wait_ge(s_p, j - 1)
                ch.link(dve.tensor_reduce(maxes[:r, j % 2, 0:1], score_bank(i, w)[:r], AX, ALU.max))
                dve.tensor_scalar(maxes[:r, j % 2, 1:2], maxes[:r, j % 2, 0:1], -MLA_SCALE, None, ALU.mult)\
                    .then_inc(s_mx, 1)

            def stick_logits(i):
                n = UNITS[i][0]
                r, w, j = rows_of(n), n_keys(n), count_units("S", i)
                dve.wait_ge(s_sc, i + 1)
                if j >= 2:
                    dve.wait_ge(s_wa, j - 1)
                if w > r:
                    dve.tensor_copy(zsb[:r, j % 2, :w - r], score_bank(i, w)[:r, :w - r])
                dve.tensor_tensor(zsb[:r, j % 2, w - r:w], score_bank(i, w)[:r, w - r:w], causal[:r, :r], ALU.add)\
                    .then_inc(s_zsb, 1)

            def stick_sums(i):
                n = UNITS[i][0]
                r, w, j = rows_of(n), n_keys(n), count_units("S", i)
                e = esb[:r, j % 2, :w]
                dve.wait_ge(s_l, j + 1)
                ch.link(dve.scalar_tensor_tensor(out=e, in0=zsb[:r, j % 2, :w], scalar=0.0, in1=e, op0=ALU.max,
                                                 op1=ALU.add))
                back = e[:, ::-1]
                dve.tensor_tensor_scan(back, back, zeros[:r, :w], 0.0, ALU.add, ALU.add).then_inc(s_c, 1)

            def copy_piece(x):
                kind, i, j = x
                q, wn = PIECE_NO[x], W_NO[x]
                n = UNITS[i][0]
                r = rows_of(n)
                blocks = key_blocks(n)[4 * j:4 * j + 4]
                dve.wait_ge(s_tr, q + 1)
                if wn >= 4:
                    dve.wait_ge(s_pv, wn - 3)
                src = bank[4 + q % 2].rearrange("p (k n) -> p k n", k=4)
                full = len(blocks) - (blocks[-1][1] < P)
                if full:
                    last = dve.tensor_copy(pT[:, wn % 4, :full, :r], src[:, :full, :r])
                if full < len(blocks):
                    last = dve.tensor_copy(pT[:LS, wn % 4, full, :r], src[:LS, full, :r])
                last.then_inc(s_ptD, 1)

            def head_output(i):
                n, kind, h = UNITS[i]
                r, v = rows_of(n), PV_NO[i]
                nb = len(key_blocks(n))
                o = bank[6][:r, 64 * (v % 8):64 * (v % 8) + 64]
                if kind == "M":
                    j = count_units("M", i)
                    dve.wait_ge(s_p, j + 1)
                    ch.link(dve.reciprocal(rowsum[:r, j % 4, 1:2], rowsum[:r, j % 4, 0:1]))
                    dve.wait_ge(s_pv, W_NO[kind, i, (nb + 3) // 4 - 1] + 1)
                    dve.tensor_scalar(mixtok[:r, n % 2, 64 * h:64 * h + 64], o, rowsum[:r, j % 4, 1:2], None,
                                      ALU.mult).then_inc(s_o, 1)
                else:
                    dve.wait_ge(s_pv, W_NO[kind, i, (nb + 3) // 4 - 1] + 1)
                    dve.tensor_copy(mixtok[:r, n % 2, 768 + 64 * h:832 + 64 * h], o).then_inc(s_o, 1)

            for step in range(-12, STEPS):
                m, s = divmod(step + 12, 12)
                if 0 <= step < len(UNITS):
                    (row_max if UNITS[step][1] == "M" else stick_logits)(step)
                if 0 <= step - 2 < len(UNITS) and UNITS[step - 2][1] == "S":
                    stick_sums(step - 2)
                for x in PIECES.get(step - 1, []):
                    if x[0] != "X" and x[2] == 0:
                        head_output(x[1])
                for x in PIECES.get(step, []):
                    if COPIER[x[0]] == "D":
                        copy_piece(x)
                if s == 0 and 0 < m <= NTILE:
                    retention_out(m - 1)
                if m < NTILE:
                    front(m, s)

            def split_lo(n3, raw, slot):
                dve.wait_ge(s_wh, 3 * n3 + raw + 1)
                dve.tensor_tensor(wt_lo[:, slot], wt_raw[:, raw], wt_hi[:, slot].bitcast(F32), ALU.subtract)\
                    .then_inc(s_wlow, 1)

            for k in range(KT):
                dve.wait_ge(s_mhi, k + 1)
                dve.tensor_tensor(a_lo[:, k], mix_raw[:, k % 2], a_hi[:, k].bitcast(F32), ALU.subtract)\
                    .then_inc(s_mlo, 1)
                if k < 3:
                    split_lo(0, k, k)
            for idx in range(3, 6):
                split_lo(1, idx % 3, idx)
            dve.wait_ge(s_res, 16)
            for d in range(KT):
                for c in range(3):
                    dve.wait_ge(s_y, 3 * d + c + 1)
                    for a, b, which in segments(c):
                        last = dve.scalar_tensor_tensor(
                            out=res[:, d, a:b], in0=bank[(3 * d + c) % 5][:, a - CHUNKS[c][0]:b - CHUNKS[c][0]],
                            scalar=mod[:, 16 + d, which:which + 1], in1=res[:, d, a:b], op0=ALU.mult, op1=ALU.add)
                    last.then_inc(s_yr, 1)
                if d + 6 < 10:
                    split_lo((d + 6) // 3, d % 3, d)
            norm(1)

            dve.memset(a_ext[:, 0, 0:2], 0.0).then_inc(s_cvi, 1)
            dve.memset(a_ext[:, 1, 0:2], 0.0).then_inc(s_cvi, 1)
            b_taps = vec_b[:].rearrange("p (j f) -> p f j", j=4)
            b_state = vec_c[:].rearrange("p (j f) -> p f j", j=2)

            def vectors(f, slot, first=False):
                if not first:
                    dve.wait_ge(s_cv, f - 1)
                    dve.wait_ge(s_cs, f - 1)
                dve.tensor_copy(f_vec[:, slot, :].unsqueeze(1), b_taps[:, bass.ds(f, 1), :])
                dve.tensor_copy(a_ext[:, slot, LP + 2:LP + 4].unsqueeze(1), b_state[:, bass.ds(f, 1), :])\
                    .then_inc(s_fv, 1)

            def taps(f, slot):
                dve.wait_ge(s_cv, f + 1)
                dve.scalar_tensor_tensor(out=conv[:], in0=a_ext[:, slot, 1:T + 3], scalar=f_vec[:, slot, 1:2],
                                         in1=conv[:], op0=ALU.mult, op1=ALU.add).then_inc(s_c1, 1)
                for j, at in enumerate((LP, T + 2)):
                    last = dve.tensor_copy(conv_out[:, 2 * j:2 * j + 2, bass.ds(f, 1)],
                                           a_ext[:, slot, at:at + 2].unsqueeze(2))
                last.then_inc(s_co, 1)
                dve.wait_ge(s_c1, f + 1)
                dve.scalar_tensor_tensor(out=conv[:], in0=a_ext[:, slot, 0:T + 2], scalar=f_vec[:, slot, 0:1],
                                         in1=conv[:], op0=ALU.mult, op1=ALU.add).then_inc(s_cs, 1)

            def gate_u(f, slot, c):
                dve.wait_ge(s_up, 6 * f + 4 + c)
                if c == 0:
                    dve.wait_ge(s_sl, f + 1)
                if not (isinstance(f, int) and 3 * f + c < 2):
                    dve.wait_ge(s_ul, 3 * f + c - 1)
                for a, b, which in segments(c):
                    last = dve.tensor_tensor(u_val[:, c % 2, a - CHUNKS[c][0]:b - CHUNKS[c][0]],
                                             bank[2 + (3 * slot + c) % 2][:, a - CHUNKS[c][0]:b - CHUNKS[c][0]],
                                             conv[:, a + 2 * which:b + 2 * which], ALU.mult)
                last.then_inc(s_u, 1)

            def u_low(f, slot, c):
                a, b = CHUNKS[c]
                dve.wait_ge(s_uh, 3 * f + c + 1)
                dve.tensor_tensor(u_lo[:, slot, a:b], u_val[:, c % 2, :b - a], u_hi[:, slot, a:b].bitcast(F32),
                                  ALU.subtract).then_inc(s_ul, 1)

            def add_down(f, n):
                for q in range(4 * n, 4 * n + 4):
                    d, c = divmod(q, 3)
                    dve.wait_ge(s_dn, 24 * f + q + 1)
                    for a, b, which in segments(c):
                        last = dve.scalar_tensor_tensor(
                            out=res[:, d, a:b], in0=bank[4 + q % 4][:, a - CHUNKS[c][0]:b - CHUNKS[c][0]],
                            scalar=mod[:, 40 + d, which:which + 1], in1=res[:, d, a:b], op0=ALU.mult, op1=ALU.add)
                    last.then_inc(s_dr, 1)

            def ffn_tile(f, slot, tiles, early=False, down=True):
                vectors(f, slot, first=early)
                for n in range(6):
                    if n == 4:
                        gate_u(f, slot, 0)
                    if n == 5:
                        gate_u(f, slot, 1)
                        u_low(f, slot, 0)
                    if n == 0 and tiles:
                        split_lo(*tiles[0])
                    if n == 3:
                        taps(f, slot)
                        if len(tiles) > 1:
                            split_lo(*tiles[1])
                    if down:
                        add_down(f - 1, n)
                u_low(f, slot, 1)
                gate_u(f, slot, 2)
                u_low(f, slot, 2)
                for t in tiles[2:]:
                    split_lo(*t)

            for idx in (10, 11):
                split_lo(idx // 3, idx % 3, idx % 6)
            ffn_tile(0, 0, [(4, 0, 0), (4, 1, 1), (4, 2, 2)], early=True, down=False)
            ffn_tile(1, 1, [(5, 0, 3), (5, 1, 4), (5, 2, 5)], early=True)
            with dve.Fori(1, NF // 2 - 1) as i:
                ffn_tile(2 * i, 0, [(2 * i + 4, raw, raw) for raw in range(3)])
                ffn_tile(2 * i + 1, 1, [(2 * i + 5, raw, raw + 3) for raw in range(3)])
            ffn_tile(20, 0, [(24, 0, 0), (24, 1, 1)])
            ffn_tile(21, 1, [])
            for n in range(6):
                add_down(21, n)

            dve.wait_ge(s_cvt, 1)
            dve.tensor_copy(conv_rows[0:88, :], bank[7][0:88, 0:P]).then_inc(s_cvc, 1)
            dve.wait_ge(s_gf, 16)
            for t in range(NTILE):
                r, slot = ROWS[t], t % 2
                dve.wait_ge(s_fs, t + 1)
                if t >= 2:
                    dve.wait_ge(s_yst[slot], 16 * (t // 2))
                dve.scalar_tensor_tensor(out=y_out[:r, slot], in0=psum[:r, 2 * slot:2 * slot + 2, :]
                                         .rearrange("p a b -> p (a b)"), scalar=fin[:r, slot, 2:3], in1=g_fin[:r],
                                         op0=ALU.mult, op1=ALU.mult).then_inc(s_fy, 1)

        @block.tensor
        def _(pe):
            pe.wait_ge(s_const, 16 * n_const)
            for i, n in enumerate((N_A, N_B, N_C)):
                pe.transpose(bank[7][:, 128 * i:128 * i + n], vec_in[:n, i, :], ident[:n, :n]).then_inc(s_vt, 1)

            def ada_group(n, slot):
                pe.wait_ge(s_ada[slot], 16 * n + 16)
                if not isinstance(n, int) or n:
                    pe.wait_ge(s_mod, 2 * n + slot - 1)
                for j in range(2):
                    for k in range(KT):
                        last = pe.matmul(bank[5 + slot][:, 2 * j:2 * j + 2], ada_w[:, slot, k, P * j:P * j + P],
                                         silu_c[:, :, k], start=(k == 0), stop=(k == KT - 1))
                last.then_inc(s_adamm, 1)

            def x_transposes(t):
                pe.wait_ge(s_x[t % 2], 16 * (t // 2 + 1))
                if t >= 2:
                    pe.wait_ge(s_xeD, t - 1)
                    pe.wait_ge(s_xeA, t - 1)
                for j in range(2):
                    for k in range(4):
                        last = pe.transpose(bank[2 * (t % 2) + j][:, P * k:P * k + ROWS[t]],
                                            x_in[:ROWS[t], t % 2, P * (4 * j + k):P * (4 * j + k) + P],
                                            ident[:ROWS[t], :ROWS[t]])
                    last.then_inc(s_xt, 1)

            x_transposes(0)
            x_transposes(1)
            pe.wait_ge(s_siluv, 1)
            for g in range(8):
                ada_group(g // 2, g % 2)
                if g + 2 < NTILE:
                    x_transposes(g + 2)

            def sum_squares(n, c):
                a, b = CHUNKS[c]
                for k in range(KT):
                    j = 24 * n + 8 * c + k
                    if j == 0:
                        pe.wait_ge(s_set, 2)
                    if k == 0 and 3 * n + c > 0:
                        pe.wait_ge(s_ln, 3 * n + c)
                    pe.wait_ge(s_sq, j + 1)
                    pe.matmul(bank[4][:, :b - a], ones[:], sq[:, k % 2, :b - a], start=(k == 0), stop=(k == KT - 1))\
                        .then_inc(s_ms, 1)

            for c in range(3):
                sum_squares(0, c)

            def z_group(g, slot, first=False):
                pe.wait_ge(s_wlo, 2 * g + 2)
                for t in range(NTILE):
                    r = ROWS[t]
                    if first:
                        pe.wait_ge(s_h, 8 * (chunk_of(t) + 1))
                    if not first or t >= 3:
                        pe.wait_ge(s_zc, 9 * g + t - 2)
                    for k in range(KT):
                        for m, (hh, ww) in enumerate(((h_hi, w_hi), (h_hi, w_lo), (h_lo, w_hi))):
                            last = pe.matmul(bank[t % 3][:r, 0:ZG], hh[:, k, P * t:P * t + r], ww[:, slot, k, :],
                                             start=(k == 0 and m == 0), stop=(k == KT - 1 and m == 2))
                    last.then_inc(s_z, 1)
                for j in range(2):
                    ada_group(g + 4, j)

            z_group(0, 0, first=True)
            with pe.Fori(0, 3) as i:
                for s in range(2):
                    z_group(2 * i + 1 + s, 1 - s)
            ada_group(11, 0)
            ada_group(11, 1)

            pe.wait_ge(s_cache, 48)
            pe.wait_ge(s_zc, 9 * NZG)
            pe.wait_ge(s_mod, ADA_G)
            pe.wait_ge(s_ln, 3)
            for j in range(4):
                for k in range(2):
                    last = pe.transpose(bank[k][:, P * j:P * j + P], c_lat[:, j, P * k:P * k + P], ident[:])
            last.then_inc(s_cT, 1)
            for j in range(4):
                for k in range(2):
                    last = pe.transpose(bank[2 + k][:, P * j:P * j + P], c_sk[:, j, P * k:P * k + P], ident[:])
            last.then_inc(s_cT, 1)
            for j in range(4):
                last = pe.transpose(bank[4][0:32, P * j:P * j + P], c_kr[:, j, :], ident[:])
            last.then_inc(s_cT, 1)

            def nope_keys(out, q, lhs_latT, n):
                for k in range(2):
                    last = pe.matmul(out, w_uk[:, k, P * q:P * q + P], lhs_latT[:, k, :n], start=(k == 0), stop=(k == 1))
                return last

            def values(out, latT_tile, r):
                for k in range(2):
                    last = pe.matmul(out, latT_tile[:, k, :r], w_uv[:, k, :], start=(k == 0), stop=(k == 1))
                return last

            pe.wait_ge(s_tab, 16 * N_TAB)
            pe.wait_ge(s_cA, 1)
            pe.wait_ge(s_cD, 1)
            for q in range(4):
                last = nope_keys(bank[q], q, c_latT, 512)
            last.then_inc(s_cT, 1)
            pe.wait_ge(s_cA, 2)
            for j in range(4):
                last = values(bank[4 + j], c_latT[:, :, P * j:P * j + P], P)
                if j % 2:
                    last.then_inc(s_cT, 1)

            def front(m, s):
                r, slot, b7 = rows_of(m), m % 2, bank[7]
                x = z_in[:r, slot, :]

                def turn(at, src, width):
                    return pe.transpose(b7[:width, P * at:P * at + r], src, ident[:r, :r])

                if m == 0 and s == 0:
                    pe.wait_ge(s_cD, 3)
                else:
                    pe.wait_ge(s_fA, read_a(m, s))
                    pe.wait_ge(s_fD, read_d(m, s))
                if s == 0:
                    pe.wait_ge(s_zi[slot], 48 * (m // 2 + 1))
                    for j, at in enumerate((O_SQ, O_SQ + P, O_SK, O_SK + P)):
                        last = turn(j, x[:, at:at + P], P)
                elif s == 1:
                    pe.wait_ge(s_lat, m + 1)
                    for k in range(3):
                        last = turn(k, zqn[:r, P * k:P * k + P], P)
                elif s in (2, 3):
                    if m == 0 and s == 2:
                        pe.wait_ge(s_wuq, 1)
                    for k in range(3):
                        last = pe.matmul(b7[:r, 0:384], qnT[:, k, :r], w_uq[:, k, 384 * (s - 2):384 * (s - 1)],
                                         start=(k == 0), stop=(k == 2))
                elif s == 4:
                    pe.wait_ge(s_kr, m + 1)
                    for k in range(2):
                        turn(k, lat[:r, P * k:P * k + P], P)
                    last = turn(2, kr[:r, :], ROPE)
                elif s in (5, 6):
                    for j in range(4):
                        h = 4 * (s - 5) + j
                        last = turn(j, qtok[:r, QD * h:QD * h + QD], QD)
                elif s == 7:
                    for q in range(4):
                        last = nope_keys(b7[:, P * q:P * q + r], q, latT, r)
                elif s == 8:
                    last = values(b7[:r, :], latT, r)
                elif s == 9:
                    pe.wait_ge(s_rot, m + 1)
                    for j in range(4):
                        last = turn(j, rqk[:r].rearrange("p h d -> p (h d)")[:, P * j:P * j + P], P)
                elif s == 10:
                    for q in range(2):
                        last = pe.matmul(b7[:r, 256 * q:256 * q + 256].rearrange("p (a n) -> p a n", a=2)[:, :, :r],
                                         rkT[:, q, :r], rqT[:, q, :, :r], start=True, stop=True)
                elif s == 11:
                    if m == 0:
                        pe.wait_ge(s_sv, 80)
                    kd2 = kd[:r].rearrange("p h d -> p (h d)")
                    for q in range(2):
                        pe.matmul(b7[:, 256 + P * q:256 + P * q + P], kd2[:, P * q:P * q + P],
                                  x[:, O_RV + P * q:O_RV + P * q + P], start=True, stop=True)
                    for q in range(2):
                        pe.matmul(b7[:r, P * q:P * q + P], rqdT[:, q, :r], state[:, int(m > 0), q, :],
                                  start=True, stop=False)
                        for a in range(2):
                            h = 2 * q + a
                            last = pe.matmul(b7[:r, DH * h:DH * h + DH], att[:r, h, :r],
                                             x[:, O_RV + DH * h:O_RV + DH * h + DH], start=False, stop=(a == 1))
                last.then_inc(s_fp, 1)

            def scores(i):
                n, kind, h = UNITS[i]
                r, slot, w = rows_of(n), n % 2, n_keys(n)
                first = key_blocks(n)[0][0]
                if i >= 2:
                    if UNITS[i - 2][1] == "M":
                        pe.wait_ge(s_p, count_units("M", i - 2) + 1)
                    else:
                        pe.wait_ge(s_zsb, count_units("S", i - 2) + 1)
                for a in range(0, w, 512):
                    b = min(w, a + 512)
                    out = score_bank(i, w)[:r, a:b]
                    if kind == "M":
                        last = pe.matmul(out, qT[:QD, slot, h, :r], kT[:QD, h, first + a:first + b],
                                         start=True, stop=True)
                    else:
                        lo = 64 * (h % 2)
                        last = pe.matmul(out, sqT[lo:lo + 64, slot, h // 2, :r],
                                         skT[lo:lo + 64, h // 2, first + a:first + b], start=True, stop=True)
                last.then_inc(s_sc, 1)

            def transposes(x):
                kind, i, j = x
                q = PIECE_NO[x]
                if q >= 2:
                    pieces_done(pe, ORDER[q - 2])
                out = bank[4 + q % 2]
                if kind == "X":
                    r = rows_of(i)
                    if j == 0:
                        pe.wait_ge(s_ret, i + 1)
                        pe.wait_ge(s_o, 12 * (i + 1))
                    for k in range(4):
                        last = pe.transpose(out[:, P * k:P * k + r],
                                            mixtok[:r, i % 2, P * (4 * j + k):P * (4 * j + k) + P], ident[:r, :r])
                else:
                    n = UNITS[i][0]
                    r, u = rows_of(n), count_units(kind, i)
                    pe.wait_ge(s_p if kind == "M" else s_w, u + 1)
                    src = (prob if kind == "M" else esb)[:r, u % 2, :]
                    first = key_blocks(n)[0][0]
                    for k, (col, size, _) in enumerate(key_blocks(n)[4 * j:4 * j + 4]):
                        last = pe.transpose(out[:size, P * k:P * k + r], src[:, col - first:col - first + size],
                                            ident[:r, :r])
                last.then_inc(s_tr, 1)

            def weigh(i):
                n, kind, h = UNITS[i]
                r, v = rows_of(n), PV_NO[i]
                if v:
                    pe.wait_ge(s_o, v)
                if kind == "S":
                    pe.wait_ge(s_sv, 80 if n < 5 else 96)
                blocks = key_blocks(n)
                for k, (_, size, tile_) in enumerate(blocks):
                    x = (kind, i, k // 4)
                    if k % 4 == 0:
                        pieces_done(pe, x)
                    vals = v_mla[:size, tile_, 64 * h:64 * h + 64] if kind == "M" else \
                        sv[:size, tile_, 64 * h:64 * h + 64]
                    last = pe.matmul(bank[6][:r, 64 * (v % 8):64 * (v % 8) + 64], pT[:size, W_NO[x] % 4, k % 4, :r],
                                     vals, start=(k == 0), stop=(k == len(blocks) - 1))
                    if k % 4 == 3 or k == len(blocks) - 1:
                        last.then_inc(s_pv, 1)

            for step in range(-12, STEPS):
                m, s = divmod(step + 12, 12)
                if 0 <= step < len(UNITS):
                    scores(step)
                for x in PIECES.get(step - 1, []):
                    if x[0] != "X" and x[2] == 0:
                        weigh(x[1])
                for x in PIECES.get(step, []):
                    transposes(x)
                if m < NTILE:
                    front(m, s)

            pieces_done(pe, ORDER[-1])
            pieces_done(pe, ORDER[-2])
            pe.wait_ge(s_mlo, KT)
            thirds = ((wt_hi, a_hi), (wt_lo, a_hi), (wt_hi, a_lo))

            def project(out, c, slot, last_pass=None):
                a, b = CHUNKS[c]
                for k in range(KT):
                    for m, (ww, aa) in enumerate(thirds):
                        last = pe.matmul(out[:, :b - a], ww[:, slot, P * k:P * k + P], aa[:, k, a:b],
                                         start=(k == 0 and m == 0), stop=(k == KT - 1 and m == 2))
                return last

            def sum_square(j):
                c = j % 3
                a, b = CHUNKS[c]
                pe.wait_ge(s_sq, 24 + j + 1)
                pe.matmul(bank[5 + c][:, :b - a], ones[:], norm_bufs[1]["sq"][:, j % 2, :b - a],
                          start=(j < 3), stop=(j >= 21)).then_inc(s_ms, 1)

            for d in range(KT):
                pe.wait_ge(s_wlow, d + 1)
                for c in range(3):
                    q = 3 * d + c
                    if q >= 5:
                        pe.wait_ge(s_yr, q - 4)
                    last = project(bank[q % 5], c, d % 6)
                    last.then_inc(s_y, 1)
                    if q >= 2:
                        sum_square(q - 2)
            sum_square(22)
            sum_square(23)

            def up(f, slot, ring_a, ring_b, tile_no, ring_down=None, first=False):
                for n in range(6):
                    branch, c = divmod(n, 3)
                    if c == 0:
                        pe.wait_ge(s_wlow, tile_no + branch + 1)
                    if first and branch == 0:
                        pe.wait_ge(s_h, 24 + 8 * (c + 1))
                    if branch == 0 and not (first and c < 2):
                        pe.wait_ge(s_ac, 3 * f + c - 1)
                    if branch == 1 and not (first and c < 2):
                        pe.wait_ge(s_u, 3 * f + c - 1)
                    last = project(bank[2 * branch + (3 * slot + c) % 2], c, ring_b if branch else ring_a)
                    last.then_inc(s_up, 1)
                    if ring_down is not None:
                        down(f - 1, 1 - slot, ring_down, tile_no + 2, n, first=first)

            def down(f, slot, ring, tile_no, n, first=False, very_first=False):
                if n == 0:
                    pe.wait_ge(s_wlow, tile_no + 1)
                    pe.wait_ge(s_ul, 3 * f + 3)
                for q in range(4 * n, 4 * n + 4):
                    d, c = divmod(q, 3)
                    a, b = CHUNKS[c]
                    if not (isinstance(f, int) and f == 0 and q < 4):
                        pe.wait_ge(s_dr, 24 * f + q - 3)
                    for m, (ww, uu) in enumerate(((wt_hi, u_hi), (wt_lo, u_hi), (wt_hi, u_lo))):
                        last = pe.matmul(bank[4 + q % 4][:, :b - a], ww[:, ring, P * d:P * d + P], uu[:, slot, a:b],
                                         start=(m == 0), stop=(m == 2))
                    last.then_inc(s_dn, 1)

            pe.wait_ge(s_yr, 24)
            pe.wait_ge(s_ln, 6)
            up(0, 0, 2, 3, 8, first=True)
            up(1, 1, 4, 5, 10, ring_down=0)
            up(2, 0, 1, 2, 13, ring_down=3)
            with pe.Fori(1, NF // 2 - 1) as i:
                up(2 * i + 1, 1, 4, 5, 6 * i + 10, ring_down=0)
                up(2 * i + 2, 0, 1, 2, 6 * i + 13, ring_down=3)
            up(21, 1, 4, 5, 70, ring_down=0)
            for n in range(6):
                down(21, 1, 1, 73, n)

            pe.wait_ge(s_dr, 24 * NF)
            pe.wait_ge(s_co, NF)
            pe.transpose(bank[7][0:88, 0:P], conv_out[:].rearrange("p j f -> p (j f)"), ident[:]).then_inc(s_cvt, 1)
            for t in range(NTILE):
                r = ROWS[t]
                if t >= 2:
                    pe.wait_ge(s_fy, t - 1)
                for k in range(KT):
                    last = pe.transpose(bank[2 * (t % 2) + k // 4][:r, P * (k % 4):P * (k % 4) + P],
                                        res[:, k, P * t:P * t + r], ident[:])
                last.then_inc(s_ft, 1)


def make(nc, outs):
    I = {n: nc.dram_tensor(f"in_{n}", s, F32, kind="ExternalInput").ap() for n, s in {**INS, **TABLES}.items()}
    O = {n: nc.dram_tensor(f"out_{n}", s, F32, kind="ExternalOutput").ap() for n, s in outs}
    build(nc, I, O)


def kernel(**inputs):
    import concourse.bacc as bacc
    from concourse.bass_utils import run_bass_kernel_spmd

    nc = bacc.Bacc("TRN2", target_bir_lowering=False, num_devices=1)
    make(nc, OUTS)
    arrays = {f"in_{n}": np.ascontiguousarray(inputs[n]).reshape(s) for n, s in INS.items()}
    arrays.update({f"in_{n}": a for n, a in tables().items()})
    r = run_bass_kernel_spmd(nc, [arrays], core_ids=[0])
    return tuple(r.results[0][f"out_{n}"] for n, _ in OUTS)
```

```python
from contextlib import ExitStack

import numpy as np

import concourse.bass as bass
from concourse import mybir

F32 = mybir.dt.float32
F32R = mybir.dt.float32r
ALU = mybir.AluOpType
ACT = mybir.ActivationFunctionType
AX = mybir.AxisListType.X

P = 128
D = 1024
KT = D // P
LP, LS = 1024, 64
T = LP + LS
PAST = 512
NTILE = 9
ROWS = [P] * 8 + [LS]
CHUNKS = [(0, 364), (364, 726), (726, 1088)]
CW = 364
H_MLA, NOPE, ROPE, HV = 8, 64, 32, 64
QD = NOPE + ROPE
QR, KVR = 384, 256
H_RET, H_SB, DH = 4, 4, 64
IN_COLS = 2464
ZG = 308
NZG = IN_COLS // ZG
O_ZQ, O_KV, O_KR, O_RQ, O_RK, O_RV, O_RG, O_SQ, O_SK, O_SV = 0, 384, 640, 672, 928, 1184, 1440, 1696, 1952, 2208
FF = 2816
NF = FF // P
EPS = 1e-6
NEG = -1e30
RAW_SLOTS, WT_SLOTS = 3, 6
N_TAB = 11
AG = 512
SQ_SLOTS = (5, 2)
ADA_A, ADA_G = 4, 12
MLA_SCALE = float(QD) ** -0.5
SB_SCALE = float(DH) ** -0.5


def segments(c):
    a, b = CHUNKS[c]
    return [(a, b, 0)] if b <= LP else [(a, LP, 0), (LP, b, 1)]


def chunk_of(t):
    end = min(P * (t + 1), T)
    return next(c for c, (a, b) in enumerate(CHUNKS) if end <= b)


def tables():
    out = {}
    pos = np.arange(T, dtype=np.float64)
    pos[LP:] = PAST + np.arange(LS)
    for name, d in (("rope64", DH), ("rope32", ROPE)):
        inv = (10000.0 ** (-np.arange(0, d, 2, dtype=np.float32) / np.float32(d))).astype(np.float32)
        ang = (pos.astype(np.float32)[:, None] * inv[None, :]).astype(np.float64)
        cos, sin = np.cos(ang), np.sin(ang)
        tab = np.concatenate([cos, cos, -sin, sin], axis=1)
        pad = np.zeros((NTILE * P, 2 * d), np.float32)
        pad[:T] = tab
        out[name] = pad.reshape(NTILE, P, 2 * d).transpose(1, 0, 2).reshape(P, NTILE * 2 * d).copy()
    lg = np.log(1.0 - 2.0 ** (-5.0 - np.arange(H_RET, dtype=np.float32))).astype(np.float64)
    i = np.arange(P)
    rel = i[None, :] - i[:, None]
    dec = np.where(rel[:, None, :] >= 0, np.exp(lg[None, :, None] * np.maximum(rel, 0)[:, None, :]), 0.0)
    out["decayT"] = dec.reshape(P, H_RET * P).astype(np.float32)
    qd = np.zeros((P, 2, P))
    gam = np.zeros((P, 2, 2, P))
    for h in range(H_RET):
        rows = slice(64 * (h % 2), 64 * (h % 2) + 64)
        qd[rows, h // 2, :] = np.exp(lg[h] * (i + 1.0)) * DH ** -0.5
        for n, length in enumerate((P, LS)):
            gam[rows, n, h // 2, :] = np.exp(lg[h] * length)
    out["q_decayT"] = qd.reshape(P, 2 * P).astype(np.float32)
    out["state_decay"] = gam.reshape(P, 4 * P).astype(np.float32)
    kd = np.zeros((P, 2, H_RET))
    for n, length in enumerate((P, LS)):
        kd[:length, n, :] = np.exp(lg[None, :] * (length - 1.0 - i[:length, None]))
    out["k_decay"] = kd.reshape(P, 2 * H_RET).astype(np.float32)
    out["ident"] = np.eye(P, dtype=np.float32)
    out["causal"] = np.where(i[None, :] < i[:, None], 0.0, NEG).astype(np.float32)
    return out


TABLES = {"rope64": (P, NTILE * 128), "rope32": (P, NTILE * 64), "decayT": (P, 512), "q_decayT": (P, 256),
          "state_decay": (P, 512), "k_decay": (P, 8), "ident": (P, P), "causal": (P, P)}
INS = {"x_prompt": (LP, D), "x_sample": (LS, D), "c_prompt": (8, P), "c_sample": (8, P),
       "cache_mla_latent": (PAST, KVR), "cache_mla_krope": (PAST, ROPE), "cache_sb_k": (PAST, 256),
       "cache_sb_v": (PAST, 256), "state_ret": (256, 64), "state_ffn_conv": (44, P), "w_in": (D, IN_COLS),
       "g_q_norm": (3, P), "w_uq": (QR, 768), "g_kv_norm": (1, KVR), "w_ukv": (KVR, 1024), "g_ret_norm": (1, 256),
       "w_o": (D, D), "w_up": (D, 2 * FF), "conv_w": (66, P), "conv_b": (22, P), "w_down": (FF, D),
       "g_norm1": (8, P), "g_norm2": (8, P), "w_ada": (D, 6 * D), "b_ada": (48, P), "g_final": (1, D)}
OUTS = [("y_prompt", (1, LP, D)), ("y_sample", (1, LS, D)),
        ("p_mla_latent", (1, 1, LP, KVR)), ("p_mla_krope", (1, 1, LP, ROPE)),
        ("p_sb_k", (1, 1, LP, 4, 64)), ("p_sb_v", (1, 1, LP, 4, 64)),
        ("p_ret_state", (1, 1, 4, 64, 64)), ("p_ffn_conv", (1, 1, 2, FF)),
        ("s_mla_latent", (1, 1, LS, KVR)), ("s_mla_krope", (1, 1, LS, ROPE)),
        ("s_sb_k", (1, 1, LS, 4, 64)), ("s_sb_v", (1, 1, LS, 4, 64)),
        ("s_ret_state", (1, 1, 4, 64, 64)), ("s_ffn_conv", (1, 1, 2, FF))]
VEC_A = [("b_ada", 48, 0), ("g_norm1", 8, 48), ("g_norm2", 8, 56), ("c_prompt", 8, 64), ("c_sample", 8, 72),
         ("g_q_norm", 3, 80)]
N_A = 83
VEC_B = [("conv_w", 66, 0), ("conv_b", 22, 66)]
N_B = 88
N_C = 44


SEQ = [8] + list(range(8))
KINDS = [("S", 0), ("M", 0), ("M", 1), ("S", 1), ("M", 2), ("M", 3), ("S", 2), ("M", 4), ("M", 5), ("S", 3),
         ("M", 6), ("M", 7)]
UNITS = [(n, kind, h) for n in range(NTILE) for kind, h in KINDS]
FF_SPARE = KT * T - (4 * T + 2 * (T + 4) + T + 2 + 2 * CW + 8 + 4 * NF + 6)
T_LAG = {"M": 2, "S": 5}
EARLY_SPLIT = 105
MIX_STEP = 16




def rows_of(n):
    return ROWS[SEQ[n]]


def key_col(n):
    return P * SEQ[n]


def key_blocks(n):
    if n == 0:
        return [(512 + P * j, P, 4 + j) for j in range(4)] + [(LP, LS, 8)]
    return [(P * j, P, j) for j in range(SEQ[n] + 1)]


def n_keys(n):
    return sum(size for _, size, _ in key_blocks(n))


def count_units(kind, i):
    return sum(k == kind for _, k, _ in UNITS[:i])


def plan_pieces():
    steps = {}
    for step in range(12 * (NTILE - 1) + MIX_STEP + 1):
        out = []
        for kind in "MS":
            i = step - T_LAG[kind]
            if 0 <= i < len(UNITS) and UNITS[i][1] == kind:
                nb = len(key_blocks(UNITS[i][0]))
                out += [(kind, i, j) for j in range((nb + 3) // 4)]
        n, rest = divmod(step - MIX_STEP, 12)
        if rest == 0 and 0 <= n < NTILE:
            out += [("X", n, 0), ("X", n, 1)]
        steps[step] = out
    return steps


PIECES = plan_pieces()
STEPS = len(PIECES)
ORDER = [x for step in range(STEPS) for x in PIECES[step]]
PIECE_NO = {x: q for q, x in enumerate(ORDER)}
W_NO = {x: w for w, x in enumerate(x for x in ORDER if x[0] != "X")}
N_PIECES = len(W_NO)
COPIER = {"M": "A", "S": "D", "X": "A"}
COPY_NO = {x: sum(COPIER[y[0]] == COPIER[x[0]] for y in ORDER[:q]) for q, x in enumerate(ORDER)}
PV_ORDER = [x[1] for x in ORDER if x[0] != "X" and x[2] == 0]
PV_NO = {i: v for v, i in enumerate(PV_ORDER)}
READ_A = [0, 1, 2, 3, 4, 5, 7, 8, 9]
READ_D = [0, 2, 3, 4, 6, 7, 9, 10, 11]


def read_a(m, s):
    return len(READ_A) * m + sum(x < s for x in READ_A)


def read_d(m, s):
    return len(READ_D) * m + sum(x < s for x in READ_D)


def build(nc, I, O, stop_after=None):
    ctx = ExitStack()
    z_dram = nc.dram_tensor("z_scratch", (T, IN_COLS), F32, kind="Internal").ap()
    xT_dram = nc.dram_tensor("xT_scratch", (P, KT, T), F32, kind="Internal").ap()
    mod_a_dram = nc.dram_tensor("mod_a_scratch", (4, AG * ADA_A), F32, kind="Internal").ap()
    mod_b_dram = nc.dram_tensor("mod_b_scratch", (4, AG * (ADA_G - ADA_A)), F32, kind="Internal").ap()
    mixT_dram = nc.dram_tensor("mixT_scratch", (P, KT, T), F32, kind="Internal").ap()
    with ctx:
        def sem(name):
            return ctx.enter_context(nc.semaphore(name))

        def sbuf(scope):
            return lambda name, shape, dt=F32: scope.enter_context(nc.sbuf_tensor(name, [P, *shape], dt))

        keep = sbuf(ctx)
        psum = ctx.enter_context(nc.psum_tensor("psum", [P, 8, 512], F32))
        bank = [psum[:, i, :] for i in range(8)]

        ident = keep("ident_sb", [P])
        ones = keep("ones", [P])
        vec_a = keep("vec_a", [N_A])
        vec_b = keep("vec_b", [N_B])
        vec_c = keep("vec_c", [N_C])
        mod = keep("mod", [48, 2])
        scale_n = keep("scale_n", [2, KT, 2])
        eps = keep("eps", [1])
        mod_rows = keep("mod_rows", [P])

        early = ExitStack()
        s1 = sbuf(early)
        xT = s1("xT", [KT, T])
        rb = s1("rb", [T])
        sq_hn = s1("sq_hn", [5, CW])
        h_hi = s1("h_hi", [KT, T], F32R)
        h_lo = s1("h_lo", [KT, T], F32R)
        vec_in = s1("vec_in", [3, P])
        silu_c = s1("silu_c", [2, KT])
        silu_e = s1("silu_e", [2, KT])
        c_parts = s1("c_parts", [KT, 4], F32R)
        ada_raw = s1("ada_raw", [4, 2, AG])
        ada_hi = s1("ada_hi", [4, AG], F32R)
        ada_lo = s1("ada_lo", [4, AG], F32R)
        ada_row = s1("ada_row", [AG])
        z_out = s1("z_out", [3, ZG])
        x_scope = ExitStack()
        x_in = sbuf(x_scope)("x_in", [NTILE, D])
        x_scope.close()
        w_raw = s1("w_raw", [2, 4, ZG])
        w_hi = s1("w_hi", [2, KT, ZG], F32R)
        w_lo = s1("w_lo", [2, KT, ZG], F32R)
        early.close()

        mid = ExitStack()
        s3 = sbuf(mid)
        w_uq = s3("w_uq_sb", [3, 768])
        w_uk = s3("w_uk", [2, 512])
        w_uv = s3("w_uv", [2, 512])
        decayT = s3("decayT_sb", [H_RET, P])
        q_decayT = s3("q_decayT_sb", [2, P])
        state_decay = s3("state_decay_sb", [2, 2, P])
        k_decay = s3("k_decay_sb", [2, H_RET])
        g_kv = s3("g_kv_sb", [KVR])
        g_ret = s3("g_ret_sb", [256])
        cache_scope = ExitStack()
        s_c3 = sbuf(cache_scope)
        c_lat = s_c3("c_lat", [4, KVR])
        c_sk = s_c3("c_sk", [4, 256])
        c_kr = s_c3("c_kr", [4, ROPE])
        cache_scope.close()
        qtok = s3("qtok", [768])
        att = s3("att", [H_RET, P])
        rkT = s3("rkT", [2, P])
        rqdT = s3("rqdT", [2, P])
        rqT = s3("rqT", [2, 2, P])
        z_in = s3("z_in", [2, IN_COLS])
        rope_t = s3("rope_t", [2, 192])
        zqn = s3("zqn", [QR])
        lat = s3("lat", [KVR])
        latT = s3("latT", [2, P])
        qnT = s3("qnT", [3, P])
        junk = s3("junk", [QR + KVR])
        sums = s3("sums", [2])
        rs = s3("rs", [2])
        rope_a = s3("rope_a", [512])
        rope_b = s3("rope_b", [512])
        q_a = s3("q_a", [4, ROPE])
        q_b = s3("q_b", [4, ROPE])
        kr = s3("kr", [ROPE])
        rqk = s3("rqk", [8, DH])
        kd = s3("kd", [H_RET, DH])
        state = s3("state", [2, 2, P])
        eg = s3("eg", [256])
        kT = s3("kT", [H_MLA, T])
        v_mla = s3("v_mla", [NTILE, 512])
        skT = s3("skT", [2, T])
        sv = s3("sv", [NTILE, 256])
        qT = s3("qT", [2, H_MLA, P])
        sqT = s3("sqT", [2, 2, P])
        prob = s3("prob", [3, 1024])
        zsb = s3("zsb", [2, 1024])
        esb = s3("esb", [2, 1024])
        pT = s3("pT", [4, 4, P])
        mixtok = s3("mixtok", [2, D])
        mixT = s3("mixT", [KT, P])
        causal = s3("causal_sb", [P])
        zero = s3("zero", [1])
        gate = s3("gate", [256])
        oc = s3("oc", [H_RET, DH])
        oc2 = s3("oc2", [H_RET, DH])
        stat = s3("stat", [4, H_RET])
        maxes = s3("maxes", [2, 2])
        rowsum = s3("rowsum", [4, 2])
        mid.close()
        late = ExitStack()
        s4 = sbuf(late)
        mix_scope = ExitStack()
        mix_raw = sbuf(mix_scope)("mix_raw", [KT, T])
        mix_scope.close()
        u_hi = s4("u_hi", [2, T], F32R)
        u_lo = s4("u_lo", [2, T], F32R)
        a_ext = s4("a_ext", [2, T + 4])
        conv = s4("conv", [T + 2])
        u_val = s4("u_val", [2, CW])
        f_vec = s4("f_vec", [2, 4])
        conv_out = s4("conv_out", [4, NF])
        fin = s4("final_stats", [2, 3])
        spare = s4("spare", [FF_SPARE])
        wt_raw = s4("wt_raw", [RAW_SLOTS, KT * P])
        wt_parts = s4("wt_parts", [WT_SLOTS, 2, KT * P], F32R)
        wt_hi, wt_lo = wt_parts[:, :, 0, :], wt_parts[:, :, 1, :]
        a_hi = s4("act_hi", [KT, T], F32R)
        a_lo = s4("act_lo", [KT, T], F32R)
        res = s4("residual", [KT, T])
        late.close()
        norm_bufs = [dict(x=xT, hi=h_hi, lo=h_lo, rb=rb, sq=sq_hn, hn=sq_hn[:, 2:5]),
                     dict(x=res, hi=a_hi, lo=a_lo, rb=conv,
                          sq=a_ext[:, 0, 0:2 * CW].rearrange("p (a n) -> p a n", a=2),
                          hn=a_ext[:, 1, 0:3 * CW].rearrange("p (a n) -> p a n", a=3))]
        late_out = a_ext[:].rearrange("p a n -> p (a n)")
        g_fin = conv[:, 0:D]
        y_out = late_out[:, 0:2 * D].rearrange("p (a n) -> p a n", a=2)
        conv_rows = u_val[:, 0, 0:P]
        c_latT = zsb[:, :, :].rearrange("p a (b c) -> p a b c", b=2)[:, :, 0, :]

        s_id = sem("identity_loaded")
        s_const = sem("vectors_loaded")
        s_x = [sem(f"x_loaded_{i}") for i in range(NTILE)]
        s_set = sem("memsets_done")
        s_xt = sem("x_transposed")
        s_xeD = sem("xT_first_half_written")
        s_xeA = sem("xT_second_half_written")
        s_vt = sem("vectors_transposed")
        s_vec = sem("vectors_written")
        s_silu = sem("silu_steps")
        s_siluv = sem("silu_ready")
        s_chi = sem("silu_high_written")
        s_cpl = sem("silu_low_written")
        s_ada = [sem(f"ada_loaded_{i}") for i in range(4)]
        s_ahi = sem("ada_hi_written")
        s_alo = sem("ada_lo_written")
        s_adamm = sem("ada_rows_multiplied")
        s_row = sem("ada_row_copied")
        s_rowst = sem("ada_row_stored")
        s_modl = sem("mod_rows_loaded")
        s_modt = sem("mod_rows_transposed")
        s_mod = sem("mod_written")
        s_scale = sem("norm_scales_written")
        s_sq = sem("squares_written")
        s_ms = sem("squares_summed")
        s_ln = sem("log_written")
        s_rb = sem("rstd_written")
        s_hn = sem("normed_written")
        s_hhi = sem("h_hi_written")
        s_h = sem("h_lo_written")
        s_raw = [sem(f"w_raw_loaded_{i}") for i in range(2)]
        s_whi = sem("w_hi_written")
        s_wlo = sem("w_lo_written")
        s_z = sem("z_multiplied")
        s_zc = sem("z_copied")
        s_zst = [sem(f"z_stored_{i}") for i in range(3)]

        s_xst = sem("xT_stored")
        s_tab = sem("mixer_constants_loaded")
        s_cau = sem("causal_mask_loaded")
        s_cache = sem("caches_loaded")
        s_init = sem("mixer_memsets_done")
        s_sv = sem("values_loaded")
        s_wuq = sem("w_uq_scaled")
        s_zi = [sem(f"z_tile_loaded_{i}") for i in range(2)]
        s_cT = sem("cache_stage_multiplied")
        s_cA = sem("cache_copied_by_scalar")
        s_cD = sem("cache_copied_by_vector")
        s_rs = sem("latent_rstd_ready")
        s_eg = sem("gate_exp_ready")
        s_lat = sem("latents_normed")
        s_latst = sem("latents_stored")
        s_kr = sem("k_rope_ready")
        s_rot = sem("retention_qk_ready")
        s_g1 = sem("gate_denominator_ready")
        s_g2 = sem("gate_reciprocal_ready")
        s_gate = sem("gate_ready")
        s_fp = sem("front_step_multiplied")
        s_fA = sem("front_bank_read_by_scalar")
        s_fD = sem("front_bank_read_by_vector")
        s_var = sem("group_variance_ready")
        s_rr = sem("group_rstd_ready")
        s_ret = sem("retention_written")
        s_sc = sem("scores_multiplied")
        s_mx = sem("maximum_ready")
        s_p = sem("softmax_exp_written")
        s_zsb = sem("stick_logits_copied")
        s_l = sem("stick_log_written")
        s_c = sem("stick_sums_written")
        s_wa = sem("stick_exponents_written")
        s_w = sem("stick_weights_written")
        s_tr = sem("piece_transposed")
        s_ptA = sem("piece_copied_by_scalar")
        s_ptD = sem("piece_copied_by_vector")
        s_pv = sem("piece_weighed")
        s_o = sem("head_output_written")
        s_mst = sem("mixT_stored")
        s_out = sem("outputs_stored")
        s_res = sem("residual_loaded")
        s_mx4 = sem("mix_rows_loaded")
        s_mhi = sem("mix_hi_written")
        s_mlo = sem("mix_lo_written")
        s_wl = [sem(f"weight_tile_loaded_{i}") for i in range(RAW_SLOTS)]
        s_wh = sem("weight_hi_written")
        s_wlow = sem("weight_lo_written")
        s_y = sem("projection_multiplied")
        s_yr = sem("residual_updated")
        s_up = sem("ffn_chunk_multiplied")
        s_ac = sem("ffn_a_copied")
        s_fv = sem("ffn_vectors_copied")
        s_cv = sem("conv_first_tap")
        s_c1 = sem("conv_second_tap")
        s_cs = sem("conv_summed")
        s_sl = sem("silu_written")
        s_u = sem("u_written")
        s_uh = sem("u_hi_written")
        s_ul = sem("u_lo_written")
        s_co = sem("conv_state_kept")
        s_dn = sem("down_multiplied")
        s_dr = sem("down_added")
        s_cvt = sem("conv_state_transposed")
        s_cvc = sem("conv_state_copied")
        s_ft = sem("final_transposed")
        s_fs = sem("final_rstd_ready")
        s_fy = sem("final_written")
        s_yst = [sem(f"final_stored_{i}") for i in range(2)]
        s_gf = sem("final_gain_loaded")
        s_cvi = sem("conv_edges_cleared")
        s_chA = sem("scalar_chain")
        s_chD = sem("vector_chain")
        s_chP = sem("pool_chain")

        def score_bank(i, width):
            return psum[:, 2 * (i % 2):2 * (i % 2) + 2, :].rearrange("p a b -> p (a b)")[:, :width]

        def pieces_done(eng, x):
            eng.wait_ge(s_ptA if COPIER[x[0]] == "A" else s_ptD, COPY_NO[x] + 1)

        class Chain:

            def __init__(self, eng, s):
                self.eng, self.s, self.n = eng, s, 0

            def link(self, ins):
                self.n += 1
                ins.then_inc(self.s, 1)
                self.eng.wait_ge(self.s, self.n)

        w_in_v = I["w_in"].rearrange("(k p) n -> p k n", p=P)
        w_ada_v = I["w_ada"].rearrange("(k p) n -> p k n", p=P)
        n_const = len(VEC_A) + len(VEC_B) + 1

        def x_rows(t):
            return I["x_prompt"][P * t:P * t + P, :] if t < 8 else I["x_sample"]

        block = ctx.enter_context(nc.Block())

        @block.sync
        def _(sp):
            sp.dma_start(ident[:], I["ident"]).then_inc(s_id, 16)
            for t in range(4):
                sp.dma_start(x_in[:ROWS[t], t, :], x_rows(t)).then_inc(s_x[t], 16)
            for i, vecs in enumerate((VEC_A, VEC_B, [("state_ffn_conv", 44, 0)])):
                for name, rows, at in vecs:
                    sp.dma_start(vec_in[at:at + rows, i, :], I[name]).then_inc(s_const, 16)

            for t in range(4, NTILE):
                sp.dma_start(x_in[:ROWS[t], t, :], x_rows(t)).then_inc(s_x[t], 16)

            def load_ada(g, first=False):
                for q in range(4):
                    if not first:
                        sp.wait_ge(s_alo, 8 * g + 2 * q - 6)
                    sp.dma_start(ada_raw[:, q], w_ada_v[:, 2 * q:2 * q + 2, bass.ds(g * AG, AG)])\
                        .then_inc(s_ada[q], 16)

            def load_w_in(g, half):
                sp.dma_start(w_raw[:, half], w_in_v[:, 4 * half:4 * half + 4, bass.ds(g * ZG, ZG)])\
                    .then_inc(s_raw[half], 16)

            for g in range(ADA_A):
                load_ada(g, first=(g == 0))
            sp.wait_ge(s_xt, 2 * NTILE)
            load_w_in(0, 0)
            load_w_in(0, 1)
            load_ada(ADA_A)
            sp.wait_ge(s_rowst, 16 * ADA_A)
            sp.dma_start(mod_rows[0:64, :], mod_a_dram.rearrange("r (j p) -> (r j) p", p=P)).then_inc(s_modl, 16)
            sp.wait_ge(s_xeD, NTILE)
            sp.wait_ge(s_xeA, NTILE)

            def group_loads(g):
                for half in range(2):
                    sp.wait_ge(s_wlo, 2 * g + half + 1)
                    load_w_in(g + 1, half)
                load_ada(g + 1 + ADA_A)

            group_loads(0)
            sp.dma_start(xT_dram, xT[:]).then_inc(s_xst, 16)
            with sp.Fori(1, NZG - 1) as g:
                group_loads(g)

            sp.wait_ge(s_xst, 16)
            sp.wait_ge(s_h, 24)
            for name, tile_ in (("decayT", decayT), ("q_decayT", q_decayT), ("state_decay", state_decay),
                                ("k_decay", k_decay)):
                flat = tile_[:]
                if len(flat.shape) == 3:
                    flat = flat.rearrange("p a b -> p (a b)")
                elif len(flat.shape) == 4:
                    flat = flat.rearrange("p a b c -> p (a b c)")
                sp.dma_start(flat, I[name]).then_inc(s_tab, 16)
            sp.dma_start(g_kv[:], I["g_kv_norm"].broadcast_to([P, KVR])).then_inc(s_tab, 16)
            sp.dma_start(g_ret[:], I["g_ret_norm"].broadcast_to([P, 256])).then_inc(s_tab, 16)
            sp.dma_start(w_uq[:], I["w_uq"].rearrange("(k p) n -> p k n", p=P)).then_inc(s_tab, 16)
            for part, lo in ((w_uk, 0), (w_uv, NOPE)):
                for k in range(2):
                    sp.dma_start(part[:, k, :].rearrange("p (h c) -> p h c", h=8),
                                 I["w_ukv"][P * k:P * k + P, :].rearrange("p (h c) -> p h c", h=8)[:, :, lo:lo + 64])\
                        .then_inc(s_tab, 16)
            sp.dma_start(c_lat[:], I["cache_mla_latent"].rearrange("(j p) c -> p j c", p=P)).then_inc(s_cache, 16)
            sp.dma_start(c_sk[:], I["cache_sb_k"].rearrange("(j p) c -> p j c", p=P)).then_inc(s_cache, 16)
            sp.dma_start(c_kr[:], I["cache_mla_krope"].rearrange("(j p) c -> p j c", p=P)).then_inc(s_cache, 16)

            sp.wait_ge(s_rowst, 16 * ADA_G)
            sp.dma_start(mod_rows[:], mod_b_dram.rearrange("r (j p) -> (r j) p", p=P)).then_inc(s_modl, 16)
            sp.wait_ge(s_z, 9 * NZG)
            sp.wait_ge(s_adamm, 8 * ADA_G)
            for i in range(3):
                sp.wait_ge(s_zst[i], 16 * 3 * NZG)

            def load_z(m):
                r, t = rows_of(m), SEQ[m]
                sp.dma_start(z_in[:r, m % 2, :], z_dram[P * t:P * t + r, :]).then_inc(s_zi[m % 2], 16)
                sp.dma_start(rope_t[:, m % 2, 0:128], I["rope64"][:, 128 * t:128 * t + 128]).then_inc(s_zi[m % 2], 16)
                sp.dma_start(rope_t[:, m % 2, 128:192], I["rope32"][:, 64 * t:64 * t + 64]).then_inc(s_zi[m % 2], 16)

            def diagonal(of, n):
                heads = of.rearrange("(q two) d e -> two d q e", two=2)
                for two in range(2):
                    lo = 64 * two
                    yield state[lo:lo + 64, n, :, lo:lo + 64], heads[two]

            load_z(0)
            sp.dma_start(causal[:], I["causal"]).then_inc(s_cau, 16)
            load_z(1)
            sp.dma_start(sv[:, 4:8, :], I["cache_sb_v"].rearrange("(j p) c -> p j c", p=P)).then_inc(s_sv, 16)
            sp.dma_start(sv[:LS, 8, :], z_dram[LP:T, O_SV:O_SV + 256]).then_inc(s_sv, 16)
            sp.dma_start(sv[:, 0:4, :], z_dram[0:512, O_SV:O_SV + 256].rearrange("(j p) c -> p j c", p=P))\
                .then_inc(s_sv, 16)
            sp.wait_ge(s_init, 1)
            for part, heads in diagonal(I["state_ret"].rearrange("(h d) e -> h d e", h=4), 0):
                sp.dma_start(part, heads).then_inc(s_sv, 16)
            for name, at in (("sb_k", O_SK), ("sb_v", O_SV)):
                for who, lo, hi in (("p", 0, LP), ("s", LP, T)):
                    sp.dma_start(O[f"{who}_{name}"].rearrange("a b t h d -> (a b t) (h d)"),
                                 z_dram[lo:hi, at:at + 256]).then_inc(s_out, 16)

            def store_latent(m):
                who, a, r = ("s", 0, LS) if m == 0 else ("p", P * (m - 1), P)
                sp.wait_ge(s_lat, m + 1)
                sp.dma_start(O[f"{who}_mla_latent"].rearrange("a b t c -> (a b t) c")[a:a + r, :], lat[:r, :])\
                    .then_inc(s_latst, 16)
                sp.wait_ge(s_kr, m + 1)
                sp.dma_start(O[f"{who}_mla_krope"].rearrange("a b t c -> (a b t) c")[a:a + r, :], kr[:r, :])\
                    .then_inc(s_latst, 16)

            def store_state(m, name):
                sp.wait_ge(s_fD, read_d(m + 1, 0))
                for part, heads in diagonal(O[name].rearrange("a b h d e -> (a b h) d e"), int(m > 0)):
                    sp.dma_start(heads, part).then_inc(s_out, 16)

            def store_mix(n):
                r, t = rows_of(n), SEQ[n]
                pieces_done(sp, ("X", n, 1))
                sp.dma_start(mixT_dram[:, :, P * t:P * t + r], mixT[:, :, :r]).then_inc(s_mst, 16)

            store_latent(0)
            for n in range(NTILE):
                if n == 0:
                    store_state(0, "s_ret_state")
                if n + 2 < NTILE:
                    sp.wait_ge(s_ret, n + 1)
                    sp.wait_ge(s_gate, n + 1)
                    sp.wait_ge(s_fp, 12 * (n + 1))
                    load_z(n + 2)
                if n + 1 < NTILE:
                    store_latent(n + 1)
                if n == 2:
                    sp.wait_ge(s_o, 12)
                    sp.dma_start(sv[:, 4:8, :], z_dram[512:LP, O_SV:O_SV + 256].rearrange("(j p) c -> p j c", p=P))\
                        .then_inc(s_sv, 16)
                if n:
                    store_mix(n - 1)
            store_state(8, "p_ret_state")
            sp.wait_ge(s_mst, 16 * (NTILE - 1))
            sp.wait_ge(s_latst, 32 * NTILE)
            sp.wait_ge(s_out, 16 * 8)
            sp.wait_ge(s_gate, NTILE)
            sp.wait_ge(s_fp, 12 * NTILE)
            sp.wait_ge(s_fA, read_a(NTILE, 0))
            sp.wait_ge(s_fD, read_d(NTILE, 0))
            for d in range(3):
                sp.dma_start(wt_raw[:, d, :].rearrange("p (k n) -> p k n", k=KT),
                             I["w_o"].rearrange("(k p) n -> p k n", p=P)[:, :, P * d:P * d + P]).then_inc(s_wl[d], 16)
            sp.dma_start(mix_raw[:, :, 0:LP - P], mixT_dram[:, :, 0:LP - P]).then_inc(s_mx4, 16)
            sp.dma_start(mix_raw[:, :, LP:T], mixT_dram[:, :, LP:T]).then_inc(s_mx4, 16)

            w_o_v = I["w_o"].rearrange("(k p) n -> p k n", p=P)
            w_up_v = I["w_up"].rearrange("(k p) n -> p k n", p=P)

            def load_tile(idx, slot, src):
                sp.wait_ge(s_wlow, idx - 2)
                dst = wt_raw[:, slot, :]
                if len(src.shape) == 3:
                    dst = dst.rearrange("p (k n) -> p k n", k=KT)
                sp.dma_start(dst, src).then_inc(s_wl[slot], 16)

            def load_up(idx, slot, f, branch):
                load_tile(idx, slot, w_up_v[:, :, bass.ds(FF * branch + f * P, P)])

            def load_down(idx, slot, f):
                load_tile(idx, slot, I["w_down"][bass.ds(f * P, P), :])

            for d in range(3, 6):
                load_tile(d, d % 3, w_o_v[:, :, P * d:P * d + P])
            sp.wait_ge(s_tr, len(ORDER))
            sp.wait_ge(s_ret, NTILE)
            sp.wait_ge(s_o, len(UNITS))
            sp.dma_start(res[:], xT_dram).then_inc(s_res, 16)
            for d in range(6, KT):
                load_tile(d, d % 3, w_o_v[:, :, P * d:P * d + P])

            load_up(8, 2, 0, 0)
            load_up(9, 0, 0, 1)
            with sp.Fori(0, NF // 2 - 1) as i:
                for half in range(2):
                    at = 10 + 6 * i + 3 * half
                    load_up(at, 1, 2 * i + 1 + half, 0)
                    load_up(at + 1, 2, 2 * i + 1 + half, 1)
                    load_down(at + 2, 0, 2 * i + half)
            load_up(70, 1, 21, 0)
            load_up(71, 2, 21, 1)
            load_down(72, 0, 20)
            load_down(73, 1, 21)

            sp.wait_ge(s_wlow, 74)
            sp.wait_ge(s_dn, 24 * NF)
            sp.dma_start(g_fin, I["g_final"].broadcast_to([P, D])).then_inc(s_gf, 16)
            sp.wait_ge(s_cvc, 1)
            for who, lo in (("p", 0), ("s", 44)):
                sp.dma_start(O[f"{who}_ffn_conv"].rearrange("a b j (f p) -> (a b j f) p", p=P),
                             conv_rows[lo:lo + 44, :]).then_inc(s_out, 16)
            for t in range(NTILE):
                sp.wait_ge(s_fy, t + 1)
                dst = O["y_prompt"][0, P * t:P * t + P, :] if t < 8 else O["y_sample"][0]
                sp.dma_start(dst, y_out[:ROWS[t], t % 2, :]).then_inc(s_yst[t % 2], 16)
            sp.wait_ge(s_out, 16 * 10)
            sp.wait_ge(s_yst[0], 16 * 5)
            sp.wait_ge(s_yst[1], 16 * 4)

        @block.gpsimd
        def _(pool):
            def store_z(g):
                for t in range(NTILE):
                    pool.wait_ge(s_zc, 9 * g + t + 1)
                    pool.dma_start(z_dram[P * t:P * t + ROWS[t], bass.ds(g * ZG, ZG)],
                                   z_out[:ROWS[t], t % 3, :]).then_inc(s_zst[t % 3], 16)

            with pool.Fori(0, NZG) as g:
                store_z(g)

            ch = Chain(pool, s_chP)
            pool.wait_ge(s_tab, 16 * N_TAB)

            def rope(x, heads, half, table, out, r):
                d = 2 * half

                def tab(a, n):
                    return table[:r, a:a + n].unsqueeze(1).broadcast_to([r, heads, n])

                a = rope_a[:r, :heads * d].rearrange("p (h d) -> p h d", h=heads)
                b = rope_b[:r, :heads * d].rearrange("p (h d) -> p h d", h=heads)
                pool.tensor_tensor(a, x, tab(0, d), ALU.mult)
                pool.tensor_tensor(b[:, :, :half], x[:, :, half:], tab(d, half), ALU.mult)
                ch.link(pool.tensor_tensor(b[:, :, half:], x[:, :, :half], tab(d + half, half), ALU.mult))
                return pool.tensor_tensor(out, a, b, ALU.add)

            def front(m, s):
                r, slot = rows_of(m), m % 2
                if s == 0:
                    pool.wait_ge(s_zi[slot], 48 * (m // 2 + 1))
                    if m:
                        pool.wait_ge(s_latst, 32 * m)
                        pool.wait_ge(s_fp, 12 * m)
                    x = z_in[:r, slot, :]
                    ch.link(rope(x[:, O_KR:O_KR + ROPE].unsqueeze(1), 1, 16, rope_t[:, slot, 128:192],
                                 kr[:r, :].unsqueeze(1), r))
                    pool.sem_inc(s_kr, 1)
                    ch.link(rope(x[:, O_RQ:O_RQ + 512].rearrange("p (h d) -> p h d", h=8), 8, 32,
                                 rope_t[:, slot, 0:128], rqk[:r], r))
                    pool.tensor_tensor(kd[:r], rqk[:r, 4:8, :],
                                       k_decay[:r, int(m == 0), :].unsqueeze(2).broadcast_to([r, H_RET, DH]),
                                       ALU.mult).then_inc(s_rot, 1)
                if s == 1:
                    x = z_in[:r, slot, O_RG:O_RG + 256]
                    pool.wait_ge(s_eg, m + 1)
                    if m:
                        pool.wait_ge(s_ret, m)
                    pool.tensor_scalar(eg[:r], eg[:r], 1.0, None, ALU.add).then_inc(s_g1, 1)
                    ch.link(pool.tensor_tensor(gate[:r], x, g_ret[:r], ALU.mult))
                if s == 2:
                    pool.wait_ge(s_g2, m + 1)
                    pool.tensor_tensor(gate[:r], gate[:r], eg[:r], ALU.mult).then_inc(s_gate, 1)

            def stick_exponents(i):
                n = UNITS[i][0]
                r, w, j = rows_of(n), n_keys(n), count_units("S", i)
                pool.wait_ge(s_c, j + 1)
                pool.tensor_tensor(esb[:r, j % 2, :w], zsb[:r, j % 2, :w], esb[:r, j % 2, :w], ALU.subtract)\
                    .then_inc(s_wa, 1)

            for step in range(-12, STEPS):
                m, s = divmod(step + 12, 12)
                if m < NTILE:
                    front(m, s)
                if 0 <= step - 2 < len(UNITS) and UNITS[step - 2][1] == "S":
                    stick_exponents(step - 2)

        @block.scalar
        def _(act):
            act.preload_act_table_set("natural_log_exp_and_others")
            def copy_x(t):
                act.wait_ge(s_xt, 2 * t + 2)
                act.activation(xT[:, 4:8, P * t:P * t + ROWS[t]],
                               bank[2 * (t % 2) + 1][:, :].rearrange("p (k n) -> p k n", k=4)[:, :, :ROWS[t]],
                               ACT.Copy).then_inc(s_xeA, 1)

            def ada_high(g, q):
                act.wait_ge(s_ada[q], 16 * g + 16)
                for k in (2 * q, 2 * q + 1):
                    if not (isinstance(g, int) and g == 0 and k < 4):
                        act.wait_ge(s_adamm, 8 * g + k - 3)
                    act.activation(ada_hi[:, k % 4], ada_raw[:, q, k % 2], ACT.Copy).then_inc(s_ahi, 1)

            def copy_row(g, dram, at, first=False):
                act.wait_ge(s_adamm, 8 * g + 8)
                if not first:
                    act.wait_ge(s_rowst, 16 * g)
                act.activation(ada_row[0:4, :], bank[5][0:4, :], ACT.Copy).then_inc(s_row, 1)
                act.wait_ge(s_row, g + 1)
                act.dma_start(dram[:, bass.ds(at * AG, AG)], ada_row[0:4, :]).then_inc(s_rowst, 16)

            def square(n, c, k, j):
                a, b = CHUNKS[c]
                if j >= SQ_SLOTS[n]:
                    act.wait_ge(s_ms, 24 * n + j - SQ_SLOTS[n] + 1)
                act.activation(norm_bufs[n]["sq"][:, j % SQ_SLOTS[n], :b - a], norm_bufs[n]["x"][:, k, a:b], ACT.Square)\
                    .then_inc(s_sq, 1)

            def squares(n, c):
                for k in range(KT):
                    square(n, c, k, 8 * c + k)

            def rstd(n, c):
                a, b = CHUNKS[c]
                j = 3 * n + c
                out = norm_bufs[n]["rb"][:, a:b]
                act.wait_ge(s_ms, 8 * (j + 1) if n == 0 else 24 + 21 + c + 1)
                act.activation(out, bank[4 if n == 0 else 5 + c][:, :b - a], ACT.Ln, bias=eps[:], scale=1.0 / D)\
                    .then_inc(s_ln, 1)
                act.wait_ge(s_ln, j + 1)
                act.activation(out, out, ACT.Exp, scale=-0.5).then_inc(s_rb, 1)

            def h_high(n, c):
                for k in range(KT):
                    j = 24 * n + 8 * c + k
                    act.wait_ge(s_hn, j + 1)
                    for a, b, which in segments(c):
                        last = act.activation(norm_bufs[n]["hi"][:, k, a:b],
                                              norm_bufs[n]["hn"][:, (8 * c + k) % 3, a - CHUNKS[c][0]:b - CHUNKS[c][0]],
                                              ACT.Identity, bias=mod[:, 24 * n + k, which:which + 1])
                    last.then_inc(s_hhi, 1)

            def split_w_in(g, slot):
                for half in range(2):
                    act.wait_ge(s_raw[half], 16 * (g + 1))
                    act.activation(w_hi[:, slot, 4 * half:4 * half + 4], w_raw[:, half], ACT.Copy)\
                        .then_inc(s_whi, 1)

            def x_chunk(c):
                for t in range(3 * c, 3 * c + 3):
                    copy_x(t)
                if c:
                    rstd(0, c - 1)
                act.wait_ge(s_xeD, 3 * c + 3)
                act.wait_ge(s_xeA, 3 * c + 3)
                squares(0, c)

            act.wait_ge(s_set, 2)
            x_chunk(0)
            act.wait_ge(s_vec, 1)
            act.activation(silu_e[:], vec_a[:, 64:80].rearrange("p (c k) -> p c k", c=2), ACT.Exp, scale=-1.0)\
                .then_inc(s_silu, 1)
            act.wait_ge(s_siluv, 1)
            act.activation(c_parts[:, :, 0:2], silu_c[:].rearrange("p c k -> p k c"), ACT.Copy).then_inc(s_chi, 1)
            x_chunk(1)
            ada_high(0, 0)
            ada_high(0, 1)
            x_chunk(2)
            ada_high(0, 2)
            ada_high(0, 3)
            rstd(0, 2)
            for g in range(1, ADA_A):
                ada_high(g, 0)
                ada_high(g, 1)
                copy_row(g - 1, mod_a_dram, g - 1, first=(g == 1))
                ada_high(g, 2)
                ada_high(g, 3)
            copy_row(ADA_A - 1, mod_a_dram, ADA_A - 1)
            split_w_in(0, 0)
            ada_high(ADA_A, 0)
            ada_high(ADA_A, 1)
            for c in range(3):
                h_high(0, c)

            def group(g, slot, first=False, last=False):
                if not first:
                    copy_row(g + ADA_A - 1, mod_b_dram, g - 1)
                    act.wait_ge(s_z, 9 * g)
                    ada_high(g + ADA_A, 0)
                if not last:
                    split_w_in(g + 1, 1 - slot)
                for q in range(2 if first else 1, 4):
                    ada_high(g + ADA_A, q)

            group(0, 0, first=True)
            with act.Fori(0, 3) as i:
                for s in range(2):
                    group(2 * i + 1 + s, 1 - s)
            group(NZG - 1, 1, last=True)
            copy_row(ADA_G - 1, mod_b_dram, NZG - 1)

            ch = Chain(act, s_chA)
            for i in range(3):
                act.wait_ge(s_zst[i], 16 * 3 * NZG)
            act.wait_ge(s_rowst, 16 * ADA_G)
            act.wait_ge(s_cT, 1)
            act.activation(c_latT, psum[:, 0:2, :], ACT.Copy).then_inc(s_cA, 1)
            act.wait_ge(s_cT, 3)
            act.activation(kT[64:96, :, 512:1024], bank[4][0:32, :].unsqueeze(1).broadcast_to([32, H_MLA, 512]),
                           ACT.Copy).then_inc(s_cA, 1)
            act.wait_ge(s_cT, 4)
            for q in range(4):
                last = act.activation(kT[0:64, 2 * q, 512:1024], bank[q][0:64, :], ACT.Copy)
            last.then_inc(s_cA, 1)
            act.wait_ge(s_cT, 5)
            act.activation(v_mla[:, 4:6, :], psum[:, 4:6, :], ACT.Copy).then_inc(s_cA, 1)

            def front(m, s):
                r, slot = rows_of(m), m % 2
                b7, col = bank[7], key_col(m)
                x = z_in[:r, slot, :]
                if s == 0:
                    act.wait_ge(s_zi[slot], 48 * (m // 2 + 1))
                    if m:
                        act.wait_ge(s_lat, m)
                    act.activation(junk[:r, :QR], x[:, O_ZQ:O_ZQ + QR], ACT.Square, scale=QR ** -0.5,
                                   accum_out=sums[:r, 0:1])
                    ch.link(act.activation(junk[:r, QR:], x[:, O_KV:O_KV + KVR], ACT.Square, scale=KVR ** -0.5,
                                           accum_out=sums[:r, 1:2]))
                    ch.link(act.activation(rs[:r], sums[:r], ACT.Ln, bias=eps[:r]))
                    act.activation(rs[:r], rs[:r], ACT.Exp, scale=-0.5).then_inc(s_rs, 1)
                    if m:
                        act.wait_ge(s_gate, m)
                    act.activation(eg[:r], x[:, O_RG:O_RG + 256], ACT.Exp, scale=-1.0).then_inc(s_eg, 1)
                if s not in READ_A:
                    return
                act.wait_ge(s_fp, 12 * m + s + 1)
                v4 = b7.rearrange("p (k n) -> p k n", k=4)
                if s == 0:
                    last = act.activation(sqT[:, slot, :, :r], v4[:, 0:2, :r], ACT.Copy, scale=SB_SCALE)
                elif s == 1:
                    last = act.activation(qnT[:, :, :r], v4[:, 0:3, :r], ACT.Copy)
                elif s in (2, 3):
                    q4 = b7[:r, 0:384].rearrange("p (h d) -> p h d", h=4)
                    last = act.activation(qtok[:r, 384 * (s - 2):384 * (s - 1)].rearrange("p (h d) -> p h d", h=4)
                                          [:, :, 0:NOPE], q4[:, :, 0:NOPE], ACT.Copy)
                elif s == 4:
                    last = act.activation(latT[:, :, :r], v4[:, 0:2, :r], ACT.Copy)
                elif s == 5:
                    last = act.activation(qT[:QD, slot, 0:4, :r], v4[:QD, :, :r], ACT.Copy)
                elif s == 7:
                    last = act.activation(kT[0:64, 0:H_MLA:2, col:col + r], v4[0:64, :, :r], ACT.Copy)
                elif s == 8:
                    last = act.activation(v_mla[:r, SEQ[m], :], b7[:r, :], ACT.Copy)
                elif s == 9:
                    if m == 0:
                        act.wait_ge(s_init, 3)
                    for a in range(2):
                        act.activation(rqT[64 * a:64 * a + 64, :, a, :r], v4[64 * a:64 * a + 64, 0:2, :r], ACT.Copy,
                                       scale=DH ** -0.5)
                    last = act.activation(rkT[:, :, :r], v4[:, 2:4, :r], ACT.Copy)
                last.then_inc(s_fA, 1)

            def group_rstd(m):
                r = rows_of(m)
                act.wait_ge(s_var, m + 1)
                ch.link(act.activation(stat[:r, 2, :], stat[:r, 1, :], ACT.Ln, bias=eps[:r], scale=1.0 / DH))
                act.activation(stat[:r, 3, :], stat[:r, 2, :], ACT.Exp, scale=-0.5).then_inc(s_rr, 1)

            def softmax_exp(i):
                n = UNITS[i][0]
                r, w, j = rows_of(n), n_keys(n), count_units("M", i)
                act.wait_ge(s_mx, j + 1)
                if j >= 3:
                    before = max(x for x in range(i) if UNITS[x][1] == "M" and count_units("M", x) == j - 3)
                    nb = len(key_blocks(UNITS[before][0]))
                    act.wait_ge(s_tr, PIECE_NO["M", before, (nb + 3) // 4 - 1] + 1)
                if j >= 4:
                    act.wait_ge(s_o, 1 + PV_NO[[x for x in range(i) if UNITS[x][1] == "M"][-4]])
                act.activation(prob[:r, j % 3, :w], score_bank(i, w)[:r], ACT.Exp, bias=maxes[:r, j % 2, 1:2],
                               scale=MLA_SCALE, accum_out=rowsum[:r, j % 4, 0:1]).then_inc(s_p, 1)

            def stick_log(i):
                n = UNITS[i][0]
                r, w, j = rows_of(n), n_keys(n), count_units("S", i)
                e = esb[:r, j % 2, :w]
                act.wait_ge(s_zsb, j + 1)
                if j >= 2:
                    before = [x for x in range(i) if UNITS[x][1] == "S"][-2]
                    nb = len(key_blocks(UNITS[before][0]))
                    act.wait_ge(s_tr, PIECE_NO["S", before, (nb + 3) // 4 - 1] + 1)
                ch.link(act.activation(e, zsb[:r, j % 2, :w], ACT.Abs))
                ch.link(act.activation(e, e, ACT.Exp, scale=-1.0))
                act.activation(e, e, ACT.Ln, bias=1.0).then_inc(s_l, 1)

            def stick_weights(i):
                n = UNITS[i][0]
                r, w, j = rows_of(n), n_keys(n), count_units("S", i)
                act.wait_ge(s_wa, j + 1)
                act.activation(esb[:r, j % 2, :w], esb[:r, j % 2, :w], ACT.Exp).then_inc(s_w, 1)

            def copy_piece(x):
                kind, i, j = x
                q = PIECE_NO[x]
                act.wait_ge(s_tr, q + 1)
                src = bank[4 + q % 2].rearrange("p (k n) -> p k n", k=4)
                if kind == "X":
                    if i and j == 0:
                        act.wait_ge(s_mst, 16 * min(i, NTILE - 1))
                    r = rows_of(i)
                    out = mixT[:, 4 * j:4 * j + 4, :r] if i < NTILE - 1 else mix_raw[:, 4 * j:4 * j + 4, LP - P:LP]
                    act.activation(out, src[:, :, :r], ACT.Copy).then_inc(s_ptA, 1)
                    return
                n, wn = UNITS[i][0], W_NO[x]
                r = rows_of(n)
                blocks = key_blocks(n)[4 * j:4 * j + 4]
                if wn >= 4:
                    act.wait_ge(s_pv, wn - 3)
                last = act.activation(pT[:, wn % 4, :len(blocks), :r], src[:, :len(blocks), :r], ACT.Copy)\
                    if blocks[-1][1] == P else None
                if last is None:
                    if len(blocks) > 1:
                        act.activation(pT[:, wn % 4, :len(blocks) - 1, :r], src[:, :len(blocks) - 1, :r], ACT.Copy)
                    last = act.activation(pT[:LS, wn % 4, len(blocks) - 1, :r], src[:LS, len(blocks) - 1, :r], ACT.Copy)
                last.then_inc(s_ptA, 1)

            def split_hi(n3, raw, slot, first=False):
                act.wait_ge(s_wl[raw], 16 * n3 + 16)
                if not first:
                    idx = 3 * n3 + raw if isinstance(n3, int) else 16
                    if idx < 14:
                        act.wait_ge(s_y, 3 * (idx - 5))
                    elif idx < 16:
                        act.wait_ge(s_up, 3 * (idx - 13))
                    elif raw == 0:
                        act.wait_ge(s_dn, 24 * (n3 - 5))
                    else:
                        act.wait_ge(s_up, 6 * (n3 - 4) + 3 * raw)
                act.activation(wt_hi[:, slot], wt_raw[:, raw], ACT.Copy).then_inc(s_wh, 1)

            for step in range(-12, STEPS):
                m, s = divmod(step + 12, 12)
                for lag, kind, do in ((1, "M", softmax_exp), (1, "S", stick_log), (3, "S", stick_weights)):
                    if 0 <= step - lag < len(UNITS) and UNITS[step - lag][1] == kind:
                        do(step - lag)
                for x in PIECES.get(step, []):
                    if COPIER[x[0]] == "A":
                        copy_piece(x)
                if m < NTILE:
                    front(m, s)
                if step - EARLY_SPLIT in range(3):
                    split_hi(0, step - EARLY_SPLIT, step - EARLY_SPLIT, first=True)
                if s == 0 and 0 < m <= NTILE:
                    group_rstd(m - 1)

            act.wait_ge(s_pv, N_PIECES)
            act.wait_ge(s_mx4, 32)
            pieces_done(act, ORDER[-1])
            for c, (lo, hi) in enumerate(CHUNKS):
                for k in (0, 4):
                    act.activation(a_hi[:, k:k + 4, lo:hi], mix_raw[:, k:k + 4, lo:hi], ACT.Copy).then_inc(s_mhi, 1)
            for idx in range(3, 6):
                split_hi(1, idx % 3, idx, first=True)
            n_sq = 0
            for d in range(KT):
                if d + 6 < 10:
                    split_hi((d + 6) // 3, d % 3, d)
                for c in range(3):
                    act.wait_ge(s_yr, 3 * d + c + 1)
                    if n_sq == 0:
                        act.wait_ge(s_mlo, 6)
                    square(1, c, d, n_sq)
                    n_sq += 1
            rstd(1, 0)
            rstd(1, 1)
            rstd(1, 2)
            for c in range(3):
                h_high(1, c)

            act.preload_act_table_set("silu_and_others")
            act.wait_ge(s_h, 48)

            def copy_a(f, slot, first=False):
                for c in range(3):
                    act.wait_ge(s_up, 6 * f + c + 1)
                    if c == 0 and not first:
                        act.wait_ge(s_cs, f - 1)
                        act.wait_ge(s_co, f - 1)
                    for a, b, which in segments(c):
                        at = a + 2 + 2 * which
                        last = act.activation(a_ext[:, slot, at:at + b - a],
                                              bank[(3 * slot + c) % 2][:, a - CHUNKS[c][0]:b - CHUNKS[c][0]], ACT.Copy)
                    last.then_inc(s_ac, 1)

            def first_tap(f, slot, first=False):
                act.wait_ge(s_ac, 3 * f + 3)
                act.wait_ge(s_fv, f + 1)
                if not first:
                    act.wait_ge(s_u, 3 * f)
                act.activation(conv[:], a_ext[:, slot, 2:T + 4], ACT.Identity, bias=f_vec[:, slot, 3:4],
                               scale=f_vec[:, slot, 2:3]).then_inc(s_cv, 1)

            def silu(f):
                act.wait_ge(s_cs, f + 1)
                act.activation(conv[:], conv[:], ACT.Silu).then_inc(s_sl, 1)

            def u_high(f, slot, c, first=False):
                act.wait_ge(s_u, 3 * f + c + 1)
                if not first and c == 0:
                    act.wait_ge(s_dn, 24 * (f - 1))
                a, b = CHUNKS[c]
                act.activation(u_hi[:, slot, a:b], u_val[:, c % 2, :b - a], ACT.Copy).then_inc(s_uh, 1)

            def ffn_tile(f, slot, tiles, first=False, early=False):
                for n3, raw, ring in tiles[:1]:
                    split_hi(n3, raw, ring)
                copy_a(f, slot, first=early)
                first_tap(f, slot, first)
                for n3, raw, ring in tiles[1:2]:
                    split_hi(n3, raw, ring)
                silu(f)
                for c in range(3):
                    u_high(f, slot, c, first=early)
                for n3, raw, ring in tiles[2:]:
                    split_hi(n3, raw, ring)

            for idx in (10, 11):
                split_hi(idx // 3, idx % 3, idx % 6)
            ffn_tile(0, 0, [(4, 0, 0), (4, 1, 1), (4, 2, 2)], first=True, early=True)
            ffn_tile(1, 1, [(5, 0, 3), (5, 1, 4), (5, 2, 5)], early=True)
            with act.Fori(1, NF // 2 - 1) as i:
                ffn_tile(2 * i, 0, [(2 * i + 4, raw, raw) for raw in range(3)])
                ffn_tile(2 * i + 1, 1, [(2 * i + 5, raw, raw + 3) for raw in range(3)])
            ffn_tile(20, 0, [(24, 0, 0), (24, 1, 1)])
            ffn_tile(21, 1, [])

            act.preload_act_table_set("natural_log_exp_and_others")
            for t in range(NTILE):
                r, slot = ROWS[t], t % 2
                act.wait_ge(s_ft, t + 1)
                full = psum[:r, 2 * slot:2 * slot + 2, :].rearrange("p a b -> p (a b)")
                if t == 0:
                    act.wait_ge(s_wlow, 74)
                ch.link(act.activation(wt_raw[:r, t % 2, :], full, ACT.Square, accum_out=fin[:r, slot, 0:1]))
                ch.link(act.activation(fin[:r, slot, 1:2], fin[:r, slot, 0:1], ACT.Ln, bias=eps[:r], scale=1.0 / D))
                if t >= 2:
                    act.wait_ge(s_fy, t - 1)
                act.activation(fin[:r, slot, 2:3], fin[:r, slot, 1:2], ACT.Exp, scale=-0.5).then_inc(s_fs, 1)

        @block.vector
        def _(dve):
            dve.memset(ones[:], 1.0).then_inc(s_set, 1)
            dve.memset(eps[:], EPS).then_inc(s_set, 1)
            def write_mod(n, src, at, count):
                parts = src.rearrange("p (s c j) -> p s j c", s=2, c=2)
                out = mod[:, at:at + count, :]
                dve.wait_ge(s_modt, n + 1)
                dve.tensor_tensor(out, parts[:, 0], vec_a[:, at:at + count].unsqueeze(2).broadcast_to([P, count, 2]),
                                  ALU.add).then_inc(s_mod, 1)
                dve.wait_ge(s_mod, 2 * n + 1)
                dve.tensor_tensor(out, parts[:, 1], out, ALU.add).then_inc(s_mod, 1)
                dve.wait_ge(s_mod, 2 * n + 2)

            def copy_x(t):
                dve.wait_ge(s_xt, 2 * t + 1)
                dve.tensor_copy(xT[:, 0:4, P * t:P * t + ROWS[t]],
                                bank[2 * (t % 2)][:, :].rearrange("p (k n) -> p k n", k=4)[:, :, :ROWS[t]])\
                    .then_inc(s_xeD, 1)

            def ada_low(g, q):
                for k in (2 * q, 2 * q + 1):
                    dve.wait_ge(s_ahi, 8 * g + k + 1)
                    dve.tensor_tensor(ada_lo[:, k % 4], ada_raw[:, q, k % 2], ada_hi[:, k % 4].bitcast(F32),
                                      ALU.subtract).then_inc(s_alo, 1)

            for t in range(3):
                copy_x(t)
            dve.wait_ge(s_vt, 3)
            dve.tensor_copy(vec_a[:], bank[7][:, 0:N_A]).then_inc(s_vec, 1)
            dve.tensor_copy(vec_b[:], bank[7][:, 128:128 + N_B]).then_inc(s_vec, 1)
            dve.tensor_copy(vec_c[:], bank[7][:, 256:256 + N_C]).then_inc(s_vec, 1)
            dve.wait_ge(s_silu, 1)
            dve.tensor_scalar(silu_e[:], silu_e[:], 1.0, None, ALU.add).then_inc(s_silu, 1)
            dve.wait_ge(s_silu, 2)
            dve.reciprocal(silu_e[:], silu_e[:]).then_inc(s_silu, 1)
            dve.wait_ge(s_silu, 3)
            dve.tensor_tensor(silu_c[:], silu_e[:], vec_a[:, 64:80].rearrange("p (c k) -> p c k", c=2), ALU.mult)\
                .then_inc(s_siluv, 1)

            dve.wait_ge(s_chi, 1)
            dve.wait_ge(s_siluv, 1)
            dve.tensor_tensor(c_parts[:, :, 2:4], silu_c[:].rearrange("p c k -> p k c"),
                              c_parts[:, :, 0:2].bitcast(F32), ALU.subtract).then_inc(s_cpl, 1)
            for t in range(3, 6):
                copy_x(t)
            ada_low(0, 0)
            ada_low(0, 1)
            for t in range(6, NTILE):
                copy_x(t)
            for i in range(2, 4 * ADA_A):
                ada_low(i // 4, i % 4)

            def norm_scale(n):
                dve.scalar_tensor_tensor(out=scale_n[:, n], in0=mod[:, 24 * n + 8:24 * n + 16, :], scalar=1.0,
                                         in1=vec_a[:, 48 + 8 * n:56 + 8 * n].unsqueeze(2).broadcast_to([P, KT, 2]),
                                         op0=ALU.add, op1=ALU.mult).then_inc(s_scale, 1)


            def normed(n, c, k):
                bufs = norm_bufs[n]
                j = 24 * n + 8 * c + k
                if k == 0:
                    dve.wait_ge(s_rb, 3 * n + c + 1)
                if j >= 3:
                    dve.wait_ge(s_h, j - 2)
                for a, b, which in segments(c):
                    last = dve.scalar_tensor_tensor(out=bufs["hn"][:, (8 * c + k) % 3, a - CHUNKS[c][0]:b - CHUNKS[c][0]],
                                                    in0=bufs["x"][:, k, a:b], scalar=scale_n[:, n, k, which:which + 1],
                                                    in1=bufs["rb"][:, a:b], op0=ALU.mult, op1=ALU.mult)
                last.then_inc(s_hn, 1)

            def h_low(n, c, k):
                bufs = norm_bufs[n]
                j = 24 * n + 8 * c + k
                dve.wait_ge(s_hn, j + 1)
                dve.wait_ge(s_hhi, j + 1)
                for a, b, which in segments(c):
                    last = dve.scalar_tensor_tensor(out=bufs["lo"][:, k, a:b],
                                                    in0=bufs["hn"][:, (8 * c + k) % 3, a - CHUNKS[c][0]:b - CHUNKS[c][0]],
                                                    scalar=mod[:, 24 * n + k, which:which + 1],
                                                    in1=bufs["hi"][:, k, a:b].bitcast(F32), op0=ALU.add, op1=ALU.subtract)
                last.then_inc(s_h, 1)

            def norm(n, chunks):
                order = [(c, k) for c in chunks for k in range(KT)]
                for i, (c, k) in enumerate(order):
                    normed(n, c, k)
                    if i:
                        h_low(n, *order[i - 1])
                h_low(n, *order[-1])

            def split_w_in(g, slot, half):
                dve.wait_ge(s_whi, 2 * g + half + 1)
                dve.tensor_tensor(w_lo[:, slot, 4 * half:4 * half + 4], w_raw[:, half],
                                  w_hi[:, slot, 4 * half:4 * half + 4].bitcast(F32), ALU.subtract)\
                    .then_inc(s_wlo, 1)

            def z_group(g, slot, split_next=True, first=False):
                if not first:
                    ada_low(g + ADA_A, 0)
                for t in range(NTILE):
                    dve.wait_ge(s_z, 9 * g + t + 1)
                    if not first or t >= 3:
                        dve.wait_ge(s_zst[t % 3], 48 * g + 16 * (t // 3))
                    dve.tensor_copy(z_out[:ROWS[t], t % 3, :], bank[t % 3][:ROWS[t], 0:ZG]).then_inc(s_zc, 1)
                    if first and t == 1:
                        norm(0, [2])
                    if t in (1, 3, 5) and not (first and t == 1):
                        ada_low(g + ADA_A, (t + 1) // 2)
                    if split_next and t in (2, 4):
                        split_w_in(g + 1, 1 - slot, t // 2 - 1)

            split_w_in(0, 0, 0)
            split_w_in(0, 0, 1)
            ada_low(ADA_A, 0)
            ada_low(ADA_A, 1)
            write_mod(0, bank[7][:, 384:448], 0, 16)
            norm_scale(0)
            dve.wait_ge(s_scale, 1)
            norm(0, [0, 1])
            z_group(0, 0, first=True)
            with dve.Fori(0, 3) as i:
                for s in range(2):
                    z_group(2 * i + 1 + s, 1 - s)
            z_group(NZG - 1, 1, split_next=False)

            ch = Chain(dve, s_chD)
            dve.wait_ge(s_z, 9 * NZG)
            dve.wait_ge(s_adamm, 8 * ADA_G)
            dve.wait_ge(s_row, ADA_G)
            dve.wait_ge(s_rowst, 16 * ADA_G)
            dve.wait_ge(s_xst, 16)
            for i in range(3):
                dve.wait_ge(s_zst[i], 16 * 3 * NZG)
            dve.memset(state[:], 0.0).then_inc(s_init, 1)
            dve.memset(zero[:], 0.0).then_inc(s_init, 1)
            dve.wait_ge(s_cT, 3)
            dve.memset(rqT[:], 0.0).then_inc(s_init, 1)
            dve.wait_ge(s_tab, 16 * N_TAB)
            dve.wait_ge(s_cau, 16)
            for k in range(3):
                last = dve.tensor_scalar(w_uq[:, k, :], w_uq[:, k, :], vec_a[:, 80 + k:81 + k], None, ALU.mult)
            last.then_inc(s_wuq, 1)
            write_mod(1, bank[7][:, 0:P], 16, 32)
            norm_scale(1)
            dve.wait_ge(s_cT, 2)
            dve.tensor_copy(skT[:, :, 512:1024], psum[:, 2:4, :]).then_inc(s_cD, 1)
            dve.wait_ge(s_cT, 4)
            for q in range(4):
                last = dve.tensor_copy(kT[0:64, 2 * q + 1, 512:1024], bank[q][64:128, :])
            last.then_inc(s_cD, 1)
            dve.wait_ge(s_cT, 6)
            dve.tensor_copy(v_mla[:, 6:8, :], psum[:, 6:8, :]).then_inc(s_cD, 1)

            def front(m, s):
                r, slot = rows_of(m), m % 2
                b7, col = bank[7], key_col(m)
                v4 = b7.rearrange("p (k n) -> p k n", k=4)
                x = z_in[:r, slot, :]
                if s == 0:
                    dve.wait_ge(s_rs, m + 1)
                    if m:
                        dve.wait_ge(s_fp, 12 * m)
                        dve.wait_ge(s_latst, 32 * m)
                    dve.tensor_scalar(zqn[:r], x[:, O_ZQ:O_ZQ + QR], rs[:r, 0:1], None, ALU.mult)
                    dve.scalar_tensor_tensor(out=lat[:r], in0=x[:, O_KV:O_KV + KVR], scalar=rs[:r, 1:2],
                                             in1=g_kv[:r], op0=ALU.mult, op1=ALU.mult).then_inc(s_lat, 1)
                if s == 1:
                    dve.wait_ge(s_g1, m + 1)
                    dve.reciprocal(eg[:r], eg[:r]).then_inc(s_g2, 1)
                if s not in READ_D:
                    return
                dve.wait_ge(s_fp, 12 * m + s + 1)
                if s in READ_A and s != 7:
                    dve.wait_ge(s_fA, read_a(m, s) + 1)
                if s == 0:
                    last = dve.tensor_copy(skT[:, :, col:col + r], v4[:, 2:4, :r])
                elif s in (2, 3):
                    q4 = b7[:r, 0:384].rearrange("p (h d) -> p h d", h=4)

                    def tab(a, n):
                        return rope_t[:r, slot, 128 + a:128 + a + n].unsqueeze(1).broadcast_to([r, 4, n])

                    if not (m == 0 and s == 2):
                        dve.wait_ge(s_fD, read_d(m, s))
                    dve.tensor_tensor(q_a[:r], q4[:, :, NOPE:QD], tab(0, ROPE), ALU.mult)
                    dve.tensor_tensor(q_b[:r, :, 0:16], q4[:, :, NOPE + 16:QD], tab(32, 16), ALU.mult)
                    ch.link(dve.tensor_tensor(q_b[:r, :, 16:32], q4[:, :, NOPE:NOPE + 16], tab(48, 16), ALU.mult))
                    last = dve.tensor_tensor(qtok[:r, 384 * (s - 2):384 * (s - 1)]
                                             .rearrange("p (h d) -> p h d", h=4)[:, :, NOPE:QD],
                                             q_a[:r], q_b[:r], ALU.add)
                elif s == 4:
                    last = dve.tensor_copy(kT[64:96, :, col:col + r],
                                           v4[0:32, 2, :r].unsqueeze(1).broadcast_to([32, H_MLA, r]))
                elif s == 6:
                    last = dve.tensor_copy(qT[:QD, slot, 4:8, :r], v4[:QD, :, :r])
                elif s == 7:
                    last = dve.tensor_copy(kT[0:64, 1:H_MLA:2, col:col + r], v4[64:128, :, :r])
                elif s == 9:
                    last = dve.tensor_tensor(rqdT[:, :, :r], v4[:, 0:2, :r], q_decayT[:, :, :r], ALU.mult)
                elif s == 10:
                    last = dve.tensor_tensor(att[:r, :, :r], v4[:r, :, :r], decayT[:r, :, :r], ALU.mult)
                elif s == 11:
                    st = state[:, int(m > 0)]
                    o4 = b7[:r, 0:256].rearrange("p (h d) -> p h d", h=4)
                    ch.link(dve.tensor_tensor(st, st, state_decay[:, int(m == 0)], ALU.mult))
                    dve.tensor_reduce(stat[:r, 0, :], o4, AX, ALU.add)
                    dve.tensor_tensor(st[0:64, :, 0:64], st[0:64, :, 0:64], v4[0:64, 2:4, 0:64], ALU.add)
                    ch.link(dve.tensor_tensor(st[64:128, :, 64:128], st[64:128, :, 64:128], v4[64:128, 2:4, 64:128],
                                              ALU.add))
                    ch.link(dve.tensor_scalar(stat[:r, 0, :], stat[:r, 0, :], -1.0 / DH, None, ALU.mult))
                    last = dve.tensor_tensor(oc[:r], o4, stat[:r, 0, :].unsqueeze(2).broadcast_to([r, H_RET, DH]),
                                             ALU.add)
                last.then_inc(s_fD, 1)
                if s == 11:
                    dve.wait_ge(s_fD, read_d(m + 1, 0))
                    ch.link(dve.tensor_tensor(oc2[:r], oc[:r], oc[:r], ALU.mult))
                    dve.tensor_reduce(stat[:r, 1, :], oc2[:r], AX, ALU.add).then_inc(s_var, 1)

            def retention_out(m):
                r = rows_of(m)
                dve.wait_ge(s_rr, m + 1)
                ch.link(dve.tensor_tensor(oc[:r], oc[:r], stat[:r, 3, :].unsqueeze(2).broadcast_to([r, H_RET, DH]),
                                          ALU.mult))
                dve.wait_ge(s_gate, m + 1)
                dve.tensor_tensor(mixtok[:r, m % 2, 512:768], oc[:r].rearrange("p h d -> p (h d)"), gate[:r],
                                  ALU.mult).then_inc(s_ret, 1)

            def row_max(i):
                n = UNITS[i][0]
                r, w, j = rows_of(n), n_keys(n), count_units("M", i)
                dve.wait_ge(s_sc, i + 1)
                if n:
                    ch.link(dve.memset(score_bank(i, w)[0:64, w - 64:w], NEG))
                if j >= 2:
                    dve.wait_ge(s_p, j - 1)
                ch.link(dve.tensor_reduce(maxes[:r, j % 2, 0:1], score_bank(i, w)[:r], AX, ALU.max))
                dve.tensor_scalar(maxes[:r, j % 2, 1:2], maxes[:r, j % 2, 0:1], -MLA_SCALE, None, ALU.mult)\
                    .then_inc(s_mx, 1)

            def stick_logits(i):
                n = UNITS[i][0]
                r, w, j = rows_of(n), n_keys(n), count_units("S", i)
                dve.wait_ge(s_sc, i + 1)
                if j >= 2:
                    dve.wait_ge(s_wa, j - 1)
                if w > r:
                    dve.tensor_copy(zsb[:r, j % 2, :w - r], score_bank(i, w)[:r, :w - r])
                dve.tensor_tensor(zsb[:r, j % 2, w - r:w], score_bank(i, w)[:r, w - r:w], causal[:r, :r], ALU.add)\
                    .then_inc(s_zsb, 1)

            def stick_sums(i):
                n = UNITS[i][0]
                r, w, j = rows_of(n), n_keys(n), count_units("S", i)
                e = esb[:r, j % 2, :w]
                dve.wait_ge(s_l, j + 1)
                ch.link(dve.scalar_tensor_tensor(out=e, in0=zsb[:r, j % 2, :w], scalar=0.0, in1=e, op0=ALU.max,
                                                 op1=ALU.add))
                back = e[:, ::-1]
                dve.tensor_tensor_scan(back, back, zero[:r, :].broadcast_to([r, w]), 0.0, ALU.add, ALU.add).then_inc(s_c, 1)

            def copy_piece(x):
                kind, i, j = x
                q, wn = PIECE_NO[x], W_NO[x]
                n = UNITS[i][0]
                r = rows_of(n)
                blocks = key_blocks(n)[4 * j:4 * j + 4]
                dve.wait_ge(s_tr, q + 1)
                if wn >= 4:
                    dve.wait_ge(s_pv, wn - 3)
                src = bank[4 + q % 2].rearrange("p (k n) -> p k n", k=4)
                full = len(blocks) - (blocks[-1][1] < P)
                if full:
                    last = dve.tensor_copy(pT[:, wn % 4, :full, :r], src[:, :full, :r])
                if full < len(blocks):
                    last = dve.tensor_copy(pT[:LS, wn % 4, full, :r], src[:LS, full, :r])
                last.then_inc(s_ptD, 1)

            def head_output(i):
                n, kind, h = UNITS[i]
                r, v = rows_of(n), PV_NO[i]
                nb = len(key_blocks(n))
                o = bank[6][:r, 64 * (v % 8):64 * (v % 8) + 64]
                if kind == "M":
                    j = count_units("M", i)
                    dve.wait_ge(s_p, j + 1)
                    ch.link(dve.reciprocal(rowsum[:r, j % 4, 1:2], rowsum[:r, j % 4, 0:1]))
                    dve.wait_ge(s_pv, W_NO[kind, i, (nb + 3) // 4 - 1] + 1)
                    dve.tensor_scalar(mixtok[:r, n % 2, 64 * h:64 * h + 64], o, rowsum[:r, j % 4, 1:2], None,
                                      ALU.mult).then_inc(s_o, 1)
                else:
                    dve.wait_ge(s_pv, W_NO[kind, i, (nb + 3) // 4 - 1] + 1)
                    dve.tensor_copy(mixtok[:r, n % 2, 768 + 64 * h:832 + 64 * h], o).then_inc(s_o, 1)

            def split_lo(n3, raw, slot):
                dve.wait_ge(s_wh, 3 * n3 + raw + 1)
                dve.tensor_tensor(wt_lo[:, slot], wt_raw[:, raw], wt_hi[:, slot].bitcast(F32), ALU.subtract)\
                    .then_inc(s_wlow, 1)

            for step in range(-12, STEPS):
                m, s = divmod(step + 12, 12)
                if 0 <= step < len(UNITS):
                    (row_max if UNITS[step][1] == "M" else stick_logits)(step)
                if 0 <= step - 2 < len(UNITS) and UNITS[step - 2][1] == "S":
                    stick_sums(step - 2)
                for x in PIECES.get(step - 1, []):
                    if x[0] != "X" and x[2] == 0:
                        head_output(x[1])
                for x in PIECES.get(step, []):
                    if COPIER[x[0]] == "D":
                        copy_piece(x)
                if s == 0 and 0 < m <= NTILE:
                    retention_out(m - 1)
                if step - EARLY_SPLIT in range(3):
                    split_lo(0, step - EARLY_SPLIT, step - EARLY_SPLIT)
                if m < NTILE:
                    front(m, s)

            for c, (lo, hi) in enumerate(CHUNKS):
                for k in (0, 4):
                    dve.wait_ge(s_mhi, 2 * c + k // 4 + 1)
                    dve.tensor_tensor(a_lo[:, k:k + 4, lo:hi], mix_raw[:, k:k + 4, lo:hi],
                                      a_hi[:, k:k + 4, lo:hi].bitcast(F32), ALU.subtract).then_inc(s_mlo, 1)
            for idx in range(3, 6):
                split_lo(1, idx % 3, idx)
            dve.wait_ge(s_res, 16)
            for d in range(KT):
                for c in range(3):
                    dve.wait_ge(s_y, 3 * d + c + 1)
                    for a, b, which in segments(c):
                        last = dve.scalar_tensor_tensor(
                            out=res[:, d, a:b], in0=bank[(3 * d + c) % 5][:, a - CHUNKS[c][0]:b - CHUNKS[c][0]],
                            scalar=mod[:, 16 + d, which:which + 1], in1=res[:, d, a:b], op0=ALU.mult, op1=ALU.add)
                    last.then_inc(s_yr, 1)
                if d + 6 < 10:
                    split_lo((d + 6) // 3, d % 3, d)
            norm(1, range(3))

            dve.memset(a_ext[:, 0, 0:2], 0.0).then_inc(s_cvi, 1)
            dve.memset(a_ext[:, 1, 0:2], 0.0).then_inc(s_cvi, 1)
            b_taps = vec_b[:].rearrange("p (j f) -> p f j", j=4)
            b_state = vec_c[:].rearrange("p (j f) -> p f j", j=2)

            def vectors(f, slot, first=False):
                if not first:
                    dve.wait_ge(s_cv, f - 1)
                    dve.wait_ge(s_cs, f - 1)
                dve.tensor_copy(f_vec[:, slot, :].unsqueeze(1), b_taps[:, bass.ds(f, 1), :])
                dve.tensor_copy(a_ext[:, slot, LP + 2:LP + 4].unsqueeze(1), b_state[:, bass.ds(f, 1), :])\
                    .then_inc(s_fv, 1)

            def taps(f, slot):
                dve.wait_ge(s_cv, f + 1)
                dve.scalar_tensor_tensor(out=conv[:], in0=a_ext[:, slot, 1:T + 3], scalar=f_vec[:, slot, 1:2],
                                         in1=conv[:], op0=ALU.mult, op1=ALU.add).then_inc(s_c1, 1)
                for j, at in enumerate((LP, T + 2)):
                    last = dve.tensor_copy(conv_out[:, 2 * j:2 * j + 2, bass.ds(f, 1)],
                                           a_ext[:, slot, at:at + 2].unsqueeze(2))
                last.then_inc(s_co, 1)
                dve.wait_ge(s_c1, f + 1)
                dve.scalar_tensor_tensor(out=conv[:], in0=a_ext[:, slot, 0:T + 2], scalar=f_vec[:, slot, 0:1],
                                         in1=conv[:], op0=ALU.mult, op1=ALU.add).then_inc(s_cs, 1)

            def gate_u(f, slot, c):
                dve.wait_ge(s_up, 6 * f + 4 + c)
                if c == 0:
                    dve.wait_ge(s_sl, f + 1)
                if not (isinstance(f, int) and 3 * f + c < 2):
                    dve.wait_ge(s_ul, 3 * f + c - 1)
                for a, b, which in segments(c):
                    last = dve.tensor_tensor(u_val[:, c % 2, a - CHUNKS[c][0]:b - CHUNKS[c][0]],
                                             bank[2 + (3 * slot + c) % 2][:, a - CHUNKS[c][0]:b - CHUNKS[c][0]],
                                             conv[:, a + 2 * which:b + 2 * which], ALU.mult)
                last.then_inc(s_u, 1)

            def u_low(f, slot, c):
                a, b = CHUNKS[c]
                dve.wait_ge(s_uh, 3 * f + c + 1)
                dve.tensor_tensor(u_lo[:, slot, a:b], u_val[:, c % 2, :b - a], u_hi[:, slot, a:b].bitcast(F32),
                                  ALU.subtract).then_inc(s_ul, 1)

            def add_down(f, n):
                for q in range(4 * n, 4 * n + 4):
                    d, c = divmod(q, 3)
                    dve.wait_ge(s_dn, 24 * f + q + 1)
                    for a, b, which in segments(c):
                        last = dve.scalar_tensor_tensor(
                            out=res[:, d, a:b], in0=bank[4 + q % 4][:, a - CHUNKS[c][0]:b - CHUNKS[c][0]],
                            scalar=mod[:, 40 + d, which:which + 1], in1=res[:, d, a:b], op0=ALU.mult, op1=ALU.add)
                    last.then_inc(s_dr, 1)

            def ffn_tile(f, slot, tiles, early=False, down=True):
                vectors(f, slot, first=early)
                for n in range(6):
                    if n == 4:
                        gate_u(f, slot, 0)
                    if n == 5:
                        gate_u(f, slot, 1)
                        u_low(f, slot, 0)
                    if n == 0 and tiles:
                        split_lo(*tiles[0])
                    if n == 3:
                        taps(f, slot)
                        if len(tiles) > 1:
                            split_lo(*tiles[1])
                    if down:
                        add_down(f - 1, n)
                u_low(f, slot, 1)
                gate_u(f, slot, 2)
                u_low(f, slot, 2)
                for t in tiles[2:]:
                    split_lo(*t)

            for idx in (10, 11):
                split_lo(idx // 3, idx % 3, idx % 6)
            ffn_tile(0, 0, [(4, 0, 0), (4, 1, 1), (4, 2, 2)], early=True, down=False)
            ffn_tile(1, 1, [(5, 0, 3), (5, 1, 4), (5, 2, 5)], early=True)
            with dve.Fori(1, NF // 2 - 1) as i:
                ffn_tile(2 * i, 0, [(2 * i + 4, raw, raw) for raw in range(3)])
                ffn_tile(2 * i + 1, 1, [(2 * i + 5, raw, raw + 3) for raw in range(3)])
            ffn_tile(20, 0, [(24, 0, 0), (24, 1, 1)])
            ffn_tile(21, 1, [])
            for n in range(6):
                add_down(21, n)

            dve.wait_ge(s_cvt, 1)
            dve.tensor_copy(conv_rows[0:88, :], bank[7][0:88, 0:P]).then_inc(s_cvc, 1)
            dve.wait_ge(s_gf, 16)
            for t in range(NTILE):
                r, slot = ROWS[t], t % 2
                dve.wait_ge(s_fs, t + 1)
                if t >= 2:
                    dve.wait_ge(s_yst[slot], 16 * (t // 2))
                dve.scalar_tensor_tensor(out=y_out[:r, slot], in0=psum[:r, 2 * slot:2 * slot + 2, :]
                                         .rearrange("p a b -> p (a b)"), scalar=fin[:r, slot, 2:3], in1=g_fin[:r],
                                         op0=ALU.mult, op1=ALU.mult).then_inc(s_fy, 1)

        @block.tensor
        def _(pe):
            def ada_piece(g, q):
                if q == 0 and not (isinstance(g, int) and g == 0):
                    pe.wait_ge(s_row, g)
                for k in (2 * q, 2 * q + 1):
                    pe.wait_ge(s_alo, 8 * g + k + 1)
                    pe.matmul(bank[5][0:4, :], c_parts[:, k, :], ada_hi[:, k % 4, :], start=(k == 0), stop=False)
                    pe.matmul(bank[5][0:4, :], c_parts[:, k, :], ada_lo[:, k % 4, :], start=False,
                              stop=(k == KT - 1)).then_inc(s_adamm, 1)

            def x_transposes(t):
                pe.wait_ge(s_x[t], 16)
                if t >= 2:
                    pe.wait_ge(s_xeD, t - 1)
                    pe.wait_ge(s_xeA, t - 1)
                for j in range(2):
                    for k in range(4):
                        last = pe.transpose(bank[2 * (t % 2) + j][:, P * k:P * k + ROWS[t]],
                                            x_in[:ROWS[t], t, P * (4 * j + k):P * (4 * j + k) + P],
                                            ident[:ROWS[t], :ROWS[t]])
                    last.then_inc(s_xt, 1)

            def sum_squares(n, c):
                a, b = CHUNKS[c]
                for k in range(KT):
                    j = 24 * n + 8 * c + k
                    if j == 0:
                        pe.wait_ge(s_set, 2)
                    if k == 0 and 3 * n + c > 0:
                        pe.wait_ge(s_ln, 3 * n + c)
                    pe.wait_ge(s_sq, j + 1)
                    pe.matmul(bank[4][:, :b - a], ones[:], sq_hn[:, j % SQ_SLOTS[0], :b - a], start=(k == 0), stop=(k == KT - 1))\
                        .then_inc(s_ms, 1)

            pe.wait_ge(s_id, 16)
            for c, tiles in enumerate(((0, 1, 2, 3), (4, 5, 6), (7, 8))):
                for t in tiles:
                    x_transposes(t)
                    if t == 2:
                        pe.wait_ge(s_const, 16 * n_const)
                        for i, n in enumerate((N_A, N_B, N_C)):
                            pe.transpose(bank[7][:, 128 * i:128 * i + n], vec_in[:n, i, :], ident[:n, :n])\
                                .then_inc(s_vt, 1)
                sum_squares(0, c)
                if c == 1:
                    pe.wait_ge(s_cpl, 1)
                    ada_piece(0, 0)
                    ada_piece(0, 1)
            for i in range(2, 4 * ADA_A):
                ada_piece(i // 4, i % 4)
            pe.wait_ge(s_modl, 16)
            pe.transpose(bank[7][:, 384:448], mod_rows[0:64, :], ident[0:64, 0:64]).then_inc(s_modt, 1)

            def z_group(g, slot, first=False):
                pe.wait_ge(s_wlo, 2 * g + 2)
                for t in range(NTILE):
                    r = ROWS[t]
                    if first:
                        pe.wait_ge(s_h, 8 * (chunk_of(t) + 1))
                    if not first or t >= 3:
                        pe.wait_ge(s_zc, 9 * g + t - 2)
                    for k in range(KT):
                        for m, (hh, ww) in enumerate(((h_hi, w_hi), (h_hi, w_lo), (h_lo, w_hi))):
                            last = pe.matmul(bank[t % 3][:r, 0:ZG], hh[:, k, P * t:P * t + r], ww[:, slot, k, :],
                                             start=(k == 0 and m == 0), stop=(k == KT - 1 and m == 2))
                    last.then_inc(s_z, 1)
                    if t % 2:
                        ada_piece(g + ADA_A, t // 2)

            z_group(0, 0, first=True)
            with pe.Fori(0, 3) as i:
                for s in range(2):
                    z_group(2 * i + 1 + s, 1 - s)
            z_group(NZG - 1, 1)

            pe.wait_ge(s_cache, 48)
            pe.wait_ge(s_zc, 9 * NZG)
            pe.wait_ge(s_row, ADA_G)
            pe.wait_ge(s_ln, 3)
            pe.wait_ge(s_modl, 32)
            pe.transpose(bank[7][:, 0:P], mod_rows[:], ident[:]).then_inc(s_modt, 1)
            for j in range(4):
                for k in range(2):
                    last = pe.transpose(bank[k][:, P * j:P * j + P], c_lat[:, j, P * k:P * k + P], ident[:])
            last.then_inc(s_cT, 1)
            for j in range(4):
                for k in range(2):
                    last = pe.transpose(bank[2 + k][:, P * j:P * j + P], c_sk[:, j, P * k:P * k + P], ident[:])
            last.then_inc(s_cT, 1)
            for j in range(4):
                last = pe.transpose(bank[4][0:32, P * j:P * j + P], c_kr[:, j, :], ident[:])
            last.then_inc(s_cT, 1)

            def nope_keys(out, q, lhs_latT, n):
                for k in range(2):
                    last = pe.matmul(out, w_uk[:, k, P * q:P * q + P], lhs_latT[:, k, :n], start=(k == 0), stop=(k == 1))
                return last

            def values(out, latT_tile, r):
                for k in range(2):
                    last = pe.matmul(out, latT_tile[:, k, :r], w_uv[:, k, :], start=(k == 0), stop=(k == 1))
                return last

            pe.wait_ge(s_tab, 16 * N_TAB)
            pe.wait_ge(s_cA, 1)
            pe.wait_ge(s_cD, 1)
            for q in range(4):
                last = nope_keys(bank[q], q, c_latT, 512)
            last.then_inc(s_cT, 1)
            pe.wait_ge(s_cA, 2)
            pe.wait_ge(s_mod, 4)
            for j in range(4):
                last = values(bank[4 + j], c_latT[:, :, P * j:P * j + P], P)
                if j % 2:
                    last.then_inc(s_cT, 1)

            def front(m, s):
                r, slot, b7 = rows_of(m), m % 2, bank[7]
                x = z_in[:r, slot, :]

                def turn(at, src, width):
                    return pe.transpose(b7[:width, P * at:P * at + r], src, ident[:r, :r])

                if m == 0 and s == 0:
                    pe.wait_ge(s_cD, 3)
                else:
                    pe.wait_ge(s_fA, read_a(m, s))
                    pe.wait_ge(s_fD, read_d(m, s))
                if s == 0:
                    pe.wait_ge(s_zi[slot], 48 * (m // 2 + 1))
                    for j, at in enumerate((O_SQ, O_SQ + P, O_SK, O_SK + P)):
                        last = turn(j, x[:, at:at + P], P)
                elif s == 1:
                    pe.wait_ge(s_lat, m + 1)
                    for k in range(3):
                        last = turn(k, zqn[:r, P * k:P * k + P], P)
                elif s in (2, 3):
                    if m == 0 and s == 2:
                        pe.wait_ge(s_wuq, 1)
                    for k in range(3):
                        last = pe.matmul(b7[:r, 0:384], qnT[:, k, :r], w_uq[:, k, 384 * (s - 2):384 * (s - 1)],
                                         start=(k == 0), stop=(k == 2))
                elif s == 4:
                    pe.wait_ge(s_kr, m + 1)
                    for k in range(2):
                        turn(k, lat[:r, P * k:P * k + P], P)
                    last = turn(2, kr[:r, :], ROPE)
                elif s in (5, 6):
                    for j in range(4):
                        h = 4 * (s - 5) + j
                        last = turn(j, qtok[:r, QD * h:QD * h + QD], QD)
                elif s == 7:
                    for q in range(4):
                        last = nope_keys(b7[:, P * q:P * q + r], q, latT, r)
                elif s == 8:
                    last = values(b7[:r, :], latT, r)
                elif s == 9:
                    pe.wait_ge(s_rot, m + 1)
                    for j in range(4):
                        last = turn(j, rqk[:r].rearrange("p h d -> p (h d)")[:, P * j:P * j + P], P)
                elif s == 10:
                    for q in range(2):
                        last = pe.matmul(b7[:r, 256 * q:256 * q + 256].rearrange("p (a n) -> p a n", a=2)[:, :, :r],
                                         rkT[:, q, :r], rqT[:, q, :, :r], start=True, stop=True)
                elif s == 11:
                    if m == 0:
                        pe.wait_ge(s_sv, 80)
                    kd2 = kd[:r].rearrange("p h d -> p (h d)")
                    for q in range(2):
                        pe.matmul(b7[:, 256 + P * q:256 + P * q + P], kd2[:, P * q:P * q + P],
                                  x[:, O_RV + P * q:O_RV + P * q + P], start=True, stop=True)
                    for q in range(2):
                        pe.matmul(b7[:r, P * q:P * q + P], rqdT[:, q, :r], state[:, int(m > 0), q, :],
                                  start=True, stop=False)
                        for a in range(2):
                            h = 2 * q + a
                            last = pe.matmul(b7[:r, DH * h:DH * h + DH], att[:r, h, :r],
                                             x[:, O_RV + DH * h:O_RV + DH * h + DH], start=False, stop=(a == 1))
                last.then_inc(s_fp, 1)

            def scores(i):
                n, kind, h = UNITS[i]
                r, slot, w = rows_of(n), n % 2, n_keys(n)
                first = key_blocks(n)[0][0]
                if i >= 2:
                    if UNITS[i - 2][1] == "M":
                        pe.wait_ge(s_p, count_units("M", i - 2) + 1)
                    else:
                        pe.wait_ge(s_zsb, count_units("S", i - 2) + 1)
                for a in range(0, w, 512):
                    b = min(w, a + 512)
                    out = score_bank(i, w)[:r, a:b]
                    if kind == "M":
                        last = pe.matmul(out, qT[:QD, slot, h, :r], kT[:QD, h, first + a:first + b],
                                         start=True, stop=True)
                    else:
                        lo = 64 * (h % 2)
                        last = pe.matmul(out, sqT[lo:lo + 64, slot, h // 2, :r],
                                         skT[lo:lo + 64, h // 2, first + a:first + b], start=True, stop=True)
                last.then_inc(s_sc, 1)

            def transposes(x):
                kind, i, j = x
                q = PIECE_NO[x]
                if q >= 2:
                    pieces_done(pe, ORDER[q - 2])
                out = bank[4 + q % 2]
                if kind == "X":
                    r = rows_of(i)
                    if j == 0:
                        pe.wait_ge(s_ret, i + 1)
                        pe.wait_ge(s_o, 12 * (i + 1))
                    for k in range(4):
                        last = pe.transpose(out[:, P * k:P * k + r],
                                            mixtok[:r, i % 2, P * (4 * j + k):P * (4 * j + k) + P], ident[:r, :r])
                else:
                    n = UNITS[i][0]
                    r, u = rows_of(n), count_units(kind, i)
                    pe.wait_ge(s_p if kind == "M" else s_w, u + 1)
                    src = prob[:r, u % 3, :] if kind == "M" else esb[:r, u % 2, :]
                    first = key_blocks(n)[0][0]
                    for k, (col, size, _) in enumerate(key_blocks(n)[4 * j:4 * j + 4]):
                        last = pe.transpose(out[:size, P * k:P * k + r], src[:, col - first:col - first + size],
                                            ident[:r, :r])
                last.then_inc(s_tr, 1)

            def weigh(i):
                n, kind, h = UNITS[i]
                r, v = rows_of(n), PV_NO[i]
                if v:
                    pe.wait_ge(s_o, v)
                if kind == "S":
                    pe.wait_ge(s_sv, 80 if n < 5 else 96)
                blocks = key_blocks(n)
                for k, (_, size, tile_) in enumerate(blocks):
                    x = (kind, i, k // 4)
                    if k % 4 == 0:
                        pieces_done(pe, x)
                    vals = v_mla[:size, tile_, 64 * h:64 * h + 64] if kind == "M" else \
                        sv[:size, tile_, 64 * h:64 * h + 64]
                    last = pe.matmul(bank[6][:r, 64 * (v % 8):64 * (v % 8) + 64], pT[:size, W_NO[x] % 4, k % 4, :r],
                                     vals, start=(k == 0), stop=(k == len(blocks) - 1))
                    if k % 4 == 3 or k == len(blocks) - 1:
                        last.then_inc(s_pv, 1)

            for step in range(-12, STEPS):
                m, s = divmod(step + 12, 12)
                if 0 <= step < len(UNITS):
                    scores(step)
                for x in PIECES.get(step - 1, []):
                    if x[0] != "X" and x[2] == 0:
                        weigh(x[1])
                for x in PIECES.get(step, []):
                    transposes(x)
                if m < NTILE:
                    front(m, s)

            pieces_done(pe, ORDER[-1])
            pieces_done(pe, ORDER[-2])
            thirds = ((wt_hi, a_hi), (wt_lo, a_hi), (wt_hi, a_lo))

            def project(out, c, slot, last_pass=None):
                a, b = CHUNKS[c]
                for k in range(KT):
                    for m, (ww, aa) in enumerate(thirds):
                        last = pe.matmul(out[:, :b - a], ww[:, slot, P * k:P * k + P], aa[:, k, a:b],
                                         start=(k == 0 and m == 0), stop=(k == KT - 1 and m == 2))
                return last

            def sum_square(j):
                c = j % 3
                a, b = CHUNKS[c]
                pe.wait_ge(s_sq, 24 + j + 1)
                pe.matmul(bank[5 + c][:, :b - a], ones[:], norm_bufs[1]["sq"][:, j % 2, :b - a],
                          start=(j < 3), stop=(j >= 21)).then_inc(s_ms, 1)

            for d in range(KT):
                pe.wait_ge(s_wlow, d + 1)
                for c in range(3):
                    q = 3 * d + c
                    if d == 0:
                        pe.wait_ge(s_mlo, 2 * c + 2)
                    if q >= 5:
                        pe.wait_ge(s_yr, q - 4)
                    last = project(bank[q % 5], c, d % 6)
                    last.then_inc(s_y, 1)
                    if q >= 2:
                        sum_square(q - 2)
            sum_square(22)
            sum_square(23)

            def up(f, slot, ring_a, ring_b, tile_no, ring_down=None, first=False):
                for n in range(6):
                    branch, c = divmod(n, 3)
                    if c == 0:
                        pe.wait_ge(s_wlow, tile_no + branch + 1)
                    if first and branch == 0:
                        pe.wait_ge(s_h, 24 + 8 * (c + 1))
                    if branch == 0 and not (first and c < 2):
                        pe.wait_ge(s_ac, 3 * f + c - 1)
                    if branch == 1 and not (first and c < 2):
                        pe.wait_ge(s_u, 3 * f + c - 1)
                    last = project(bank[2 * branch + (3 * slot + c) % 2], c, ring_b if branch else ring_a)
                    last.then_inc(s_up, 1)
                    if ring_down is not None:
                        down(f - 1, 1 - slot, ring_down, tile_no + 2, n, first=first)

            def down(f, slot, ring, tile_no, n, first=False, very_first=False):
                if n == 0:
                    pe.wait_ge(s_wlow, tile_no + 1)
                    pe.wait_ge(s_ul, 3 * f + 3)
                for q in range(4 * n, 4 * n + 4):
                    d, c = divmod(q, 3)
                    a, b = CHUNKS[c]
                    if not (isinstance(f, int) and f == 0 and q < 4):
                        pe.wait_ge(s_dr, 24 * f + q - 3)
                    for m, (ww, uu) in enumerate(((wt_hi, u_hi), (wt_lo, u_hi), (wt_hi, u_lo))):
                        last = pe.matmul(bank[4 + q % 4][:, :b - a], ww[:, ring, P * d:P * d + P], uu[:, slot, a:b],
                                         start=(m == 0), stop=(m == 2))
                    last.then_inc(s_dn, 1)

            pe.wait_ge(s_yr, 24)
            pe.wait_ge(s_ln, 6)
            up(0, 0, 2, 3, 8, first=True)
            up(1, 1, 4, 5, 10, ring_down=0)
            up(2, 0, 1, 2, 13, ring_down=3)
            with pe.Fori(1, NF // 2 - 1) as i:
                up(2 * i + 1, 1, 4, 5, 6 * i + 10, ring_down=0)
                up(2 * i + 2, 0, 1, 2, 6 * i + 13, ring_down=3)
            up(21, 1, 4, 5, 70, ring_down=0)
            for n in range(6):
                down(21, 1, 1, 73, n)

            pe.wait_ge(s_dr, 24 * NF)
            pe.wait_ge(s_co, NF)
            pe.transpose(bank[7][0:88, 0:P], conv_out[:].rearrange("p j f -> p (j f)"), ident[:]).then_inc(s_cvt, 1)
            for t in range(NTILE):
                r = ROWS[t]
                if t >= 2:
                    pe.wait_ge(s_fy, t - 1)
                for k in range(KT):
                    last = pe.transpose(bank[2 * (t % 2) + k // 4][:r, P * (k % 4):P * (k % 4) + P],
                                        res[:, k, P * t:P * t + r], ident[:])
                last.then_inc(s_ft, 1)


def make(nc, outs):
    I = {n: nc.dram_tensor(f"in_{n}", s, F32, kind="ExternalInput").ap() for n, s in {**INS, **TABLES}.items()}
    O = {n: nc.dram_tensor(f"out_{n}", s, F32, kind="ExternalOutput").ap() for n, s in outs}
    build(nc, I, O)


def kernel(**inputs):
    import concourse.bacc as bacc
    from concourse.bass_utils import run_bass_kernel_spmd

    nc = bacc.Bacc("TRN2", target_bir_lowering=False, num_devices=1)
    make(nc, OUTS)
    arrays = {f"in_{n}": np.ascontiguousarray(inputs[n]).reshape(s) for n, s in INS.items()}
    arrays.update({f"in_{n}": a for n, a in tables().items()})
    r = run_bass_kernel_spmd(nc, [arrays], core_ids=[0])
    return tuple(r.results[0][f"out_{n}"] for n, _ in OUTS)
```

```python
from contextlib import ExitStack

import numpy as np

import concourse.bass as bass
from concourse import mybir

F32 = mybir.dt.float32
F32R = mybir.dt.float32r
ALU = mybir.AluOpType
ACT = mybir.ActivationFunctionType
AX = mybir.AxisListType.X

P = 128
D = 1024
KT = D // P
LP, LS = 1024, 64
T = LP + LS
PAST = 512
NTILE = 9
ROWS = [P] * 8 + [LS]
CHUNKS = [(0, 364), (364, 726), (726, 1088)]
CW = 364
H_MLA, NOPE, ROPE, HV = 8, 64, 32, 64
QD = NOPE + ROPE
QR, KVR = 384, 256
H_RET, H_SB, DH = 4, 4, 64
IN_COLS = 2464
ZG = 308
NZG = IN_COLS // ZG
O_ZQ, O_KV, O_KR, O_RQ, O_RK, O_RV, O_RG, O_SQ, O_SK, O_SV = 0, 384, 640, 672, 928, 1184, 1440, 1696, 1952, 2208
FF = 2816
NF = FF // P
EPS = 1e-6
NEG = -1e30
RAW_SLOTS, WT_SLOTS = 3, 6
N_TAB = 11
AG = 512
NORM_RUNS = ([(0, 128), (128, 364), (364, 726), (726, 1088)], CHUNKS)
NH = (0, KT * 4)
ADA_A, ADA_G = 4, 12
MLA_SCALE = float(QD) ** -0.5
SB_SCALE = float(DH) ** -0.5


def segments(c):
    return split_run(*CHUNKS[c])


def split_run(a, b):
    return [(a, b, 0)] if b <= LP else [(a, LP, 0), (LP, b, 1)]


def chunk_of(t, runs=CHUNKS):
    end = min(P * (t + 1), T)
    return next(c for c, (a, b) in enumerate(runs) if end <= b)


def tables():
    out = {}
    pos = np.arange(T, dtype=np.float64)
    pos[LP:] = PAST + np.arange(LS)
    for name, d in (("rope64", DH), ("rope32", ROPE)):
        inv = (10000.0 ** (-np.arange(0, d, 2, dtype=np.float32) / np.float32(d))).astype(np.float32)
        ang = (pos.astype(np.float32)[:, None] * inv[None, :]).astype(np.float64)
        cos, sin = np.cos(ang), np.sin(ang)
        tab = np.concatenate([cos, cos, -sin, sin], axis=1)
        pad = np.zeros((NTILE * P, 2 * d), np.float32)
        pad[:T] = tab
        out[name] = pad.reshape(NTILE, P, 2 * d).transpose(1, 0, 2).reshape(P, NTILE * 2 * d).copy()
    lg = np.log(1.0 - 2.0 ** (-5.0 - np.arange(H_RET, dtype=np.float32))).astype(np.float64)
    i = np.arange(P)
    rel = i[None, :] - i[:, None]
    dec = np.where(rel[:, None, :] >= 0, np.exp(lg[None, :, None] * np.maximum(rel, 0)[:, None, :]), 0.0)
    out["decayT"] = dec.reshape(P, H_RET * P).astype(np.float32)
    qd = np.zeros((P, 2, P))
    gam = np.zeros((P, 2, 2, P))
    for h in range(H_RET):
        rows = slice(64 * (h % 2), 64 * (h % 2) + 64)
        qd[rows, h // 2, :] = np.exp(lg[h] * (i + 1.0)) * DH ** -0.5
        for n, length in enumerate((P, LS)):
            gam[rows, n, h // 2, :] = np.exp(lg[h] * length)
    out["q_decayT"] = qd.reshape(P, 2 * P).astype(np.float32)
    out["state_decay"] = gam.reshape(P, 4 * P).astype(np.float32)
    kd = np.zeros((P, 2, H_RET))
    for n, length in enumerate((P, LS)):
        kd[:length, n, :] = np.exp(lg[None, :] * (length - 1.0 - i[:length, None]))
    out["k_decay"] = kd.reshape(P, 2 * H_RET).astype(np.float32)
    out["ident"] = np.eye(P, dtype=np.float32)
    out["causal"] = np.where(i[None, :] < i[:, None], 0.0, NEG).astype(np.float32)
    return out


TABLES = {"rope64": (P, NTILE * 128), "rope32": (P, NTILE * 64), "decayT": (P, 512), "q_decayT": (P, 256),
          "state_decay": (P, 512), "k_decay": (P, 8), "ident": (P, P), "causal": (P, P)}
INS = {"x_prompt": (LP, D), "x_sample": (LS, D), "c_prompt": (8, P), "c_sample": (8, P),
       "cache_mla_latent": (PAST, KVR), "cache_mla_krope": (PAST, ROPE), "cache_sb_k": (PAST, 256),
       "cache_sb_v": (PAST, 256), "state_ret": (256, 64), "state_ffn_conv": (44, P), "w_in": (D, IN_COLS),
       "g_q_norm": (3, P), "w_uq": (QR, 768), "g_kv_norm": (1, KVR), "w_ukv": (KVR, 1024), "g_ret_norm": (1, 256),
       "w_o": (D, D), "w_up": (D, 2 * FF), "conv_w": (66, P), "conv_b": (22, P), "w_down": (FF, D),
       "g_norm1": (8, P), "g_norm2": (8, P), "w_ada": (D, 6 * D), "b_ada": (48, P), "g_final": (1, D)}
OUTS = [("y_prompt", (1, LP, D)), ("y_sample", (1, LS, D)),
        ("p_mla_latent", (1, 1, LP, KVR)), ("p_mla_krope", (1, 1, LP, ROPE)),
        ("p_sb_k", (1, 1, LP, 4, 64)), ("p_sb_v", (1, 1, LP, 4, 64)),
        ("p_ret_state", (1, 1, 4, 64, 64)), ("p_ffn_conv", (1, 1, 2, FF)),
        ("s_mla_latent", (1, 1, LS, KVR)), ("s_mla_krope", (1, 1, LS, ROPE)),
        ("s_sb_k", (1, 1, LS, 4, 64)), ("s_sb_v", (1, 1, LS, 4, 64)),
        ("s_ret_state", (1, 1, 4, 64, 64)), ("s_ffn_conv", (1, 1, 2, FF))]
VEC_A = [("b_ada", 48, 0), ("g_norm1", 8, 48), ("g_norm2", 8, 56), ("c_prompt", 8, 64), ("c_sample", 8, 72),
         ("g_q_norm", 3, 80)]
N_A = 83
VEC_B = [("conv_w", 66, 0), ("conv_b", 22, 66)]
N_B = 88
N_C = 44


SEQ = [8] + list(range(8))
KINDS = [("S", 0), ("M", 0), ("M", 1), ("S", 1), ("M", 2), ("M", 3), ("S", 2), ("M", 4), ("M", 5), ("S", 3),
         ("M", 6), ("M", 7)]
UNITS = [(n, kind, h) for n in range(NTILE) for kind, h in KINDS]
FF_SPARE = KT * T - (4 * T + 2 * (T + 4) + T + 2 + 2 * CW + 8 + 4 * NF + 9)
T_LAG = {"M": 2, "S": 5}
EARLY_SPLIT = 103
MIX_STEP = 17


PROJ = [(d, c) for d in range(KT - 2) for c in range(3)] + [(d, c) for c in range(3) for d in (KT - 2, KT - 1)]
FIN_SLOTS = 3


def down_order(f, q):
    return (q % KT, q // KT) if isinstance(f, int) and f == NF - 1 else divmod(q, 3)


PROJ_DONE = [PROJ.index((KT - 1, c)) + 1 for c in range(3)]




def rows_of(n):
    return ROWS[SEQ[n]]


def key_col(n):
    return P * SEQ[n]


def key_blocks(n):
    if n == 0:
        return [(512 + P * j, P, 4 + j) for j in range(4)] + [(LP, LS, 8)]
    return [(P * j, P, j) for j in range(SEQ[n] + 1)]


def n_keys(n):
    return sum(size for _, size, _ in key_blocks(n))


def count_units(kind, i):
    return sum(k == kind for _, k, _ in UNITS[:i])


def plan_pieces():
    steps = {}
    for step in range(12 * (NTILE - 1) + MIX_STEP + 1):
        out = []
        for kind in "MS":
            i = step - T_LAG[kind]
            if 0 <= i < len(UNITS) and UNITS[i][1] == kind:
                nb = len(key_blocks(UNITS[i][0]))
                out += [(kind, i, j) for j in range((nb + 3) // 4)]
        n, rest = divmod(step - MIX_STEP, 12)
        if rest == 0 and 0 <= n < NTILE:
            out += [("X", n, 0), ("X", n, 1)]
        steps[step] = out
    return steps


PIECES = plan_pieces()
STEPS = len(PIECES)
ORDER = [x for step in range(STEPS) for x in PIECES[step]]
PIECE_NO = {x: q for q, x in enumerate(ORDER)}
W_NO = {x: w for w, x in enumerate(x for x in ORDER if x[0] != "X")}
N_PIECES = len(W_NO)
PV_ORDER = [x[1] for x in ORDER if x[0] != "X" and x[2] == 0]
PV_NO = {i: v for v, i in enumerate(PV_ORDER)}
READ_A = [0, 1, 2, 3, 4, 5, 7, 8, 9]
READ_D = [0, 2, 3, 4, 6, 7, 9, 10, 11]


def read_a(m, s):
    return len(READ_A) * m + sum(x < s for x in READ_A)


def read_d(m, s):
    return len(READ_D) * m + sum(x < s for x in READ_D)


def build(nc, I, O, stop_after=None):
    ctx = ExitStack()
    z_dram = nc.dram_tensor("z_scratch", (T, IN_COLS), F32, kind="Internal").ap()
    xT_dram = nc.dram_tensor("xT_scratch", (P, KT, T), F32, kind="Internal").ap()
    mod_dram = nc.dram_tensor("mod_scratch", (4, AG * (ADA_G - ADA_A)), F32, kind="Internal").ap()
    mixT_dram = nc.dram_tensor("mixT_scratch", (P, KT, T), F32, kind="Internal").ap()
    with ctx:
        def sem(name):
            return ctx.enter_context(nc.semaphore(name))

        def sbuf(scope):
            return lambda name, shape, dt=F32: scope.enter_context(nc.sbuf_tensor(name, [P, *shape], dt))

        keep = sbuf(ctx)
        psum = ctx.enter_context(nc.psum_tensor("psum", [P, 8, 512], F32))
        bank = [psum[:, i, :] for i in range(8)]

        ident = keep("ident_sb", [P])
        ones = keep("ones", [P])
        vec_a = keep("vec_a", [N_A])
        vec_b = keep("vec_b", [N_B])
        vec_c = keep("vec_c", [N_C])
        mod = keep("mod", [48, 2])
        scale_n = keep("scale_n", [2, KT, 2])
        eps = keep("eps", [1])
        mod_rows = keep("mod_rows", [P])

        early = ExitStack()
        s1 = sbuf(early)
        xT = s1("xT", [KT, T])
        rb = s1("rb", [T])
        sq_hn = s1("sq_hn", [5 * CW])
        sums_x = s1("sums_x", [NTILE])
        rstd_x = s1("rstd_x", [NTILE])
        h_hi = s1("h_hi", [KT, T], F32R)
        h_lo = s1("h_lo", [KT, T], F32R)
        vec_in = s1("vec_in", [3, P])
        silu_c = s1("silu_c", [2, KT])
        silu_e = s1("silu_e", [2, KT])
        c_parts = s1("c_parts", [KT, 4], F32R)
        ada_raw = s1("ada_raw", [4, 2, AG])
        ada_hi = s1("ada_hi", [4, AG], F32R)
        ada_lo = s1("ada_lo", [4, AG], F32R)
        ada_row = s1("ada_row", [2, AG])
        z_out = s1("z_out", [3, ZG])
        x_scope = ExitStack()
        x_in = sbuf(x_scope)("x_in", [NTILE, D])
        x_scope.close()
        w_raw = s1("w_raw", [2, 4, ZG])
        w_hi = s1("w_hi", [2, KT, ZG], F32R)
        w_lo = s1("w_lo", [2, KT, ZG], F32R)
        early.close()

        mid = ExitStack()
        s3 = sbuf(mid)
        w_uq = s3("w_uq_sb", [3, 768])
        w_uk = s3("w_uk", [2, 512])
        w_uv = s3("w_uv", [2, 512])
        decayT = s3("decayT_sb", [H_RET, P])
        q_decayT = s3("q_decayT_sb", [2, P])
        state_decay = s3("state_decay_sb", [2, 2, P])
        k_decay = s3("k_decay_sb", [2, H_RET])
        g_kv = s3("g_kv_sb", [KVR])
        g_ret = s3("g_ret_sb", [256])
        cache_scope = ExitStack()
        s_c3 = sbuf(cache_scope)
        c_lat = s_c3("c_lat", [4, KVR])
        c_sk = s_c3("c_sk", [4, 256])
        c_kr = s_c3("c_kr", [4, ROPE])
        cache_scope.close()
        qtok = s3("qtok", [768])
        att = s3("att", [H_RET, P])
        rkT = s3("rkT", [2, P])
        rqdT = s3("rqdT", [2, P])
        rqT = s3("rqT", [2, 2, P])
        z_in = s3("z_in", [2, IN_COLS])
        rope_t = s3("rope_t", [2, 192])
        zqn = s3("zqn", [QR])
        lat = s3("lat", [KVR])
        latT = s3("latT", [2, P])
        qnT = s3("qnT", [3, P])
        junk = s3("junk", [QR + KVR])
        sums = s3("sums", [2])
        rs = s3("rs", [2])
        rope_a = s3("rope_a", [512])
        rope_b = s3("rope_b", [512])
        q_a = s3("q_a", [4, ROPE])
        q_b = s3("q_b", [4, ROPE])
        kr = s3("kr", [ROPE])
        rqk = s3("rqk", [8, DH])
        kd = s3("kd", [H_RET, DH])
        state = s3("state", [2, 2, P])
        eg = s3("eg", [256])
        kT = s3("kT", [H_MLA, T])
        v_mla = s3("v_mla", [NTILE, 512])
        skT = s3("skT", [2, T])
        sv = s3("sv", [NTILE, 256])
        qT = s3("qT", [2, H_MLA, P])
        sqT = s3("sqT", [2, 2, P])
        prob = s3("prob", [3, 1024])
        zsb = s3("zsb", [2, 1024])
        esb = s3("esb", [2, 1024])
        pT = s3("pT", [4, 4, P])
        mixtok = s3("mixtok", [2, D])
        mixT = s3("mixT", [KT, P])
        causal = s3("causal_sb", [P])
        zero = s3("zero", [1])
        gate = s3("gate", [256])
        oc = s3("oc", [H_RET, DH])
        oc2 = s3("oc2", [H_RET, DH])
        stat = s3("stat", [4, H_RET])
        maxes = s3("maxes", [2, 2])
        rowsum = s3("rowsum", [4, 2])
        mid.close()
        late = ExitStack()
        s4 = sbuf(late)
        mix_scope = ExitStack()
        mix_raw = sbuf(mix_scope)("mix_raw", [KT, T])
        mix_scope.close()
        u_hi = s4("u_hi", [2, T], F32R)
        u_lo = s4("u_lo", [2, T], F32R)
        a_ext = s4("a_ext", [2, T + 4])
        conv = s4("conv", [T + 2])
        u_val = s4("u_val", [2, CW])
        f_vec = s4("f_vec", [2, 4])
        conv_out = s4("conv_out", [4, NF])
        fin = s4("final_stats", [FIN_SLOTS, 3])
        spare = s4("spare", [FF_SPARE])
        wt_raw = s4("wt_raw", [RAW_SLOTS, KT * P])
        wt_parts = s4("wt_parts", [WT_SLOTS, 2, KT * P], F32R)
        wt_hi, wt_lo = wt_parts[:, :, 0, :], wt_parts[:, :, 1, :]
        a_hi = s4("act_hi", [KT, T], F32R)
        a_lo = s4("act_lo", [KT, T], F32R)
        res = s4("residual", [KT, T])
        late.close()
        sq_x = sq_hn[:, 0:D]
        diag = sq_hn[:, D:D + 3 * P].rearrange("p (a n) -> p a n", a=3)
        norm_bufs = [dict(x=xT, hi=h_hi, lo=h_lo, rb=rb, hn=sq_hn[:, 0:3 * CW].rearrange("p (a n) -> p a n", a=3)),
                     dict(x=res, hi=a_hi, lo=a_lo, rb=conv,
                          sq=a_ext[:, 0, 0:2 * CW].rearrange("p (a n) -> p a n", a=2),
                          hn=a_ext[:, 1, 0:3 * CW].rearrange("p (a n) -> p a n", a=3))]
        g_fin = conv[:, 0:D]
        y_out = wt_raw
        fin_sq = a_ext[:, :, 0:D]
        conv_rows = u_val[:, 0, 0:P]
        c_latT = zsb[:, :, :].rearrange("p a (b c) -> p a b c", b=2)[:, :, 0, :]

        s_id = sem("identity_loaded")
        s_const = sem("vectors_loaded")
        s_x = [sem(f"x_loaded_{i}") for i in range(NTILE)]
        s_set = sem("memsets_done")
        s_xt = sem("x_transposed")
        s_xeD = sem("xT_first_half_written")
        s_xeA = sem("xT_second_half_written")
        s_vt = sem("vectors_transposed")
        s_vec = sem("vectors_written")
        s_silu = sem("silu_steps")
        s_siluv = sem("silu_ready")
        s_chi = sem("silu_high_written")
        s_cpl = sem("silu_low_written")
        s_ada = [sem(f"ada_loaded_{i}") for i in range(4)]
        s_ahi = sem("ada_hi_written")
        s_alo = sem("ada_lo_written")
        s_adamm = sem("ada_rows_multiplied")
        s_row = sem("ada_row_copied")
        s_rowst = sem("ada_row_stored")
        s_modl = sem("mod_rows_loaded")
        s_modt = sem("mod_rows_transposed")
        s_mod = sem("mod_written")
        s_scale = sem("norm_scales_written")
        s_rs1 = sem("x_rstd_ready")
        s_dg = sem("diagonals_written")
        s_sq = sem("squares_written")
        s_ms = sem("squares_summed")
        s_ln = sem("log_written")
        s_rb = sem("rstd_written")
        s_hn = sem("normed_written")
        s_hhi = sem("h_hi_written")
        s_h = sem("h_lo_written")
        s_raw = [sem(f"w_raw_loaded_{i}") for i in range(2)]
        s_whi = sem("w_hi_written")
        s_wlo = sem("w_lo_written")
        s_z = sem("z_multiplied")
        s_zc = sem("z_copied")
        s_zst = [sem(f"z_stored_{i}") for i in range(3)]

        s_xst = sem("xT_stored")
        s_tab = sem("mixer_constants_loaded")
        s_cau = sem("causal_mask_loaded")
        s_cache = sem("caches_loaded")
        s_init = sem("mixer_memsets_done")
        s_sv = sem("values_loaded")
        s_wuq = sem("w_uq_scaled")
        s_zi = [sem(f"z_tile_loaded_{i}") for i in range(2)]
        s_cT = sem("cache_stage_multiplied")
        s_cA = sem("cache_copied_by_scalar")
        s_cD = sem("cache_copied_by_vector")
        s_rs = sem("latent_rstd_ready")
        s_eg = sem("gate_exp_ready")
        s_lat = sem("latents_normed")
        s_latst = sem("latents_stored")
        s_kr = sem("k_rope_ready")
        s_rot = sem("retention_qk_ready")
        s_g1 = sem("gate_denominator_ready")
        s_g2 = sem("gate_reciprocal_ready")
        s_gate = sem("gate_ready")
        s_fp = sem("front_step_multiplied")
        s_fA = sem("front_bank_read_by_scalar")
        s_fD = sem("front_bank_read_by_vector")
        s_var = sem("group_variance_ready")
        s_rr = sem("group_rstd_ready")
        s_ret = sem("retention_written")
        s_sc = sem("scores_multiplied")
        s_mx = sem("maximum_ready")
        s_p = sem("softmax_exp_written")
        s_zsb = sem("stick_logits_copied")
        s_l = sem("stick_log_written")
        s_c = sem("stick_sums_written")
        s_wa = sem("stick_exponents_written")
        s_w = sem("stick_weights_written")
        s_tr = sem("piece_transposed")
        s_pt = sem("piece_copied")
        s_pv = sem("piece_weighed")
        s_o = sem("head_output_written")
        s_mst = sem("mixT_stored")
        s_out = sem("outputs_stored")
        s_res = sem("residual_loaded")
        s_mx4 = sem("mix_rows_loaded")
        s_mhi = sem("mix_hi_written")
        s_mlo = sem("mix_lo_written")
        s_wl = [sem(f"weight_tile_loaded_{i}") for i in range(RAW_SLOTS)]
        s_wh = sem("weight_hi_written")
        s_wlow = sem("weight_lo_written")
        s_y = sem("projection_multiplied")
        s_yr = sem("residual_updated")
        s_up = sem("ffn_chunk_multiplied")
        s_ac = sem("ffn_a_copied")
        s_fv = sem("ffn_vectors_copied")
        s_cv = sem("conv_first_tap")
        s_c1 = sem("conv_second_tap")
        s_cs = sem("conv_summed")
        s_sl = sem("silu_written")
        s_u = sem("u_written")
        s_uh = sem("u_hi_written")
        s_ul = sem("u_lo_written")
        s_co = sem("conv_state_kept")
        s_dn = sem("down_multiplied")
        s_dr = sem("down_added")
        s_cvt = sem("conv_state_transposed")
        s_cvc = sem("conv_state_copied")
        s_ft = sem("final_transposed")
        s_fs = sem("final_rstd_ready")
        s_fy = sem("final_written")
        s_yst = [sem(f"final_stored_{i}") for i in range(FIN_SLOTS)]
        s_gf = sem("final_gain_loaded")
        s_cvi = sem("conv_edges_cleared")
        s_chA = sem("scalar_chain")
        s_chD = sem("vector_chain")
        s_chP = sem("pool_chain")

        def score_bank(i, width):
            return psum[:, 2 * (i % 2):2 * (i % 2) + 2, :].rearrange("p a b -> p (a b)")[:, :width]

        def pieces_done(eng, x):
            eng.wait_ge(s_pt, PIECE_NO[x] + 1)

        class Chain:

            def __init__(self, eng, s):
                self.eng, self.s, self.n = eng, s, 0

            def link(self, ins):
                self.n += 1
                ins.then_inc(self.s, 1)
                self.eng.wait_ge(self.s, self.n)

        w_in_v = I["w_in"].rearrange("(k p) n -> p k n", p=P)
        w_ada_v = I["w_ada"].rearrange("(k p) n -> p k n", p=P)
        n_const = len(VEC_A) + len(VEC_B) + 1

        def x_rows(t):
            return I["x_prompt"][P * t:P * t + P, :] if t < 8 else I["x_sample"]

        block = ctx.enter_context(nc.Block())

        @block.sync
        def _(sp):
            sp.dma_start(ident[:], I["ident"]).then_inc(s_id, 16)
            for t in range(4):
                sp.dma_start(x_in[:ROWS[t], t, :], x_rows(t)).then_inc(s_x[t], 16)
            for i, vecs in enumerate((VEC_A, VEC_B, [("state_ffn_conv", 44, 0)])):
                for name, rows, at in vecs:
                    sp.dma_start(vec_in[at:at + rows, i, :], I[name]).then_inc(s_const, 16)

            for t in range(4, NTILE):
                sp.dma_start(x_in[:ROWS[t], t, :], x_rows(t)).then_inc(s_x[t], 16)

            def load_ada(g, first=False):
                for q in range(4):
                    if not first:
                        sp.wait_ge(s_alo, 8 * g + 2 * q - 6)
                    sp.dma_start(ada_raw[:, q], w_ada_v[:, 2 * q:2 * q + 2, bass.ds(g * AG, AG)])\
                        .then_inc(s_ada[q], 16)

            def load_w_in(g, half):
                sp.dma_start(w_raw[:, half], w_in_v[:, 4 * half:4 * half + 4, bass.ds(g * ZG, ZG)])\
                    .then_inc(s_raw[half], 16)

            for g in range(ADA_A):
                load_ada(g, first=(g == 0))
            sp.wait_ge(s_xt, 2 * NTILE)
            sp.wait_ge(s_sq, NTILE)
            load_w_in(0, 0)
            load_w_in(0, 1)
            load_ada(ADA_A)
            sp.wait_ge(s_xeD, NTILE)
            sp.wait_ge(s_xeA, NTILE)

            def group_loads(g):
                for half in range(2):
                    sp.wait_ge(s_wlo, 2 * g + half + 1)
                    load_w_in(g + 1, half)
                load_ada(g + 1 + ADA_A)

            group_loads(0)
            sp.dma_start(xT_dram, xT[:]).then_inc(s_xst, 16)
            with sp.Fori(1, NZG - 1) as g:
                group_loads(g)

            sp.wait_ge(s_xst, 16)
            sp.wait_ge(s_h, NH[1])
            for name, tile_ in (("decayT", decayT), ("q_decayT", q_decayT), ("state_decay", state_decay),
                                ("k_decay", k_decay)):
                flat = tile_[:]
                if len(flat.shape) == 3:
                    flat = flat.rearrange("p a b -> p (a b)")
                elif len(flat.shape) == 4:
                    flat = flat.rearrange("p a b c -> p (a b c)")
                sp.dma_start(flat, I[name]).then_inc(s_tab, 16)
            sp.dma_start(g_kv[:], I["g_kv_norm"].broadcast_to([P, KVR])).then_inc(s_tab, 16)
            sp.dma_start(g_ret[:], I["g_ret_norm"].broadcast_to([P, 256])).then_inc(s_tab, 16)
            sp.dma_start(w_uq[:], I["w_uq"].rearrange("(k p) n -> p k n", p=P)).then_inc(s_tab, 16)
            for part, lo in ((w_uk, 0), (w_uv, NOPE)):
                for k in range(2):
                    sp.dma_start(part[:, k, :].rearrange("p (h c) -> p h c", h=8),
                                 I["w_ukv"][P * k:P * k + P, :].rearrange("p (h c) -> p h c", h=8)[:, :, lo:lo + 64])\
                        .then_inc(s_tab, 16)
            sp.dma_start(c_lat[:], I["cache_mla_latent"].rearrange("(j p) c -> p j c", p=P)).then_inc(s_cache, 16)
            sp.dma_start(c_sk[:], I["cache_sb_k"].rearrange("(j p) c -> p j c", p=P)).then_inc(s_cache, 16)
            sp.dma_start(c_kr[:], I["cache_mla_krope"].rearrange("(j p) c -> p j c", p=P)).then_inc(s_cache, 16)

            sp.wait_ge(s_rowst, 16 * (ADA_G - ADA_A))
            sp.dma_start(mod_rows[:], mod_dram.rearrange("r (j p) -> (r j) p", p=P)).then_inc(s_modl, 16)
            sp.wait_ge(s_z, 9 * NZG)
            sp.wait_ge(s_adamm, 8 * ADA_G)
            for i in range(3):
                sp.wait_ge(s_zst[i], 16 * 3 * NZG)

            def load_z(m):
                r, t = rows_of(m), SEQ[m]
                sp.dma_start(z_in[:r, m % 2, :], z_dram[P * t:P * t + r, :]).then_inc(s_zi[m % 2], 16)
                sp.dma_start(rope_t[:, m % 2, 0:128], I["rope64"][:, 128 * t:128 * t + 128]).then_inc(s_zi[m % 2], 16)
                sp.dma_start(rope_t[:, m % 2, 128:192], I["rope32"][:, 64 * t:64 * t + 64]).then_inc(s_zi[m % 2], 16)

            def diagonal(of, n):
                heads = of.rearrange("(q two) d e -> two d q e", two=2)
                for two in range(2):
                    lo = 64 * two
                    yield state[lo:lo + 64, n, :, lo:lo + 64], heads[two]

            load_z(0)
            sp.dma_start(causal[:], I["causal"]).then_inc(s_cau, 16)
            load_z(1)
            sp.dma_start(sv[:, 4:8, :], I["cache_sb_v"].rearrange("(j p) c -> p j c", p=P)).then_inc(s_sv, 16)
            sp.dma_start(sv[:LS, 8, :], z_dram[LP:T, O_SV:O_SV + 256]).then_inc(s_sv, 16)
            sp.dma_start(sv[:, 0:4, :], z_dram[0:512, O_SV:O_SV + 256].rearrange("(j p) c -> p j c", p=P))\
                .then_inc(s_sv, 16)
            sp.wait_ge(s_init, 1)
            for part, heads in diagonal(I["state_ret"].rearrange("(h d) e -> h d e", h=4), 0):
                sp.dma_start(part, heads).then_inc(s_sv, 16)
            for name, at in (("sb_k", O_SK), ("sb_v", O_SV)):
                for who, lo, hi in (("p", 0, LP), ("s", LP, T)):
                    sp.dma_start(O[f"{who}_{name}"].rearrange("a b t h d -> (a b t) (h d)"),
                                 z_dram[lo:hi, at:at + 256]).then_inc(s_out, 16)

            def store_latent(m):
                who, a, r = ("s", 0, LS) if m == 0 else ("p", P * (m - 1), P)
                sp.wait_ge(s_lat, m + 1)
                sp.dma_start(O[f"{who}_mla_latent"].rearrange("a b t c -> (a b t) c")[a:a + r, :], lat[:r, :])\
                    .then_inc(s_latst, 16)
                sp.wait_ge(s_kr, m + 1)
                sp.dma_start(O[f"{who}_mla_krope"].rearrange("a b t c -> (a b t) c")[a:a + r, :], kr[:r, :])\
                    .then_inc(s_latst, 16)

            def store_state(m, name):
                sp.wait_ge(s_fD, read_d(m + 1, 0))
                for part, heads in diagonal(O[name].rearrange("a b h d e -> (a b h) d e"), int(m > 0)):
                    sp.dma_start(heads, part).then_inc(s_out, 16)

            def store_mix(n):
                r, t = rows_of(n), SEQ[n]
                pieces_done(sp, ("X", n, 1))
                sp.dma_start(mixT_dram[:, :, P * t:P * t + r], mixT[:, :, :r]).then_inc(s_mst, 16)

            store_latent(0)
            for n in range(NTILE):
                if n == 0:
                    store_state(0, "s_ret_state")
                if n + 2 < NTILE:
                    sp.wait_ge(s_ret, n + 1)
                    sp.wait_ge(s_gate, n + 1)
                    sp.wait_ge(s_fp, 12 * (n + 1))
                    load_z(n + 2)
                if n + 1 < NTILE:
                    store_latent(n + 1)
                if n == 2:
                    sp.wait_ge(s_o, 12)
                    sp.dma_start(sv[:, 4:8, :], z_dram[512:LP, O_SV:O_SV + 256].rearrange("(j p) c -> p j c", p=P))\
                        .then_inc(s_sv, 16)
                if n:
                    store_mix(n - 1)
            store_state(8, "p_ret_state")
            sp.wait_ge(s_mst, 16 * (NTILE - 1))
            sp.wait_ge(s_latst, 32 * NTILE)
            sp.wait_ge(s_out, 16 * 8)
            sp.wait_ge(s_gate, NTILE)
            sp.wait_ge(s_fp, 12 * NTILE)
            sp.wait_ge(s_fA, read_a(NTILE, 0))
            sp.wait_ge(s_fD, read_d(NTILE, 0))
            for d in range(3):
                sp.dma_start(wt_raw[:, d, :].rearrange("p (k n) -> p k n", k=KT),
                             I["w_o"].rearrange("(k p) n -> p k n", p=P)[:, :, P * d:P * d + P]).then_inc(s_wl[d], 16)
            sp.dma_start(mix_raw[:, :, 0:LP - P], mixT_dram[:, :, 0:LP - P]).then_inc(s_mx4, 16)
            sp.dma_start(mix_raw[:, :, LP:T], mixT_dram[:, :, LP:T]).then_inc(s_mx4, 16)

            w_o_v = I["w_o"].rearrange("(k p) n -> p k n", p=P)
            w_up_v = I["w_up"].rearrange("(k p) n -> p k n", p=P)

            def load_tile(idx, slot, src):
                sp.wait_ge(s_wlow, idx - 2)
                dst = wt_raw[:, slot, :]
                if len(src.shape) == 3:
                    dst = dst.rearrange("p (k n) -> p k n", k=KT)
                sp.dma_start(dst, src).then_inc(s_wl[slot], 16)

            def load_up(idx, slot, f, branch):
                load_tile(idx, slot, w_up_v[:, :, bass.ds(FF * branch + f * P, P)])

            def load_down(idx, slot, f):
                load_tile(idx, slot, I["w_down"][bass.ds(f * P, P), :])

            for d in range(3, 6):
                load_tile(d, d % 3, w_o_v[:, :, P * d:P * d + P])
            sp.wait_ge(s_tr, len(ORDER))
            sp.wait_ge(s_ret, NTILE)
            sp.wait_ge(s_o, len(UNITS))
            sp.dma_start(res[:], xT_dram).then_inc(s_res, 16)
            for d in range(6, KT):
                load_tile(d, d % 3, w_o_v[:, :, P * d:P * d + P])

            load_up(8, 2, 0, 0)
            load_up(9, 0, 0, 1)
            with sp.Fori(0, NF // 2 - 1) as i:
                for half in range(2):
                    at = 10 + 6 * i + 3 * half
                    load_up(at, 1, 2 * i + 1 + half, 0)
                    load_up(at + 1, 2, 2 * i + 1 + half, 1)
                    load_down(at + 2, 0, 2 * i + half)
            load_up(70, 1, 21, 0)
            load_up(71, 2, 21, 1)
            load_down(72, 0, 20)
            load_down(73, 1, 21)

            sp.wait_ge(s_u, 3 * NF)
            sp.dma_start(g_fin, I["g_final"].broadcast_to([P, D])).then_inc(s_gf, 16)

            def store_final(t):
                sp.wait_ge(s_fy, t + 1)
                dst = O["y_prompt"][0, P * t:P * t + P, :] if t < 8 else O["y_sample"][0]
                sp.dma_start(dst, y_out[:ROWS[t], t % FIN_SLOTS, :]).then_inc(s_yst[t % FIN_SLOTS], 16)

            for t in range(NTILE):
                if t == 2:
                    sp.wait_ge(s_cvc, 1)
                    for who, lo in (("p", 0), ("s", 44)):
                        sp.dma_start(O[f"{who}_ffn_conv"].rearrange("a b j (f p) -> (a b j f) p", p=P),
                                     conv_rows[lo:lo + 44, :]).then_inc(s_out, 16)
                store_final(t)
            sp.wait_ge(s_out, 16 * 10)
            for i in range(FIN_SLOTS):
                sp.wait_ge(s_yst[i], 16 * len(range(i, NTILE, FIN_SLOTS)))

        @block.gpsimd
        def _(pool):
            def store_z(g):
                for t in range(NTILE):
                    pool.wait_ge(s_zc, 9 * g + t + 1)
                    pool.dma_start(z_dram[P * t:P * t + ROWS[t], bass.ds(g * ZG, ZG)],
                                   z_out[:ROWS[t], t % 3, :]).then_inc(s_zst[t % 3], 16)

            with pool.Fori(0, NZG) as g:
                store_z(g)

            ch = Chain(pool, s_chP)
            pool.wait_ge(s_tab, 16 * N_TAB)

            def rope(x, heads, half, table, out, r):
                d = 2 * half

                def tab(a, n):
                    return table[:r, a:a + n].unsqueeze(1).broadcast_to([r, heads, n])

                a = rope_a[:r, :heads * d].rearrange("p (h d) -> p h d", h=heads)
                b = rope_b[:r, :heads * d].rearrange("p (h d) -> p h d", h=heads)
                pool.tensor_tensor(a, x, tab(0, d), ALU.mult)
                pool.tensor_tensor(b[:, :, :half], x[:, :, half:], tab(d, half), ALU.mult)
                ch.link(pool.tensor_tensor(b[:, :, half:], x[:, :, :half], tab(d + half, half), ALU.mult))
                return pool.tensor_tensor(out, a, b, ALU.add)

            def front(m, s):
                r, slot = rows_of(m), m % 2
                if s == 0:
                    pool.wait_ge(s_zi[slot], 48 * (m // 2 + 1))
                    if m:
                        pool.wait_ge(s_latst, 32 * m)
                        pool.wait_ge(s_fp, 12 * m)
                    x = z_in[:r, slot, :]
                    ch.link(rope(x[:, O_KR:O_KR + ROPE].unsqueeze(1), 1, 16, rope_t[:, slot, 128:192],
                                 kr[:r, :].unsqueeze(1), r))
                    pool.sem_inc(s_kr, 1)
                    ch.link(rope(x[:, O_RQ:O_RQ + 512].rearrange("p (h d) -> p h d", h=8), 8, 32,
                                 rope_t[:, slot, 0:128], rqk[:r], r))
                    pool.tensor_tensor(kd[:r], rqk[:r, 4:8, :],
                                       k_decay[:r, int(m == 0), :].unsqueeze(2).broadcast_to([r, H_RET, DH]),
                                       ALU.mult).then_inc(s_rot, 1)
                if s == 1:
                    x = z_in[:r, slot, O_RG:O_RG + 256]
                    pool.wait_ge(s_eg, m + 1)
                    if m:
                        pool.wait_ge(s_ret, m)
                    pool.tensor_scalar(eg[:r], eg[:r], 1.0, None, ALU.add).then_inc(s_g1, 1)
                    ch.link(pool.tensor_tensor(gate[:r], x, g_ret[:r], ALU.mult))
                if s == 2:
                    pool.wait_ge(s_g2, m + 1)
                    pool.tensor_tensor(gate[:r], gate[:r], eg[:r], ALU.mult).then_inc(s_gate, 1)

            def stick_exponents(i):
                n = UNITS[i][0]
                r, w, j = rows_of(n), n_keys(n), count_units("S", i)
                pool.wait_ge(s_c, j + 1)
                pool.tensor_tensor(esb[:r, j % 2, :w], zsb[:r, j % 2, :w], esb[:r, j % 2, :w], ALU.subtract)\
                    .then_inc(s_wa, 1)

            for step in range(-12, STEPS):
                m, s = divmod(step + 12, 12)
                if m < NTILE:
                    front(m, s)
                if 0 <= step - 2 < len(UNITS) and UNITS[step - 2][1] == "S":
                    stick_exponents(step - 2)

        @block.scalar
        def _(act):
            act.preload_act_table_set("natural_log_exp_and_others")
            def copy_x(t):
                act.wait_ge(s_xt, 2 * t + 2)
                act.activation(xT[:, 4:8, P * t:P * t + ROWS[t]],
                               bank[2 * (t % 2) + 1][:, :].rearrange("p (k n) -> p k n", k=4)[:, :, :ROWS[t]],
                               ACT.Copy).then_inc(s_xeA, 1)

            def ada_high(g, q):
                act.wait_ge(s_ada[q], 16 * g + 16)
                for k in (2 * q, 2 * q + 1):
                    if not (isinstance(g, int) and g == 0 and k < 4):
                        act.wait_ge(s_adamm, 8 * g + k - 3)
                    act.activation(ada_hi[:, k % 4], ada_raw[:, q, k % 2], ACT.Copy).then_inc(s_ahi, 1)

            def copy_row(g, slot):
                act.wait_ge(s_adamm, 8 * g + 8)
                act.activation(ada_row[0:4, slot], bank[5][0:4, :], ACT.Copy).then_inc(s_row, 1)

            def copy_row_a(g):
                if g >= 2:
                    act.wait_ge(s_modt, g - 1)
                copy_row(g, g % 2)

            def store_row(i, slot):
                if isinstance(i, int) and i == 0:
                    act.wait_ge(s_modt, ADA_A)
                else:
                    act.wait_ge(s_rowst, 16 * i)
                copy_row(i + ADA_A, slot)
                act.wait_ge(s_row, i + ADA_A + 1)
                act.dma_start(mod_dram[:, bass.ds(i * AG, AG)], ada_row[0:4, slot]).then_inc(s_rowst, 16)

            def square(c, k, j):
                a, b = CHUNKS[c]
                if j >= 2:
                    act.wait_ge(s_ms, NTILE + j - 1)
                act.activation(norm_bufs[1]["sq"][:, j % 2, :b - a], res[:, k, a:b], ACT.Square).then_inc(s_sq, 1)

            def rstd(c):
                a, b = CHUNKS[c]
                out = norm_bufs[1]["rb"][:, a:b]
                act.wait_ge(s_ms, NTILE + PROJ_DONE[c])
                act.activation(out, bank[5 + c][:, :b - a], ACT.Ln, bias=eps[:], scale=1.0 / D).then_inc(s_ln, 1)
                act.wait_ge(s_ln, 3 + c + 1)
                act.activation(out, out, ACT.Exp, scale=-0.5).then_inc(s_rb, 1)

            def h_high(n, c):
                for k in range(KT):
                    j = NH[n] + 8 * c + k
                    act.wait_ge(s_hn, j + 1)
                    base = NORM_RUNS[n][c][0]
                    for a, b, which in split_run(*NORM_RUNS[n][c]):
                        last = act.activation(norm_bufs[n]["hi"][:, k, a:b],
                                              norm_bufs[n]["hn"][:, (8 * c + k) % 3, a - base:b - base],
                                              ACT.Identity, bias=mod[:, 24 * n + k, which:which + 1])
                    last.then_inc(s_hhi, 1)

            def split_w_in(g, slot):
                for half in range(2):
                    act.wait_ge(s_raw[half], 16 * (g + 1))
                    act.activation(w_hi[:, slot, 4 * half:4 * half + 4], w_raw[:, half], ACT.Copy)\
                        .then_inc(s_whi, 1)

            def copy_rstd(c):
                at, n = 3 * P * c, sum(ROWS[3 * c:3 * c + 3])
                act.wait_ge(s_ms, 3 * c + 3)
                act.activation(rb[:, at:at + n], bank[6][:, 0:n], ACT.Copy).then_inc(s_rb, 1)

            def x_chunk(c):
                for t in range(3 * c, 3 * c + 3):
                    copy_x(t)
                    if t:
                        act.wait_ge(s_sq, t)
                    act.wait_ge(s_x[t], 16)
                    act.activation(sq_x[:ROWS[t]], x_in[:ROWS[t], t, :], ACT.Square, accum_out=sums_x[:ROWS[t], t:t + 1])\
                        .then_inc(s_sq, 1)
                act.wait_ge(s_sq, 3 * c + 3)
                cols = slice(3 * c, 3 * c + 3)
                act.activation(rstd_x[:, cols], sums_x[:, cols], ACT.Ln, bias=eps[:], scale=1.0 / D).then_inc(s_ln, 1)
                act.wait_ge(s_ln, c + 1)
                act.activation(rstd_x[:, cols], rstd_x[:, cols], ACT.Exp, scale=-0.5).then_inc(s_rs1, 1)
                if c:
                    copy_rstd(c - 1)

            act.wait_ge(s_set, 3)
            x_chunk(0)
            act.wait_ge(s_vec, 1)
            act.activation(silu_e[:], vec_a[:, 64:80].rearrange("p (c k) -> p c k", c=2), ACT.Exp, scale=-1.0)\
                .then_inc(s_silu, 1)
            act.wait_ge(s_siluv, 1)
            act.activation(c_parts[:, :, 0:2], silu_c[:].rearrange("p c k -> p k c"), ACT.Copy).then_inc(s_chi, 1)
            x_chunk(1)
            ada_high(0, 0)
            ada_high(0, 1)
            x_chunk(2)
            ada_high(0, 2)
            ada_high(0, 3)
            copy_rstd(2)
            for g in range(1, ADA_A):
                ada_high(g, 0)
                ada_high(g, 1)
                copy_row_a(g - 1)
                ada_high(g, 2)
                ada_high(g, 3)
            copy_row_a(ADA_A - 1)
            split_w_in(0, 0)
            for c in range(len(NORM_RUNS[0])):
                h_high(0, c)
                if c == 0:
                    ada_high(ADA_A, 0)
                    ada_high(ADA_A, 1)

            def group(g, slot, first=False, last=False):
                if not first:
                    store_row(g - 1, 1 - slot)
                    act.wait_ge(s_z, 9 * g)
                    ada_high(g + ADA_A, 0)
                if not last:
                    split_w_in(g + 1, 1 - slot)
                for q in range(2 if first else 1, 4):
                    ada_high(g + ADA_A, q)

            group(0, 0, first=True)
            group(1, 1)
            with act.Fori(1, 3) as i:
                for s in range(2):
                    group(2 * i + s, s)
            group(NZG - 2, 0)
            group(NZG - 1, 1, last=True)
            store_row(NZG - 1, 1)

            ch = Chain(act, s_chA)
            for i in range(3):
                act.wait_ge(s_zst[i], 16 * 3 * NZG)
            act.wait_ge(s_rowst, 16 * (ADA_G - ADA_A))
            act.wait_ge(s_cT, 1)
            act.activation(c_latT, psum[:, 0:2, :], ACT.Copy).then_inc(s_cA, 1)
            act.wait_ge(s_cT, 3)
            act.activation(kT[64:96, :, 512:1024], bank[4][0:32, :].unsqueeze(1).broadcast_to([32, H_MLA, 512]),
                           ACT.Copy).then_inc(s_cA, 1)

            def cache_copy(s):
                if s < 4:
                    act.wait_ge(s_cT, 4 + s)
                    act.activation(kT[0:64, 2 * s, 512:1024], bank[s][0:64, :], ACT.Copy).then_inc(s_cA, 1)
                elif s == 4:
                    act.wait_ge(s_cT, 8)
                    act.activation(v_mla[:, 4:6, :], psum[:, 4:6, :], ACT.Copy).then_inc(s_cA, 1)

            def front(m, s):
                r, slot = rows_of(m), m % 2
                b7, col = bank[7], key_col(m)
                x = z_in[:r, slot, :]
                if s == 0:
                    act.wait_ge(s_zi[slot], 48 * (m // 2 + 1))
                    if m:
                        act.wait_ge(s_lat, m)
                    act.activation(junk[:r, :QR], x[:, O_ZQ:O_ZQ + QR], ACT.Square, scale=QR ** -0.5,
                                   accum_out=sums[:r, 0:1])
                    ch.link(act.activation(junk[:r, QR:], x[:, O_KV:O_KV + KVR], ACT.Square, scale=KVR ** -0.5,
                                           accum_out=sums[:r, 1:2]))
                    ch.link(act.activation(rs[:r], sums[:r], ACT.Ln, bias=eps[:r]))
                    act.activation(rs[:r], rs[:r], ACT.Exp, scale=-0.5).then_inc(s_rs, 1)
                    if m:
                        act.wait_ge(s_gate, m)
                    act.activation(eg[:r], x[:, O_RG:O_RG + 256], ACT.Exp, scale=-1.0).then_inc(s_eg, 1)
                if s not in READ_A:
                    return
                act.wait_ge(s_fp, 12 * m + s + 1)
                v4 = b7.rearrange("p (k n) -> p k n", k=4)
                if s == 0:
                    last = act.activation(sqT[:, slot, :, :r], v4[:, 0:2, :r], ACT.Copy, scale=SB_SCALE)
                elif s == 1:
                    last = act.activation(qnT[:, :, :r], v4[:, 0:3, :r], ACT.Copy)
                elif s in (2, 3):
                    q4 = b7[:r, 0:384].rearrange("p (h d) -> p h d", h=4)
                    last = act.activation(qtok[:r, 384 * (s - 2):384 * (s - 1)].rearrange("p (h d) -> p h d", h=4)
                                          [:, :, 0:NOPE], q4[:, :, 0:NOPE], ACT.Copy)
                elif s == 4:
                    last = act.activation(latT[:, :, :r], v4[:, 0:2, :r], ACT.Copy)
                elif s == 5:
                    last = act.activation(qT[:QD, slot, 0:4, :r], v4[:QD, :, :r], ACT.Copy)
                elif s == 7:
                    last = act.activation(kT[0:64, 0:H_MLA:2, col:col + r], v4[0:64, :, :r], ACT.Copy)
                elif s == 8:
                    last = act.activation(v_mla[:r, SEQ[m], :], b7[:r, :], ACT.Copy)
                elif s == 9:
                    if m == 0:
                        act.wait_ge(s_init, 3)
                    for a in range(2):
                        act.activation(rqT[64 * a:64 * a + 64, :, a, :r], v4[64 * a:64 * a + 64, 0:2, :r], ACT.Copy,
                                       scale=DH ** -0.5)
                    last = act.activation(rkT[:, :, :r], v4[:, 2:4, :r], ACT.Copy)
                last.then_inc(s_fA, 1)

            def group_rstd(m):
                r = rows_of(m)
                act.wait_ge(s_var, m + 1)
                ch.link(act.activation(stat[:r, 2, :], stat[:r, 1, :], ACT.Ln, bias=eps[:r], scale=1.0 / DH))
                act.activation(stat[:r, 3, :], stat[:r, 2, :], ACT.Exp, scale=-0.5).then_inc(s_rr, 1)

            def softmax_exp(i):
                n = UNITS[i][0]
                r, w, j = rows_of(n), n_keys(n), count_units("M", i)
                act.wait_ge(s_mx, j + 1)
                if j >= 3:
                    before = max(x for x in range(i) if UNITS[x][1] == "M" and count_units("M", x) == j - 3)
                    nb = len(key_blocks(UNITS[before][0]))
                    act.wait_ge(s_tr, PIECE_NO["M", before, (nb + 3) // 4 - 1] + 1)
                if j >= 4:
                    act.wait_ge(s_o, 1 + PV_NO[[x for x in range(i) if UNITS[x][1] == "M"][-4]])
                act.activation(prob[:r, j % 3, :w], score_bank(i, w)[:r], ACT.Exp, bias=maxes[:r, j % 2, 1:2],
                               scale=MLA_SCALE, accum_out=rowsum[:r, j % 4, 0:1]).then_inc(s_p, 1)

            def stick_log(i):
                n = UNITS[i][0]
                r, w, j = rows_of(n), n_keys(n), count_units("S", i)
                e = esb[:r, j % 2, :w]
                act.wait_ge(s_zsb, j + 1)
                if j >= 2:
                    before = [x for x in range(i) if UNITS[x][1] == "S"][-2]
                    nb = len(key_blocks(UNITS[before][0]))
                    act.wait_ge(s_tr, PIECE_NO["S", before, (nb + 3) // 4 - 1] + 1)
                ch.link(act.activation(e, zsb[:r, j % 2, :w], ACT.Abs))
                ch.link(act.activation(e, e, ACT.Exp, scale=-1.0))
                act.activation(e, e, ACT.Ln, bias=1.0).then_inc(s_l, 1)

            def stick_weights(i):
                n = UNITS[i][0]
                r, w, j = rows_of(n), n_keys(n), count_units("S", i)
                act.wait_ge(s_wa, j + 1)
                act.activation(esb[:r, j % 2, :w], esb[:r, j % 2, :w], ACT.Exp).then_inc(s_w, 1)

            def copy_piece(x):
                kind, i, j = x
                q = PIECE_NO[x]
                act.wait_ge(s_tr, q + 1)
                src = bank[4 + q % 2].rearrange("p (k n) -> p k n", k=4)
                if kind == "X":
                    if i and j == 0:
                        act.wait_ge(s_mst, 16 * min(i, NTILE - 1))
                    r = rows_of(i)
                    out = mixT[:, 4 * j:4 * j + 4, :r] if i < NTILE - 1 else mix_raw[:, 4 * j:4 * j + 4, LP - P:LP]
                    act.activation(out, src[:, :, :r], ACT.Copy).then_inc(s_pt, 1)
                    return
                n, wn = UNITS[i][0], W_NO[x]
                r = rows_of(n)
                blocks = key_blocks(n)[4 * j:4 * j + 4]
                if wn >= 4:
                    act.wait_ge(s_pv, wn - 3)
                last = act.activation(pT[:, wn % 4, :len(blocks), :r], src[:, :len(blocks), :r], ACT.Copy)\
                    if blocks[-1][1] == P else None
                if last is None:
                    if len(blocks) > 1:
                        act.activation(pT[:, wn % 4, :len(blocks) - 1, :r], src[:, :len(blocks) - 1, :r], ACT.Copy)
                    last = act.activation(pT[:LS, wn % 4, len(blocks) - 1, :r], src[:LS, len(blocks) - 1, :r], ACT.Copy)
                last.then_inc(s_pt, 1)

            def split_hi(n3, raw, slot, first=False):
                act.wait_ge(s_wl[raw], 16 * n3 + 16)
                if not first:
                    idx = 3 * n3 + raw if isinstance(n3, int) else 16
                    if idx < 14:
                        act.wait_ge(s_y, max(i for i, (d, _) in enumerate(PROJ) if d == idx - 6) + 1)
                    elif idx < 16:
                        act.wait_ge(s_up, idx - 9)
                    elif raw == 0:
                        act.wait_ge(s_dn, 24 * (n3 - 5))
                    else:
                        act.wait_ge(s_up, 6 * (n3 - 4) + 3 * raw)
                act.activation(wt_hi[:, slot], wt_raw[:, raw], ACT.Copy).then_inc(s_wh, 1)

            for step in range(-12, STEPS):
                m, s = divmod(step + 12, 12)
                for lag, kind, do in ((1, "M", softmax_exp), (1, "S", stick_log), (4, "S", stick_weights)):
                    if 0 <= step - lag < len(UNITS) and UNITS[step - lag][1] == kind:
                        do(step - lag)
                for x in PIECES.get(step, []):
                    copy_piece(x)
                if m == 0:
                    cache_copy(s)
                if m < NTILE:
                    front(m, s)
                if step - EARLY_SPLIT in range(3):
                    split_hi(0, step - EARLY_SPLIT, step - EARLY_SPLIT, first=True)
                if s == 0 and 0 < m <= NTILE:
                    group_rstd(m - 1)

            act.wait_ge(s_pv, N_PIECES)
            act.wait_ge(s_mx4, 32)
            pieces_done(act, ORDER[-1])
            for c, (lo, hi) in enumerate(CHUNKS):
                for k in (0, 4):
                    act.activation(a_hi[:, k:k + 4, lo:hi], mix_raw[:, k:k + 4, lo:hi], ACT.Copy).then_inc(s_mhi, 1)
            for idx in range(3, 6):
                split_hi(1, idx % 3, idx, first=True)
            for j, (d, c) in enumerate(PROJ):
                act.wait_ge(s_yr, j + 1)
                if j == 0:
                    act.wait_ge(s_mlo, 6)
                square(c, d, j)
                if c == 2 and d + 6 < 12:
                    split_hi((d + 6) // 3, d % 3, d % 6)
                if j == PROJ_DONE[0] + 1:
                    rstd(0)
                    h_high(1, 0)
            rstd(1)
            h_high(1, 1)
            rstd(2)
            h_high(1, 2)

            act.preload_act_table_set("silu_and_others")
            act.wait_ge(s_h, NH[1] + 24)

            def copy_a(f, slot, first=False):
                for c in range(3):
                    act.wait_ge(s_up, 2 * c + 1 if isinstance(f, int) and f == 0 else 6 * f + c + 1)
                    if c == 0 and not first:
                        act.wait_ge(s_cs, f - 1)
                        act.wait_ge(s_co, f - 1)
                    for a, b, which in segments(c):
                        at = a + 2 + 2 * which
                        last = act.activation(a_ext[:, slot, at:at + b - a],
                                              bank[(3 * slot + c) % 2][:, a - CHUNKS[c][0]:b - CHUNKS[c][0]], ACT.Copy)
                    last.then_inc(s_ac, 1)

            def first_tap(f, slot, first=False):
                act.wait_ge(s_ac, 3 * f + 3)
                act.wait_ge(s_fv, f + 1)
                if not first:
                    act.wait_ge(s_u, 3 * f)
                act.activation(conv[:], a_ext[:, slot, 2:T + 4], ACT.Identity, bias=f_vec[:, slot, 3:4],
                               scale=f_vec[:, slot, 2:3]).then_inc(s_cv, 1)

            def silu(f):
                act.wait_ge(s_cs, f + 1)
                act.activation(conv[:], conv[:], ACT.Silu).then_inc(s_sl, 1)

            def u_high(f, slot, c, first=False):
                act.wait_ge(s_u, 3 * f + c + 1)
                if not first and c == 0:
                    act.wait_ge(s_dn, 24 * (f - 1))
                a, b = CHUNKS[c]
                act.activation(u_hi[:, slot, a:b], u_val[:, c % 2, :b - a], ACT.Copy).then_inc(s_uh, 1)

            def ffn_tile(f, slot, tiles, first=False, early=False):
                for n3, raw, ring in tiles[:1]:
                    split_hi(n3, raw, ring)
                copy_a(f, slot, first=early)
                first_tap(f, slot, first)
                for n3, raw, ring in tiles[1:2]:
                    split_hi(n3, raw, ring)
                silu(f)
                for c in range(3):
                    u_high(f, slot, c, first=early)
                for n3, raw, ring in tiles[2:]:
                    split_hi(n3, raw, ring)

            ffn_tile(0, 0, [(4, 0, 0), (4, 1, 1), (4, 2, 2)], first=True, early=True)
            ffn_tile(1, 1, [(5, 0, 3), (5, 1, 4), (5, 2, 5)], early=True)
            with act.Fori(1, NF // 2 - 1) as i:
                ffn_tile(2 * i, 0, [(2 * i + 4, raw, raw) for raw in range(3)])
                ffn_tile(2 * i + 1, 1, [(2 * i + 5, raw, raw + 3) for raw in range(3)])
            ffn_tile(20, 0, [(24, 0, 0), (24, 1, 1)])
            ffn_tile(21, 1, [])

            act.preload_act_table_set("natural_log_exp_and_others")
            act.wait_ge(s_cs, NF)
            act.wait_ge(s_co, NF)
            for t in range(NTILE):
                r, i = ROWS[t], t % FIN_SLOTS
                act.wait_ge(s_ft, t + 1)
                full = psum[:r, 2 * i:2 * i + 2, :].rearrange("p a b -> p (a b)")
                if t >= FIN_SLOTS:
                    act.wait_ge(s_fy, t - FIN_SLOTS + 1)
                ch.link(act.activation(fin_sq[:r, t % 2, :], full, ACT.Square, accum_out=fin[:r, i, 0:1]))
                ch.link(act.activation(fin[:r, i, 1:2], fin[:r, i, 0:1], ACT.Ln, bias=eps[:r], scale=1.0 / D))
                act.activation(fin[:r, i, 2:3], fin[:r, i, 1:2], ACT.Exp, scale=-0.5).then_inc(s_fs, 1)

        @block.vector
        def _(dve):
            dve.memset(ones[:], 1.0).then_inc(s_set, 1)
            dve.memset(eps[:], EPS).then_inc(s_set, 1)
            dve.memset(sums_x[:], 1.0).then_inc(s_set, 1)
            def write_mod(n, parts, at, count):
                out = mod[:, at:at + count, :]
                dve.wait_ge(s_modt, ADA_A + n)
                dve.tensor_tensor(out, parts[:, 0], vec_a[:, at:at + count].unsqueeze(2).broadcast_to([P, count, 2]),
                                  ALU.add).then_inc(s_mod, 1)
                dve.wait_ge(s_mod, 2 * n + 1)
                dve.tensor_tensor(out, parts[:, 1], out, ALU.add).then_inc(s_mod, 1)
                dve.wait_ge(s_mod, 2 * n + 2)

            def copy_x(t):
                dve.wait_ge(s_xt, 2 * t + 1)
                dve.tensor_copy(xT[:, 0:4, P * t:P * t + ROWS[t]],
                                bank[2 * (t % 2)][:, :].rearrange("p (k n) -> p k n", k=4)[:, :, :ROWS[t]])\
                    .then_inc(s_xeD, 1)

            def diagonals(c):
                dve.wait_ge(s_id, 16)
                dve.wait_ge(s_rs1, c + 1)
                for t in range(3 * c, 3 * c + 3):
                    if c:
                        dve.wait_ge(s_ms, t - 2)
                    dve.tensor_scalar(diag[:, t % 3], ident[:], rstd_x[:, t:t + 1], None, ALU.mult).then_inc(s_dg, 1)

            def ada_low(g, q):
                for k in (2 * q, 2 * q + 1):
                    dve.wait_ge(s_ahi, 8 * g + k + 1)
                    dve.tensor_tensor(ada_lo[:, k % 4], ada_raw[:, q, k % 2], ada_hi[:, k % 4].bitcast(F32),
                                      ALU.subtract).then_inc(s_alo, 1)

            for t in range(3):
                copy_x(t)
            dve.wait_ge(s_vt, 3)
            dve.tensor_copy(vec_a[:], bank[7][:, 0:N_A]).then_inc(s_vec, 1)
            dve.tensor_copy(vec_b[:], bank[7][:, 128:128 + N_B]).then_inc(s_vec, 1)
            dve.tensor_copy(vec_c[:], bank[7][:, 256:256 + N_C]).then_inc(s_vec, 1)
            dve.wait_ge(s_silu, 1)
            dve.tensor_scalar(silu_e[:], silu_e[:], 1.0, None, ALU.add).then_inc(s_silu, 1)
            dve.wait_ge(s_silu, 2)
            dve.reciprocal(silu_e[:], silu_e[:]).then_inc(s_silu, 1)
            dve.wait_ge(s_silu, 3)
            dve.tensor_tensor(silu_c[:], silu_e[:], vec_a[:, 64:80].rearrange("p (c k) -> p c k", c=2), ALU.mult)\
                .then_inc(s_siluv, 1)

            dve.wait_ge(s_chi, 1)
            dve.wait_ge(s_siluv, 1)
            dve.tensor_tensor(c_parts[:, :, 2:4], silu_c[:].rearrange("p c k -> p k c"),
                              c_parts[:, :, 0:2].bitcast(F32), ALU.subtract).then_inc(s_cpl, 1)
            diagonals(0)
            for t in range(3, 6):
                copy_x(t)
            diagonals(1)
            ada_low(0, 0)
            ada_low(0, 1)
            for t in range(6, NTILE):
                copy_x(t)
            diagonals(2)
            for i in range(2, 4 * ADA_A):
                ada_low(i // 4, i % 4)

            def norm_scale(n):
                dve.scalar_tensor_tensor(out=scale_n[:, n], in0=mod[:, 24 * n + 8:24 * n + 16, :], scalar=1.0,
                                         in1=vec_a[:, 48 + 8 * n:56 + 8 * n].unsqueeze(2).broadcast_to([P, KT, 2]),
                                         op0=ALU.add, op1=ALU.mult).then_inc(s_scale, 1)


            def normed(n, c, k):
                bufs = norm_bufs[n]
                j = NH[n] + 8 * c + k
                if k == 0:
                    dve.wait_ge(s_rb, 3 * n + next(i for i, x in enumerate(CHUNKS) if NORM_RUNS[n][c][1] <= x[1]) + 1)
                if j >= 3:
                    dve.wait_ge(s_h, j - 2)
                base = NORM_RUNS[n][c][0]
                for a, b, which in split_run(*NORM_RUNS[n][c]):
                    last = dve.scalar_tensor_tensor(out=bufs["hn"][:, (8 * c + k) % 3, a - base:b - base],
                                                    in0=bufs["x"][:, k, a:b], scalar=scale_n[:, n, k, which:which + 1],
                                                    in1=bufs["rb"][:, a:b], op0=ALU.mult, op1=ALU.mult)
                last.then_inc(s_hn, 1)

            def h_low(n, c, k):
                bufs = norm_bufs[n]
                j = NH[n] + 8 * c + k
                dve.wait_ge(s_hn, j + 1)
                dve.wait_ge(s_hhi, j + 1)
                base = NORM_RUNS[n][c][0]
                for a, b, which in split_run(*NORM_RUNS[n][c]):
                    last = dve.scalar_tensor_tensor(out=bufs["lo"][:, k, a:b],
                                                    in0=bufs["hn"][:, (8 * c + k) % 3, a - base:b - base],
                                                    scalar=mod[:, 24 * n + k, which:which + 1],
                                                    in1=bufs["hi"][:, k, a:b].bitcast(F32), op0=ALU.add, op1=ALU.subtract)
                last.then_inc(s_h, 1)

            def norm(n, chunks):
                order = [(c, k) for c in chunks for k in range(KT)]
                for i, (c, k) in enumerate(order):
                    normed(n, c, k)
                    if i:
                        h_low(n, *order[i - 1])
                h_low(n, *order[-1])

            def split_w_in(g, slot, half):
                dve.wait_ge(s_whi, 2 * g + half + 1)
                dve.tensor_tensor(w_lo[:, slot, 4 * half:4 * half + 4], w_raw[:, half],
                                  w_hi[:, slot, 4 * half:4 * half + 4].bitcast(F32), ALU.subtract)\
                    .then_inc(s_wlo, 1)

            def z_group(g, slot, split_next=True, first=False):
                if not first:
                    ada_low(g + ADA_A, 0)
                for t in range(NTILE):
                    dve.wait_ge(s_z, 9 * g + t + 1)
                    if not first or t >= 3:
                        dve.wait_ge(s_zst[t % 3], 48 * g + 16 * (t // 3))
                    dve.tensor_copy(z_out[:ROWS[t], t % 3, :], bank[t % 3][:ROWS[t], 0:ZG]).then_inc(s_zc, 1)
                    if first and t == 1:
                        norm(0, [3])
                    if t in (1, 3, 5) and not (first and t == 1):
                        ada_low(g + ADA_A, (t + 1) // 2)
                    if split_next and t in (2, 4):
                        split_w_in(g + 1, 1 - slot, t // 2 - 1)

            write_mod(0, bank[7][:, 384:448].rearrange("p (j s c) -> p s j c", s=2, c=2), 0, 16)
            norm_scale(0)
            dve.wait_ge(s_scale, 1)
            split_w_in(0, 0, 0)
            split_w_in(0, 0, 1)
            norm(0, [0])
            ada_low(ADA_A, 0)
            ada_low(ADA_A, 1)
            norm(0, [1, 2])
            z_group(0, 0, first=True)
            with dve.Fori(0, 3) as i:
                for s in range(2):
                    z_group(2 * i + 1 + s, 1 - s)
            z_group(NZG - 1, 1, split_next=False)

            ch = Chain(dve, s_chD)
            dve.wait_ge(s_z, 9 * NZG)
            dve.wait_ge(s_adamm, 8 * ADA_G)
            dve.wait_ge(s_row, ADA_G)
            dve.wait_ge(s_rowst, 16 * (ADA_G - ADA_A))
            dve.wait_ge(s_xst, 16)
            for i in range(3):
                dve.wait_ge(s_zst[i], 16 * 3 * NZG)
            dve.memset(state[:], 0.0).then_inc(s_init, 1)
            dve.memset(zero[:], 0.0).then_inc(s_init, 1)
            dve.wait_ge(s_cT, 3)
            dve.memset(rqT[:], 0.0).then_inc(s_init, 1)
            dve.wait_ge(s_tab, 16 * N_TAB)
            dve.wait_ge(s_cau, 16)
            for k in range(3):
                last = dve.tensor_scalar(w_uq[:, k, :], w_uq[:, k, :], vec_a[:, 80 + k:81 + k], None, ALU.mult)
            last.then_inc(s_wuq, 1)
            write_mod(1, bank[7][:, 0:P].rearrange("p (s c j) -> p s j c", s=2, c=2), 16, 32)
            norm_scale(1)
            dve.wait_ge(s_cT, 2)
            dve.tensor_copy(skT[:, :, 512:1024], psum[:, 2:4, :]).then_inc(s_cD, 1)

            def cache_copy(s):
                if s < 4:
                    dve.wait_ge(s_cT, 4 + s)
                    dve.tensor_copy(kT[0:64, 2 * s + 1, 512:1024], bank[s][64:128, :]).then_inc(s_cD, 1)
                elif s == 5:
                    dve.wait_ge(s_cT, 9)
                    dve.tensor_copy(v_mla[:, 6:8, :], psum[:, 0:2, :]).then_inc(s_cD, 1)

            def front(m, s):
                r, slot = rows_of(m), m % 2
                b7, col = bank[7], key_col(m)
                v4 = b7.rearrange("p (k n) -> p k n", k=4)
                x = z_in[:r, slot, :]
                if s == 0:
                    dve.wait_ge(s_rs, m + 1)
                    if m:
                        dve.wait_ge(s_fp, 12 * m)
                        dve.wait_ge(s_latst, 32 * m)
                    dve.tensor_scalar(zqn[:r], x[:, O_ZQ:O_ZQ + QR], rs[:r, 0:1], None, ALU.mult)
                    dve.scalar_tensor_tensor(out=lat[:r], in0=x[:, O_KV:O_KV + KVR], scalar=rs[:r, 1:2],
                                             in1=g_kv[:r], op0=ALU.mult, op1=ALU.mult).then_inc(s_lat, 1)
                if s == 1:
                    dve.wait_ge(s_g1, m + 1)
                    dve.reciprocal(eg[:r], eg[:r]).then_inc(s_g2, 1)
                if s not in READ_D:
                    return
                dve.wait_ge(s_fp, 12 * m + s + 1)
                if s in READ_A and s != 7:
                    dve.wait_ge(s_fA, read_a(m, s) + 1)
                if s == 0:
                    last = dve.tensor_copy(skT[:, :, col:col + r], v4[:, 2:4, :r])
                elif s in (2, 3):
                    q4 = b7[:r, 0:384].rearrange("p (h d) -> p h d", h=4)

                    def tab(a, n):
                        return rope_t[:r, slot, 128 + a:128 + a + n].unsqueeze(1).broadcast_to([r, 4, n])

                    if not (m == 0 and s == 2):
                        dve.wait_ge(s_fD, read_d(m, s))
                    dve.tensor_tensor(q_a[:r], q4[:, :, NOPE:QD], tab(0, ROPE), ALU.mult)
                    dve.tensor_tensor(q_b[:r, :, 0:16], q4[:, :, NOPE + 16:QD], tab(32, 16), ALU.mult)
                    ch.link(dve.tensor_tensor(q_b[:r, :, 16:32], q4[:, :, NOPE:NOPE + 16], tab(48, 16), ALU.mult))
                    last = dve.tensor_tensor(qtok[:r, 384 * (s - 2):384 * (s - 1)]
                                             .rearrange("p (h d) -> p h d", h=4)[:, :, NOPE:QD],
                                             q_a[:r], q_b[:r], ALU.add)
                elif s == 4:
                    last = dve.tensor_copy(kT[64:96, :, col:col + r],
                                           v4[0:32, 2, :r].unsqueeze(1).broadcast_to([32, H_MLA, r]))
                elif s == 6:
                    last = dve.tensor_copy(qT[:QD, slot, 4:8, :r], v4[:QD, :, :r])
                elif s == 7:
                    last = dve.tensor_copy(kT[0:64, 1:H_MLA:2, col:col + r], v4[64:128, :, :r])
                elif s == 9:
                    last = dve.tensor_tensor(rqdT[:, :, :r], v4[:, 0:2, :r], q_decayT[:, :, :r], ALU.mult)
                elif s == 10:
                    last = dve.tensor_tensor(att[:r, :, :r], v4[:r, :, :r], decayT[:r, :, :r], ALU.mult)
                elif s == 11:
                    st = state[:, int(m > 0)]
                    o4 = b7[:r, 0:256].rearrange("p (h d) -> p h d", h=4)
                    ch.link(dve.tensor_tensor(st, st, state_decay[:, int(m == 0)], ALU.mult))
                    dve.tensor_reduce(stat[:r, 0, :], o4, AX, ALU.add)
                    dve.tensor_tensor(st[0:64, :, 0:64], st[0:64, :, 0:64], v4[0:64, 2:4, 0:64], ALU.add)
                    ch.link(dve.tensor_tensor(st[64:128, :, 64:128], st[64:128, :, 64:128], v4[64:128, 2:4, 64:128],
                                              ALU.add))
                    ch.link(dve.tensor_scalar(stat[:r, 0, :], stat[:r, 0, :], -1.0 / DH, None, ALU.mult))
                    last = dve.tensor_tensor(oc[:r], o4, stat[:r, 0, :].unsqueeze(2).broadcast_to([r, H_RET, DH]),
                                             ALU.add)
                last.then_inc(s_fD, 1)
                if s == 11:
                    dve.wait_ge(s_fD, read_d(m + 1, 0))
                    ch.link(dve.tensor_tensor(oc2[:r], oc[:r], oc[:r], ALU.mult))
                    dve.tensor_reduce(stat[:r, 1, :], oc2[:r], AX, ALU.add).then_inc(s_var, 1)

            def retention_out(m):
                r = rows_of(m)
                dve.wait_ge(s_rr, m + 1)
                ch.link(dve.tensor_tensor(oc[:r], oc[:r], stat[:r, 3, :].unsqueeze(2).broadcast_to([r, H_RET, DH]),
                                          ALU.mult))
                dve.wait_ge(s_gate, m + 1)
                dve.tensor_tensor(mixtok[:r, m % 2, 512:768], oc[:r].rearrange("p h d -> p (h d)"), gate[:r],
                                  ALU.mult).then_inc(s_ret, 1)

            def row_max(i):
                n = UNITS[i][0]
                r, w, j = rows_of(n), n_keys(n), count_units("M", i)
                dve.wait_ge(s_sc, i + 1)
                if n:
                    ch.link(dve.memset(score_bank(i, w)[0:64, w - 64:w], NEG))
                if j >= 2:
                    dve.wait_ge(s_p, j - 1)
                ch.link(dve.tensor_reduce(maxes[:r, j % 2, 0:1], score_bank(i, w)[:r], AX, ALU.max))
                dve.tensor_scalar(maxes[:r, j % 2, 1:2], maxes[:r, j % 2, 0:1], -MLA_SCALE, None, ALU.mult)\
                    .then_inc(s_mx, 1)

            def stick_logits(i):
                n = UNITS[i][0]
                r, w, j = rows_of(n), n_keys(n), count_units("S", i)
                dve.wait_ge(s_sc, i + 1)
                if j >= 2:
                    dve.wait_ge(s_wa, j - 1)
                if w > r:
                    dve.tensor_copy(zsb[:r, j % 2, :w - r], score_bank(i, w)[:r, :w - r])
                dve.tensor_tensor(zsb[:r, j % 2, w - r:w], score_bank(i, w)[:r, w - r:w], causal[:r, :r], ALU.add)\
                    .then_inc(s_zsb, 1)

            def stick_sums(i):
                n = UNITS[i][0]
                r, w, j = rows_of(n), n_keys(n), count_units("S", i)
                e = esb[:r, j % 2, :w]
                dve.wait_ge(s_l, j + 1)
                ch.link(dve.scalar_tensor_tensor(out=e, in0=zsb[:r, j % 2, :w], scalar=0.0, in1=e, op0=ALU.max,
                                                 op1=ALU.add))
                back = e[:, ::-1]
                dve.tensor_tensor_scan(back, back, zero[:r, :].broadcast_to([r, w]), 0.0, ALU.add, ALU.add).then_inc(s_c, 1)

            def head_output(i):
                n, kind, h = UNITS[i]
                r, v = rows_of(n), PV_NO[i]
                nb = len(key_blocks(n))
                o = bank[6][:r, 64 * (v % 8):64 * (v % 8) + 64]
                if kind == "M":
                    j = count_units("M", i)
                    dve.wait_ge(s_p, j + 1)
                    ch.link(dve.reciprocal(rowsum[:r, j % 4, 1:2], rowsum[:r, j % 4, 0:1]))
                    dve.wait_ge(s_pv, W_NO[kind, i, (nb + 3) // 4 - 1] + 1)
                    dve.tensor_scalar(mixtok[:r, n % 2, 64 * h:64 * h + 64], o, rowsum[:r, j % 4, 1:2], None,
                                      ALU.mult).then_inc(s_o, 1)
                else:
                    dve.wait_ge(s_pv, W_NO[kind, i, (nb + 3) // 4 - 1] + 1)
                    dve.tensor_copy(mixtok[:r, n % 2, 768 + 64 * h:832 + 64 * h], o).then_inc(s_o, 1)

            def split_lo(n3, raw, slot):
                dve.wait_ge(s_wh, 3 * n3 + raw + 1)
                dve.tensor_tensor(wt_lo[:, slot], wt_raw[:, raw], wt_hi[:, slot].bitcast(F32), ALU.subtract)\
                    .then_inc(s_wlow, 1)

            for step in range(-12, STEPS):
                m, s = divmod(step + 12, 12)
                if 0 <= step < len(UNITS):
                    (row_max if UNITS[step][1] == "M" else stick_logits)(step)
                for x in PIECES.get(step - 1, []):
                    if x[0] != "X" and x[2] == 0:
                        head_output(x[1])
                if 0 <= step - 2 < len(UNITS) and UNITS[step - 2][1] == "S":
                    stick_sums(step - 2)
                if s == 0 and 0 < m <= NTILE:
                    retention_out(m - 1)
                if step - EARLY_SPLIT in range(3):
                    split_lo(0, step - EARLY_SPLIT, step - EARLY_SPLIT)
                if m == 0:
                    cache_copy(s)
                if m < NTILE:
                    front(m, s)

            for c, (lo, hi) in enumerate(CHUNKS):
                for k in (0, 4):
                    dve.wait_ge(s_mhi, 2 * c + k // 4 + 1)
                    dve.tensor_tensor(a_lo[:, k:k + 4, lo:hi], mix_raw[:, k:k + 4, lo:hi],
                                      a_hi[:, k:k + 4, lo:hi].bitcast(F32), ALU.subtract).then_inc(s_mlo, 1)
            for idx in range(3, 6):
                split_lo(1, idx % 3, idx)
            dve.wait_ge(s_res, 16)
            for j, (d, c) in enumerate(PROJ):
                dve.wait_ge(s_y, j + 1)
                for a, b, which in segments(c):
                    last = dve.scalar_tensor_tensor(
                        out=res[:, d, a:b], in0=bank[j % 5][:, a - CHUNKS[c][0]:b - CHUNKS[c][0]],
                        scalar=mod[:, 16 + d, which:which + 1], in1=res[:, d, a:b], op0=ALU.mult, op1=ALU.add)
                last.then_inc(s_yr, 1)
                if c == 2 and d + 6 < 12:
                    split_lo((d + 6) // 3, d % 3, d % 6)
                if j == PROJ_DONE[0] + 1:
                    norm(1, [0])
            norm(1, [1, 2])

            dve.memset(a_ext[:, 0, 0:2], 0.0).then_inc(s_cvi, 1)
            dve.memset(a_ext[:, 1, 0:2], 0.0).then_inc(s_cvi, 1)
            b_taps = vec_b[:].rearrange("p (j f) -> p f j", j=4)
            b_state = vec_c[:].rearrange("p (j f) -> p f j", j=2)

            def vectors(f, slot, first=False):
                if not first:
                    dve.wait_ge(s_cv, f - 1)
                    dve.wait_ge(s_cs, f - 1)
                dve.tensor_copy(f_vec[:, slot, :].unsqueeze(1), b_taps[:, bass.ds(f, 1), :])
                dve.tensor_copy(a_ext[:, slot, LP + 2:LP + 4].unsqueeze(1), b_state[:, bass.ds(f, 1), :])\
                    .then_inc(s_fv, 1)

            def taps(f, slot):
                dve.wait_ge(s_cv, f + 1)
                dve.scalar_tensor_tensor(out=conv[:], in0=a_ext[:, slot, 1:T + 3], scalar=f_vec[:, slot, 1:2],
                                         in1=conv[:], op0=ALU.mult, op1=ALU.add).then_inc(s_c1, 1)
                for j, at in enumerate((LP, T + 2)):
                    last = dve.tensor_copy(conv_out[:, 2 * j:2 * j + 2, bass.ds(f, 1)],
                                           a_ext[:, slot, at:at + 2].unsqueeze(2))
                last.then_inc(s_co, 1)
                dve.wait_ge(s_c1, f + 1)
                dve.scalar_tensor_tensor(out=conv[:], in0=a_ext[:, slot, 0:T + 2], scalar=f_vec[:, slot, 0:1],
                                         in1=conv[:], op0=ALU.mult, op1=ALU.add).then_inc(s_cs, 1)

            def gate_u(f, slot, c):
                dve.wait_ge(s_up, 2 * c + 2 if isinstance(f, int) and f == 0 else 6 * f + 4 + c)
                if c == 0:
                    dve.wait_ge(s_sl, f + 1)
                if not (isinstance(f, int) and 3 * f + c < 2):
                    dve.wait_ge(s_ul, 3 * f + c - 1)
                src = bank[7] if isinstance(f, int) and (f, c) == (0, 2) else bank[2 + (3 * slot + c) % 2]
                for a, b, which in segments(c):
                    last = dve.tensor_tensor(u_val[:, c % 2, a - CHUNKS[c][0]:b - CHUNKS[c][0]],
                                             src[:, a - CHUNKS[c][0]:b - CHUNKS[c][0]],
                                             conv[:, a + 2 * which:b + 2 * which], ALU.mult)
                last.then_inc(s_u, 1)

            def u_low(f, slot, c):
                a, b = CHUNKS[c]
                dve.wait_ge(s_uh, 3 * f + c + 1)
                dve.tensor_tensor(u_lo[:, slot, a:b], u_val[:, c % 2, :b - a], u_hi[:, slot, a:b].bitcast(F32),
                                  ALU.subtract).then_inc(s_ul, 1)

            def add_down(f, n):
                for q in range(4 * n, 4 * n + 4):
                    d, c = down_order(f, q)
                    dve.wait_ge(s_dn, 24 * f + q + 1)
                    for a, b, which in segments(c):
                        last = dve.scalar_tensor_tensor(
                            out=res[:, d, a:b], in0=bank[4 + q % 4][:, a - CHUNKS[c][0]:b - CHUNKS[c][0]],
                            scalar=mod[:, 40 + d, which:which + 1], in1=res[:, d, a:b], op0=ALU.mult, op1=ALU.add)
                    last.then_inc(s_dr, 1)

            def ffn_tile(f, slot, tiles, early=False, down=True):
                vectors(f, slot, first=early)
                for n in range(6):
                    if n == 4:
                        gate_u(f, slot, 0)
                    if n == 5:
                        gate_u(f, slot, 1)
                        u_low(f, slot, 0)
                    if n == 0 and tiles:
                        split_lo(*tiles[0])
                    if n == 3:
                        taps(f, slot)
                        if len(tiles) > 1:
                            split_lo(*tiles[1])
                    if down:
                        add_down(f - 1, n)
                u_low(f, slot, 1)
                gate_u(f, slot, 2)
                u_low(f, slot, 2)
                for t in tiles[2:]:
                    split_lo(*t)

            ffn_tile(0, 0, [(4, 0, 0), (4, 1, 1), (4, 2, 2)], early=True, down=False)
            ffn_tile(1, 1, [(5, 0, 3), (5, 1, 4), (5, 2, 5)], early=True)
            with dve.Fori(1, NF // 2 - 1) as i:
                ffn_tile(2 * i, 0, [(2 * i + 4, raw, raw) for raw in range(3)])
                ffn_tile(2 * i + 1, 1, [(2 * i + 5, raw, raw + 3) for raw in range(3)])
            ffn_tile(20, 0, [(24, 0, 0), (24, 1, 1)])
            ffn_tile(21, 1, [])

            def final(t):
                r, i = ROWS[t], t % FIN_SLOTS
                if t == 0:
                    dve.wait_ge(s_gf, 16)
                dve.wait_ge(s_fs, t + 1)
                if t >= FIN_SLOTS:
                    dve.wait_ge(s_yst[i], 16 * (t // FIN_SLOTS))
                dve.scalar_tensor_tensor(out=y_out[:r, i], in0=psum[:r, 2 * i:2 * i + 2, :]
                                         .rearrange("p a b -> p (a b)"), scalar=fin[:r, i, 2:3], in1=g_fin[:r],
                                         op0=ALU.mult, op1=ALU.mult).then_inc(s_fy, 1)

            for n in range(6):
                add_down(NF - 1, n)
            dve.wait_ge(s_cvt, 1)
            dve.tensor_copy(conv_rows[0:88, :], bank[7][0:88, 0:P]).then_inc(s_cvc, 1)
            for t in range(NTILE):
                final(t)

        @block.tensor
        def _(pe):
            def ada_piece(g, q):
                if q == 0 and not (isinstance(g, int) and g == 0):
                    pe.wait_ge(s_row, g)
                for k in (2 * q, 2 * q + 1):
                    pe.wait_ge(s_alo, 8 * g + k + 1)
                    pe.matmul(bank[5][0:4, :], c_parts[:, k, :], ada_hi[:, k % 4, :], start=(k == 0), stop=False)
                    pe.matmul(bank[5][0:4, :], c_parts[:, k, :], ada_lo[:, k % 4, :], start=False,
                              stop=(k == KT - 1)).then_inc(s_adamm, 1)

            def x_transposes(t):
                pe.wait_ge(s_x[t], 16)
                if t >= 2:
                    pe.wait_ge(s_xeD, t - 1)
                    pe.wait_ge(s_xeA, t - 1)
                for j in range(2):
                    for k in range(4):
                        last = pe.transpose(bank[2 * (t % 2) + j][:, P * k:P * k + ROWS[t]],
                                            x_in[:ROWS[t], t, P * (4 * j + k):P * (4 * j + k) + P],
                                            ident[:ROWS[t], :ROWS[t]])
                    last.then_inc(s_xt, 1)

            def spread_rstd(c):
                if c == 0:
                    pe.wait_ge(s_set, 3)
                else:
                    pe.wait_ge(s_rb, c)
                for t in range(3 * c, 3 * c + 3):
                    pe.wait_ge(s_dg, t + 1)
                    pe.matmul(bank[6][:, P * (t % 3):P * (t % 3) + ROWS[t]], ones[:ROWS[t], :],
                              diag[:ROWS[t], t % 3, :ROWS[t]], start=True, stop=True).then_inc(s_ms, 1)

            pe.wait_ge(s_id, 16)
            for c, tiles in enumerate(((0, 1, 2, 3), (4, 5, 6), (7, 8))):
                for t in tiles:
                    x_transposes(t)
                    if t == 2:
                        pe.wait_ge(s_const, 16 * n_const)
                        for i, n in enumerate((N_A, N_B, N_C)):
                            pe.transpose(bank[7][:, 128 * i:128 * i + n], vec_in[:n, i, :], ident[:n, :n])\
                                .then_inc(s_vt, 1)
                spread_rstd(c)
                if c == 1:
                    pe.wait_ge(s_cpl, 1)
                    ada_piece(0, 0)
                    ada_piece(0, 1)
            def turn_row(g):
                pe.wait_ge(s_row, g + 1)
                for j in range(AG // P):
                    at = 384 + 4 * (AG // P * g + j)
                    last = pe.transpose(bank[7][:, at:at + 4], ada_row[0:4, g % 2, P * j:P * j + P], ident[0:4, 0:4])
                last.then_inc(s_modt, 1)

            for i in range(2, 4 * ADA_A):
                ada_piece(i // 4, i % 4)
                if i > 4 and i % 4 == 1:
                    turn_row(i // 4 - 1)
            turn_row(ADA_A - 1)

            def z_group(g, slot, first=False):
                pe.wait_ge(s_wlo, 2 * g + 2)
                for t in range(NTILE):
                    r = ROWS[t]
                    if first:
                        pe.wait_ge(s_h, 8 * (chunk_of(t, NORM_RUNS[0]) + 1))
                    if not first or t >= 3:
                        pe.wait_ge(s_zc, 9 * g + t - 2)
                    for k in range(KT):
                        for m, (hh, ww) in enumerate(((h_hi, w_hi), (h_hi, w_lo), (h_lo, w_hi))):
                            last = pe.matmul(bank[t % 3][:r, 0:ZG], hh[:, k, P * t:P * t + r], ww[:, slot, k, :],
                                             start=(k == 0 and m == 0), stop=(k == KT - 1 and m == 2))
                    last.then_inc(s_z, 1)
                    if t % 2:
                        ada_piece(g + ADA_A, t // 2)

            z_group(0, 0, first=True)
            with pe.Fori(0, 3) as i:
                for s in range(2):
                    z_group(2 * i + 1 + s, 1 - s)
            z_group(NZG - 1, 1)

            pe.wait_ge(s_cache, 48)
            pe.wait_ge(s_zc, 9 * NZG)
            pe.wait_ge(s_row, ADA_G)
            pe.wait_ge(s_ln, 3)
            pe.wait_ge(s_modl, 16)
            pe.transpose(bank[7][:, 0:P], mod_rows[:], ident[:]).then_inc(s_modt, 1)
            for j in range(4):
                for k in range(2):
                    last = pe.transpose(bank[k][:, P * j:P * j + P], c_lat[:, j, P * k:P * k + P], ident[:])
            last.then_inc(s_cT, 1)
            for j in range(4):
                for k in range(2):
                    last = pe.transpose(bank[2 + k][:, P * j:P * j + P], c_sk[:, j, P * k:P * k + P], ident[:])
            last.then_inc(s_cT, 1)
            for j in range(4):
                last = pe.transpose(bank[4][0:32, P * j:P * j + P], c_kr[:, j, :], ident[:])
            last.then_inc(s_cT, 1)

            def nope_keys(out, q, lhs_latT, n):
                for k in range(2):
                    last = pe.matmul(out, w_uk[:, k, P * q:P * q + P], lhs_latT[:, k, :n], start=(k == 0), stop=(k == 1))
                return last

            def values(out, latT_tile, r):
                for k in range(2):
                    last = pe.matmul(out, latT_tile[:, k, :r], w_uv[:, k, :], start=(k == 0), stop=(k == 1))
                return last

            def cache_step(s):
                if s < 4:
                    if s == 0:
                        pe.wait_ge(s_tab, 16 * N_TAB)
                        pe.wait_ge(s_cA, 1)
                    if s == 2:
                        pe.wait_ge(s_cD, 1)
                    nope_keys(bank[s], s, c_latT, 512).then_inc(s_cT, 1)
                elif s < 6:
                    pe.wait_ge(s_cA, 2 if s == 4 else 4)
                    if s == 5:
                        pe.wait_ge(s_cD, 3)
                    for j in range(2):
                        at = 2 * (s - 4) + j
                        last = values(bank[4 + j if s == 4 else j], c_latT[:, :, P * at:P * at + P], P)
                    last.then_inc(s_cT, 1)

            def front(m, s):
                r, slot, b7 = rows_of(m), m % 2, bank[7]
                x = z_in[:r, slot, :]

                def turn(at, src, width):
                    return pe.transpose(b7[:width, P * at:P * at + r], src, ident[:r, :r])

                if m == 0 and s == 0:
                    pe.wait_ge(s_mod, 4)
                else:
                    pe.wait_ge(s_fA, read_a(m, s))
                    pe.wait_ge(s_fD, read_d(m, s))
                if s == 0:
                    pe.wait_ge(s_zi[slot], 48 * (m // 2 + 1))
                    for j, at in enumerate((O_SQ, O_SQ + P, O_SK, O_SK + P)):
                        last = turn(j, x[:, at:at + P], P)
                elif s == 1:
                    pe.wait_ge(s_lat, m + 1)
                    for k in range(3):
                        last = turn(k, zqn[:r, P * k:P * k + P], P)
                elif s in (2, 3):
                    if m == 0 and s == 2:
                        pe.wait_ge(s_wuq, 1)
                    for k in range(3):
                        last = pe.matmul(b7[:r, 0:384], qnT[:, k, :r], w_uq[:, k, 384 * (s - 2):384 * (s - 1)],
                                         start=(k == 0), stop=(k == 2))
                elif s == 4:
                    pe.wait_ge(s_kr, m + 1)
                    for k in range(2):
                        turn(k, lat[:r, P * k:P * k + P], P)
                    last = turn(2, kr[:r, :], ROPE)
                elif s in (5, 6):
                    for j in range(4):
                        h = 4 * (s - 5) + j
                        last = turn(j, qtok[:r, QD * h:QD * h + QD], QD)
                elif s == 7:
                    for q in range(4):
                        last = nope_keys(b7[:, P * q:P * q + r], q, latT, r)
                elif s == 8:
                    last = values(b7[:r, :], latT, r)
                elif s == 9:
                    pe.wait_ge(s_rot, m + 1)
                    for j in range(4):
                        last = turn(j, rqk[:r].rearrange("p h d -> p (h d)")[:, P * j:P * j + P], P)
                elif s == 10:
                    for q in range(2):
                        last = pe.matmul(b7[:r, 256 * q:256 * q + 256].rearrange("p (a n) -> p a n", a=2)[:, :, :r],
                                         rkT[:, q, :r], rqT[:, q, :, :r], start=True, stop=True)
                elif s == 11:
                    if m == 0:
                        pe.wait_ge(s_sv, 80)
                    kd2 = kd[:r].rearrange("p h d -> p (h d)")
                    for q in range(2):
                        pe.matmul(b7[:, 256 + P * q:256 + P * q + P], kd2[:, P * q:P * q + P],
                                  x[:, O_RV + P * q:O_RV + P * q + P], start=True, stop=True)
                    for q in range(2):
                        pe.matmul(b7[:r, P * q:P * q + P], rqdT[:, q, :r], state[:, int(m > 0), q, :],
                                  start=True, stop=False)
                        for a in range(2):
                            h = 2 * q + a
                            last = pe.matmul(b7[:r, DH * h:DH * h + DH], att[:r, h, :r],
                                             x[:, O_RV + DH * h:O_RV + DH * h + DH], start=False, stop=(a == 1))
                last.then_inc(s_fp, 1)

            def scores(i):
                n, kind, h = UNITS[i]
                r, slot, w = rows_of(n), n % 2, n_keys(n)
                first = key_blocks(n)[0][0]
                if i == 0:
                    pe.wait_ge(s_cA, 7)
                    pe.wait_ge(s_cD, 6)
                if i >= 2:
                    if UNITS[i - 2][1] == "M":
                        pe.wait_ge(s_p, count_units("M", i - 2) + 1)
                    else:
                        pe.wait_ge(s_zsb, count_units("S", i - 2) + 1)
                for a in range(0, w, 512):
                    b = min(w, a + 512)
                    out = score_bank(i, w)[:r, a:b]
                    if kind == "M":
                        last = pe.matmul(out, qT[:QD, slot, h, :r], kT[:QD, h, first + a:first + b],
                                         start=True, stop=True)
                    else:
                        lo = 64 * (h % 2)
                        last = pe.matmul(out, sqT[lo:lo + 64, slot, h // 2, :r],
                                         skT[lo:lo + 64, h // 2, first + a:first + b], start=True, stop=True)
                last.then_inc(s_sc, 1)

            def transposes(x):
                kind, i, j = x
                q = PIECE_NO[x]
                if q >= 2:
                    pieces_done(pe, ORDER[q - 2])
                out = bank[4 + q % 2]
                if kind == "X":
                    r = rows_of(i)
                    if j == 0:
                        pe.wait_ge(s_ret, i + 1)
                        pe.wait_ge(s_o, 12 * (i + 1))
                    for k in range(4):
                        last = pe.transpose(out[:, P * k:P * k + r],
                                            mixtok[:r, i % 2, P * (4 * j + k):P * (4 * j + k) + P], ident[:r, :r])
                else:
                    n = UNITS[i][0]
                    r, u = rows_of(n), count_units(kind, i)
                    pe.wait_ge(s_p if kind == "M" else s_w, u + 1)
                    src = prob[:r, u % 3, :] if kind == "M" else esb[:r, u % 2, :]
                    first = key_blocks(n)[0][0]
                    for k, (col, size, _) in enumerate(key_blocks(n)[4 * j:4 * j + 4]):
                        last = pe.transpose(out[:size, P * k:P * k + r], src[:, col - first:col - first + size],
                                            ident[:r, :r])
                last.then_inc(s_tr, 1)

            def weigh(i):
                n, kind, h = UNITS[i]
                r, v = rows_of(n), PV_NO[i]
                if v:
                    pe.wait_ge(s_o, v)
                if kind == "S":
                    pe.wait_ge(s_sv, 80 if n < 5 else 96)
                blocks = key_blocks(n)
                for k, (_, size, tile_) in enumerate(blocks):
                    x = (kind, i, k // 4)
                    if k % 4 == 0:
                        pieces_done(pe, x)
                    vals = v_mla[:size, tile_, 64 * h:64 * h + 64] if kind == "M" else \
                        sv[:size, tile_, 64 * h:64 * h + 64]
                    last = pe.matmul(bank[6][:r, 64 * (v % 8):64 * (v % 8) + 64], pT[:size, W_NO[x] % 4, k % 4, :r],
                                     vals, start=(k == 0), stop=(k == len(blocks) - 1))
                    if k % 4 == 3 or k == len(blocks) - 1:
                        last.then_inc(s_pv, 1)

            for step in range(-12, STEPS):
                m, s = divmod(step + 12, 12)
                if 0 <= step < len(UNITS):
                    scores(step)
                for x in PIECES.get(step - 1, []):
                    if x[0] != "X" and x[2] == 0:
                        weigh(x[1])
                for x in PIECES.get(step, []):
                    transposes(x)
                if m == 0:
                    cache_step(s)
                if m < NTILE:
                    front(m, s)

            pieces_done(pe, ORDER[-1])
            pieces_done(pe, ORDER[-2])
            thirds = ((wt_hi, a_hi), (wt_lo, a_hi), (wt_hi, a_lo))

            def project(out, c, slot):
                a, b = CHUNKS[c]
                for k in range(KT):
                    for m, (ww, aa) in enumerate(thirds):
                        last = pe.matmul(out[:, :b - a], ww[:, slot, P * k:P * k + P], aa[:, k, a:b],
                                         start=(k == 0 and m == 0), stop=(k == KT - 1 and m == 2))
                return last

            def sum_square(j):
                d, c = PROJ[j]
                a, b = CHUNKS[c]
                pe.wait_ge(s_sq, NTILE + j + 1)
                pe.matmul(bank[5 + c][:, :b - a], ones[:], norm_bufs[1]["sq"][:, j % 2, :b - a],
                          start=(d == 0), stop=(d == KT - 1)).then_inc(s_ms, 1)

            for j, (d, c) in enumerate(PROJ):
                pe.wait_ge(s_wlow, d + 1)
                if d == 0:
                    pe.wait_ge(s_mlo, 2 * c + 2)
                if j >= 5:
                    pe.wait_ge(s_yr, j - 4)
                project(bank[j % 5], c, d % 6).then_inc(s_y, 1)
                if j >= 2:
                    sum_square(j - 2)

            EACH = {n: (n,) for n in range(6)}

            def up(f, slot, ring_a, ring_b, tile_no, ring_down=None, very_first=False, down_parts=EACH):
                for n in range(6):
                    c, branch = divmod(n, 2) if very_first else (n % 3, n // 3)
                    if c == 0:
                        pe.wait_ge(s_wlow, tile_no + branch + 1)
                    if very_first and branch == 0:
                        pe.wait_ge(s_h, NH[1] + 8 * (c + 1))
                    if branch == 0 and not (very_first and c < 2):
                        pe.wait_ge(s_ac, 3 * f + c - 1)
                    if branch == 1 and not very_first:
                        pe.wait_ge(s_u, 3 * f + c - 1)
                    out = bank[7] if very_first and n == 5 else bank[2 * branch + (3 * slot + c) % 2]
                    last = project(out, c, ring_b if branch else ring_a)
                    last.then_inc(s_up, 1)
                    if very_first and n == 0:
                        sum_square(22)
                        sum_square(23)
                    for part in down_parts.get(n, ()):
                        down(f - 1, 1 - slot, ring_down, tile_no + 2, part)

            def down(f, slot, ring, tile_no, n):
                if n == 0:
                    pe.wait_ge(s_wlow, tile_no + 1)
                    pe.wait_ge(s_ul, 3 * f + 3)
                for q in range(4 * n, 4 * n + 4):
                    d, c = down_order(f, q)
                    a, b = CHUNKS[c]
                    if not (isinstance(f, int) and f == 0 and q < 4):
                        pe.wait_ge(s_dr, 24 * f + q - 3)
                    for m, (ww, uu) in enumerate(((wt_hi, u_hi), (wt_lo, u_hi), (wt_hi, u_lo))):
                        last = pe.matmul(bank[4 + q % 4][:, :b - a], ww[:, ring, P * d:P * d + P], uu[:, slot, a:b],
                                         start=(m == 0), stop=(m == 2))
                    last.then_inc(s_dn, 1)

            pe.wait_ge(s_yr, 21)
            up(0, 0, 2, 3, 8, very_first=True, down_parts={})
            pe.wait_ge(s_ln, 6)
            up(1, 1, 4, 5, 10, ring_down=0, down_parts={2: (0,), 3: (1, 2), 4: (3, 4), 5: (5,)})
            up(2, 0, 1, 2, 13, ring_down=3)
            with pe.Fori(1, NF // 2 - 1) as i:
                up(2 * i + 1, 1, 4, 5, 6 * i + 10, ring_down=0)
                up(2 * i + 2, 0, 1, 2, 6 * i + 13, ring_down=3)
            up(21, 1, 4, 5, 70, ring_down=0)

            def final_transposes(t):
                r = ROWS[t]
                if t >= FIN_SLOTS:
                    pe.wait_ge(s_fy, t - FIN_SLOTS + 1)
                pe.wait_ge(s_dr, 24 * (NF - 1) + KT * (chunk_of(t) + 1))
                for k in range(KT):
                    last = pe.transpose(bank[2 * (t % FIN_SLOTS) + k // 4][:r, P * (k % 4):P * (k % 4) + P],
                                        res[:, k, P * t:P * t + r], ident[:])
                last.then_inc(s_ft, 1)

            for n in range(6):
                down(NF - 1, 1, 1, 73, n)
                if n == 4:
                    pe.wait_ge(s_u, 3 * NF)
                    final_transposes(0)
                    final_transposes(1)
            pe.wait_ge(s_dr, 24 * NF)
            pe.wait_ge(s_co, NF)
            pe.transpose(bank[7][0:88, 0:P], conv_out[:].rearrange("p j f -> p (j f)"), ident[:]).then_inc(s_cvt, 1)
            for t in range(2, NTILE):
                final_transposes(t)


def make(nc, outs):
    I = {n: nc.dram_tensor(f"in_{n}", s, F32, kind="ExternalInput").ap() for n, s in {**INS, **TABLES}.items()}
    O = {n: nc.dram_tensor(f"out_{n}", s, F32, kind="ExternalOutput").ap() for n, s in outs}
    build(nc, I, O)


def kernel(**inputs):
    import concourse.bacc as bacc
    from concourse.bass_utils import run_bass_kernel_spmd

    nc = bacc.Bacc("TRN2", target_bir_lowering=False, num_devices=1)
    make(nc, OUTS)
    arrays = {f"in_{n}": np.ascontiguousarray(inputs[n]).reshape(s) for n, s in INS.items()}
    arrays.update({f"in_{n}": a for n, a in tables().items()})
    r = run_bass_kernel_spmd(nc, [arrays], core_ids=[0])
    return tuple(r.results[0][f"out_{n}"] for n, _ in OUTS)
```
